# Optimizing a Trainium2 kernel written in Bass

```python
import numpy as np
import jax
import jax.numpy as jnp
from jax import lax

D_MODEL = 1024
BATCH = 1
SEQ = 256
DEPTH = 2

ROPE_THETA = 10000.0
NORM_EPS = 1e-6
NEG_INF = -1e30
FORCED_SCORE = 1e4

MLSTM_HEADS = 4
MLSTM_DH = D_MODEL // 8
MLSTM_W = MLSTM_HEADS * MLSTM_DH
MLSTM_CHUNK = 64
MLSTM_CONV = 4
MLSTM_GATE_CAP = 15.0
MOBA_HEADS = 4
MOBA_DH = D_MODEL // 8
MOBA_W = MOBA_HEADS * MOBA_DH
MOBA_BLOCK = 256
MOBA_TOPK = 3
MOBA_QCHUNK = 16
EVEN_SPLITS = (2 * MLSTM_W, 3 * MLSTM_W, 4 * MLSTM_W, 4 * MLSTM_W + 2 * MLSTM_HEADS,
               4 * MLSTM_W + 2 * MLSTM_HEADS + MOBA_W, 4 * MLSTM_W + 2 * MLSTM_HEADS + 2 * MOBA_W)
EVEN_IN = 4 * MLSTM_W + 2 * MLSTM_HEADS + 3 * MOBA_W

NSA_HEADS = 8
NSA_GROUPS = 2
NSA_REP = NSA_HEADS // NSA_GROUPS
NSA_DH = D_MODEL // 8
NSA_W = NSA_HEADS * NSA_DH
NSA_KV_W = NSA_GROUPS * NSA_DH
CMP_LEN = 32
CMP_STRIDE = 16
CMP_HIDDEN = 256
SEL_BLOCK = 64
SEL_TOPN = 8
WINDOW = 512
NSA_QCHUNK = 32
ODD_SPLITS = (NSA_W, NSA_W + NSA_KV_W, NSA_W + 2 * NSA_KV_W, NSA_W + 3 * NSA_KV_W,
              NSA_W + 4 * NSA_KV_W, NSA_W + 5 * NSA_KV_W, NSA_W + 6 * NSA_KV_W)
ODD_IN = NSA_W + 6 * NSA_KV_W + 3 * NSA_HEADS

MOE_GROUPS = 4
MOE_EXPERTS_PER_GROUP = 4
MOE_EXPERTS = MOE_GROUPS * MOE_EXPERTS_PER_GROUP
MOE_TOPK = 2
MOE_HIDDEN = D_MODEL // 4

kernel_name = 'hybrid_mlstm_moba_nsa_hmoe'

def rms_norm(x, g):
    xf = x.astype(jnp.float32)
    y = xf * lax.rsqrt(jnp.mean(xf * xf, axis=-1, keepdims=True) + NORM_EPS)
    return (y * g.astype(jnp.float32)).astype(x.dtype)

def rotary(x):
    S, Dh = x.shape[-2], x.shape[-1]
    half = Dh // 2
    inv = ROPE_THETA ** (-(jnp.arange(half, dtype=jnp.float32) / half))
    ang = jnp.arange(S, dtype=jnp.float32)[:, None] * inv[None, :]
    cos, sin = jnp.cos(ang), jnp.sin(ang)
    xf = x.astype(jnp.float32)
    x1, x2 = xf[..., :half], xf[..., half:]
    return jnp.concatenate([x1 * cos - x2 * sin, x2 * cos + x1 * sin], axis=-1).astype(x.dtype)

def masked_softmax(s, mask):
    s = jnp.where(mask, s.astype(jnp.float32), NEG_INF)
    e = jnp.where(mask, jnp.exp(s - jnp.max(s, axis=-1, keepdims=True)), 0.0)
    return e / jnp.maximum(jnp.sum(e, axis=-1, keepdims=True), 1e-30)

def split_heads(t, n, d):
    B, S, _ = t.shape
    return t.reshape(B, S, n, d).transpose(0, 2, 1, 3)

def merge_heads(t):
    B, n, S, d = t.shape
    return t.transpose(0, 2, 1, 3).reshape(B, S, n * d)

def causal_depthwise_conv(x, w):
    K, C = w.shape
    return lax.conv_general_dilated(x, w[:, None, :].astype(x.dtype), window_strides=(1,),
                                    padding=[(K - 1, 0)], dimension_numbers=('NWC', 'WIO', 'NWC'),
                                    feature_group_count=C)

def mlstm_chunkwise(q, k, v, log_i, log_f):
    B, H, S, Dh = q.shape
    L = MLSTM_CHUNK
    NC = S // L
    f32 = jnp.float32
    q = q.astype(f32).reshape(B, H, NC, L, Dh) * (Dh ** -0.5)
    k = k.astype(f32).reshape(B, H, NC, L, Dh)
    v = v.astype(f32).reshape(B, H, NC, L, Dh)
    log_i = log_i.astype(f32).reshape(B, H, NC, L)
    b = jnp.cumsum(log_f.astype(f32).reshape(B, H, NC, L), axis=-1)
    b_last = b[..., -1]
    g = b_last[..., None] - b + log_i
    g_max = jnp.max(g, axis=-1)
    w = jnp.exp(g - g_max[..., None])
    kv = jnp.einsum('bhcs,bhcse,bhcsd->bhced', w, v, k)
    ksum = jnp.einsum('bhcs,bhcsd->bhcd', w, k)

    def step(carry, xs):
        C, n, m = carry
        kv_c, ks_c, gm_c, bl_c = xs
        m_new = jnp.maximum(bl_c + m, gm_c)
        a = jnp.exp(bl_c + m - m_new)
        c = jnp.exp(gm_c - m_new)
        C_new = a[..., None, None] * C + c[..., None, None] * kv_c
        n_new = a[..., None] * n + c[..., None] * ks_c
        return (C_new, n_new, m_new), (C, n, m)

    init = (jnp.zeros((B, H, Dh, Dh), f32), jnp.zeros((B, H, Dh), f32), jnp.zeros((B, H), f32))
    xs = (jnp.moveaxis(kv, 2, 0), jnp.moveaxis(ksum, 2, 0), jnp.moveaxis(g_max, 2, 0), jnp.moveaxis(b_last, 2, 0))
    _, (C_in, n_in, m_in) = lax.scan(step, init, xs)
    C_in = jnp.moveaxis(C_in, 0, 2)
    n_in = jnp.moveaxis(n_in, 0, 2)
    m_in = jnp.moveaxis(m_in, 0, 2)
    causal = jnp.tril(jnp.ones((L, L), dtype=bool))
    dmat = jnp.where(causal, b[..., :, None] - b[..., None, :] + log_i[..., None, :], NEG_INF)
    inter = b + m_in[..., None]
    m_t = jnp.maximum(inter, jnp.max(dmat, axis=-1))
    s = jnp.einsum('bhctd,bhcsd->bhcts', q, k) * jnp.exp(dmat - m_t[..., None])
    w_inter = jnp.exp(inter - m_t)
    num = jnp.einsum('bhcts,bhcse->bhcte', s, v) + w_inter[..., None] * jnp.einsum('bhced,bhctd->bhcte', C_in, q)
    den = jnp.sum(s, axis=-1) + w_inter * jnp.einsum('bhcd,bhctd->bhct', n_in, q)
    h = num / jnp.maximum(jnp.abs(den), jnp.exp(-m_t))[..., None]
    return h.reshape(B, H, S, Dh)

def moba_attention(q, k, v):
    B, H, S, Dh = q.shape
    BS = MOBA_BLOCK
    NB = -(-S // BS)
    pad = NB * BS - S
    kp = jnp.pad(k, ((0, 0), (0, 0), (0, pad), (0, 0)))
    vp = jnp.pad(v, ((0, 0), (0, 0), (0, pad), (0, 0)))
    kb = kp.reshape(B, H, NB, BS, Dh)
    vb = vp.reshape(B, H, NB, BS, Dh)
    counts = np.minimum(BS, S - np.arange(NB) * BS).astype(np.float32)
    k_mean = jnp.sum(kb.astype(jnp.float32), axis=3) / counts[:, None]
    gate = jnp.einsum('bhsd,bhnd->bhsn', q.astype(jnp.float32), k_mean)
    pos = jnp.arange(S)
    past = jnp.arange(NB)[None, :] < (pos // BS)[:, None]
    gate = jnp.where(past, gate, NEG_INF)
    k_sel = min(MOBA_TOPK, NB)
    top_val, top_idx = lax.top_k(gate, k_sel)
    top_ok = top_val > 0.5 * NEG_INF
    scale = Dh ** -0.5
    Q = MOBA_QCHUNK
    bi = jnp.arange(B)[:, None, None, None]
    hi = jnp.arange(H)[None, :, None, None]

    def chunk(c):
        t0 = c * Q
        tq = t0 + jnp.arange(Q)
        qc = lax.dynamic_slice_in_dim(q, t0, Q, axis=2)
        idx = lax.dynamic_slice_in_dim(top_idx, t0, Q, axis=2)
        ok = lax.dynamic_slice_in_dim(top_ok, t0, Q, axis=2)
        kg = kb[bi, hi, idx]
        vg = vb[bi, hi, idx].reshape(B, H, Q, k_sel * BS, Dh)
        s_sel = jnp.einsum('bhqd,bhqnpd->bhqnp', qc, kg).reshape(B, H, Q, k_sel * BS)
        m_sel = jnp.repeat(ok, BS, axis=-1)
        blk0 = (t0 // BS) * BS
        k_own = lax.dynamic_slice_in_dim(kp, blk0, BS, axis=2)
        v_own = lax.dynamic_slice_in_dim(vp, blk0, BS, axis=2)
        s_own = jnp.einsum('bhqd,bhpd->bhqp', qc, k_own)
        m_own = (blk0 + jnp.arange(BS))[None, :] <= tq[:, None]
        s_all = jnp.concatenate([s_sel, s_own], axis=-1).astype(jnp.float32) * scale
        m_all = jnp.concatenate([m_sel, jnp.broadcast_to(m_own, (B, H, Q, BS))], axis=-1)
        p = masked_softmax(s_all, m_all).astype(v.dtype)
        return (jnp.einsum('bhqk,bhqkd->bhqd', p[..., :k_sel * BS], vg)
                + jnp.einsum('bhqp,bhpd->bhqd', p[..., k_sel * BS:], v_own))

    outs = lax.map(chunk, jnp.arange(S // Q))
    return outs.transpose(1, 2, 0, 3, 4).reshape(B, H, S, Dh)

def even_mixer(h, w_in, conv_w, gate_b, head_gain, w_out):
    B, S, _ = h.shape
    z = h @ w_in
    qk_m, v_m, o_m, if_m, q_b, k_b, v_b = jnp.split(z, EVEN_SPLITS, axis=-1)
    qk_m = jax.nn.silu(causal_depthwise_conv(qk_m, conv_w))
    q_m, k_m = jnp.split(qk_m, 2, axis=-1)
    pre = if_m.astype(jnp.float32) + gate_b.astype(jnp.float32)
    pre = MLSTM_GATE_CAP * jnp.tanh(pre / MLSTM_GATE_CAP)
    log_i = pre[..., :MLSTM_HEADS].transpose(0, 2, 1)
    log_f = jax.nn.log_sigmoid(pre[..., MLSTM_HEADS:]).transpose(0, 2, 1)
    h_t = mlstm_chunkwise(split_heads(q_m, MLSTM_HEADS, MLSTM_DH), split_heads(k_m, MLSTM_HEADS, MLSTM_DH),
                          split_heads(v_m, MLSTM_HEADS, MLSTM_DH), log_i, log_f)
    h_t = (h_t * lax.rsqrt(jnp.mean(h_t * h_t, axis=-1, keepdims=True) + NORM_EPS)
           * head_gain.astype(jnp.float32).reshape(MLSTM_HEADS, 1, MLSTM_DH))
    h_m = (merge_heads(h_t) * jax.nn.sigmoid(o_m.astype(jnp.float32))).astype(h.dtype)
    o_b = moba_attention(rotary(split_heads(q_b, MOBA_HEADS, MOBA_DH)), rotary(split_heads(k_b, MOBA_HEADS, MOBA_DH)),
                         split_heads(v_b, MOBA_HEADS, MOBA_DH))
    y = jnp.concatenate([h_m, merge_heads(o_b).astype(h.dtype)], axis=-1)
    return y @ w_out

def odd_mixer(h, w_in, cmp_pos, w_ck1, w_ck2, w_cv1, w_cv2, w_out):
    B, S, _ = h.shape
    dt = h.dtype
    G, R, Dh = NSA_GROUPS, NSA_REP, NSA_DH
    scale = Dh ** -0.5
    z = h @ w_in
    q, k_c, v_c, k_s, v_s, k_w, v_w, gate = jnp.split(z, ODD_SPLITS, axis=-1)
    q = q.reshape(B, S, G, R, Dh).transpose(0, 2, 3, 1, 4)
    k_c, v_c, k_s, v_s, k_w, v_w = [split_heads(t, G, Dh) for t in (k_c, v_c, k_s, v_s, k_w, v_w)]
    n_cmp = (S - CMP_LEN) // CMP_STRIDE + 1
    cmp_start = np.arange(n_cmp) * CMP_STRIDE
    cmp_end = cmp_start + CMP_LEN - 1
    blk_idx = cmp_start[:, None] + np.arange(CMP_LEN)[None, :]

    def compress(t, pe, w1, w2):
        tb = (t[:, :, blk_idx] + pe).reshape(B, G, n_cmp, CMP_LEN * Dh)
        return jax.nn.gelu(tb @ w1) @ w2

    k_cmp = compress(k_c, cmp_pos[0], w_ck1, w_ck2)
    v_cmp = compress(v_c, cmp_pos[1], w_cv1, w_cv2)
    pos = jnp.arange(S)
    cmp_ok = cmp_end[None, :] <= pos[:, None]
    p_cmp = masked_softmax(jnp.einsum('bgrsd,bgnd->bgrsn', q, k_cmp) * scale, cmp_ok)
    o_cmp = jnp.einsum('bgrsn,bgnd->bgrsd', p_cmp.astype(dt), v_cmp)
    n_blk = S // SEL_BLOCK
    blk_lo = np.arange(n_blk) * SEL_BLOCK
    overlap = ((cmp_start[:, None] <= blk_lo[None, :] + SEL_BLOCK - 1)
               & (cmp_end[:, None] >= blk_lo[None, :])).astype(np.float32)
    imp = jnp.einsum('bgrsn,nj->bgsj', p_cmp, overlap)
    cur = (pos // SEL_BLOCK)[:, None]
    jb = jnp.arange(n_blk)[None, :]
    forced = (jb == 0) | (jb == cur) | (jb == cur - 1)
    imp = jnp.where(jb <= cur, jnp.where(forced, FORCED_SCORE, imp), NEG_INF)
    n_sel = min(SEL_TOPN, n_blk)
    sel_val, sel_idx = lax.top_k(imp, n_sel)
    sel_ok = sel_val > 0.5 * NEG_INF
    q_r = rotary(q)
    k_sb = rotary(k_s).reshape(B, G, n_blk, SEL_BLOCK, Dh)
    v_sb = v_s.reshape(B, G, n_blk, SEL_BLOCK, Dh)
    k_wp = jnp.pad(rotary(k_w), ((0, 0), (0, 0), (WINDOW, 0), (0, 0)))
    v_wp = jnp.pad(v_w, ((0, 0), (0, 0), (WINDOW, 0), (0, 0)))
    Q = NSA_QCHUNK
    bi = jnp.arange(B)[:, None, None, None]
    gi = jnp.arange(G)[None, :, None, None]

    def chunk(c):
        t0 = c * Q
        tq = t0 + jnp.arange(Q)
        qc = lax.dynamic_slice_in_dim(q_r, t0, Q, axis=3)
        idx = lax.dynamic_slice_in_dim(sel_idx, t0, Q, axis=2)
        ok = lax.dynamic_slice_in_dim(sel_ok, t0, Q, axis=2)
        kg = k_sb[bi, gi, idx].reshape(B, G, Q, n_sel * SEL_BLOCK, Dh)
        vg = v_sb[bi, gi, idx].reshape(B, G, Q, n_sel * SEL_BLOCK, Dh)
        tk = (idx[..., None] * SEL_BLOCK + jnp.arange(SEL_BLOCK)).reshape(B, G, Q, n_sel * SEL_BLOCK)
        m_sel = jnp.repeat(ok, SEL_BLOCK, axis=-1) & (tk <= tq[:, None])
        p_s = masked_softmax(jnp.einsum('bgrqd,bgqkd->bgrqk', qc, kg) * scale, m_sel[:, :, None])
        o_s = jnp.einsum('bgrqk,bgqkd->bgrqd', p_s.astype(dt), vg)
        k_win = lax.dynamic_slice_in_dim(k_wp, t0, WINDOW + Q, axis=2)
        v_win = lax.dynamic_slice_in_dim(v_wp, t0, WINDOW + Q, axis=2)
        tw = t0 - WINDOW + jnp.arange(WINDOW + Q)
        gap = tq[:, None] - tw[None, :]
        m_win = (tw[None, :] >= 0) & (gap >= 0) & (gap < WINDOW)
        p_w = masked_softmax(jnp.einsum('bgrqd,bgkd->bgrqk', qc, k_win) * scale, m_win)
        o_w = jnp.einsum('bgrqk,bgkd->bgrqd', p_w.astype(dt), v_win)
        return o_s, o_w

    o_sel, o_win = lax.map(chunk, jnp.arange(S // Q))
    o_sel = o_sel.transpose(1, 2, 3, 0, 4, 5).reshape(B, G, R, S, Dh)
    o_win = o_win.transpose(1, 2, 3, 0, 4, 5).reshape(B, G, R, S, Dh)
    g = jax.nn.sigmoid(gate.astype(jnp.float32)).reshape(B, S, G, R, 3).transpose(0, 2, 3, 1, 4).astype(dt)
    o = g[..., 0:1] * o_cmp + g[..., 1:2] * o_sel + g[..., 2:3] * o_win
    o = o.transpose(0, 3, 1, 2, 4).reshape(B, S, NSA_W)
    return o @ w_out

def hier_moe(x, w_g, b_g, w_e, b_e, w1, w3, w2):
    B, S, D = x.shape
    T = B * S
    xt = x.reshape(T, D)
    xf = xt.astype(jnp.float32)
    g_logits = xf @ w_g.astype(jnp.float32) + b_g.astype(jnp.float32)
    g_prob = jax.nn.softmax(g_logits, axis=-1)
    g_top = jnp.argmax(g_logits, axis=-1)
    g_w = jnp.take_along_axis(g_prob, g_top[:, None], axis=-1)
    e_logits = (xf @ w_e.astype(jnp.float32) + b_e.astype(jnp.float32)).reshape(T, MOE_GROUPS, MOE_EXPERTS_PER_GROUP)
    e_in = jnp.take_along_axis(e_logits, g_top[:, None, None], axis=1)[:, 0]
    top_v, top_i = lax.top_k(e_in, MOE_TOPK)
    w_top = jax.nn.softmax(top_v, axis=-1) * g_w
    eid = g_top[:, None] * MOE_EXPERTS_PER_GROUP + top_i
    combine = jnp.einsum('tk,tke->te', w_top, jax.nn.one_hot(eid, MOE_EXPERTS, dtype=jnp.float32))
    out = jnp.zeros((T, D), jnp.float32)
    for e in range(MOE_EXPERTS):
        hdn = jax.nn.silu(xt @ w1[e]) * (xt @ w3[e])
        out = out + combine[:, e:e + 1] * (hdn @ w2[e]).astype(jnp.float32)
    return out.astype(x.dtype).reshape(B, S, D)

def setup_inputs(seed: int = 0) -> dict:
    key = jax.random.key(seed)
    keys = iter(jax.random.split(key, 64))
    D = D_MODEL

    def nrm(shape, scale):
        return jax.random.normal(next(keys), shape, jnp.float32) * scale

    def gain(n):
        return 1.0 + nrm((n,), 0.02)

    inp = {}
    inp['x'] = nrm((BATCH, SEQ, D), 1.0)
    inp['mix_norm_0'] = gain(D)
    inp['w_in_0'] = nrm((D, EVEN_IN), D ** -0.5)
    inp['mlstm_conv_0'] = nrm((MLSTM_CONV, 2 * MLSTM_W), MLSTM_CONV ** -0.5)
    inp['mlstm_gate_b_0'] = jnp.concatenate([nrm((MLSTM_HEADS,), 0.1),
                                             jnp.linspace(3.0, 6.0, MLSTM_HEADS, dtype=jnp.float32) + nrm((MLSTM_HEADS,), 0.1)])
    inp['mlstm_head_norm_0'] = gain(MLSTM_W)
    inp['w_out_0'] = nrm((MLSTM_W + MOBA_W, D), (MLSTM_W + MOBA_W) ** -0.5)

    def add_moe(i):
        inp[f'ffn_norm_{i}'] = gain(D)
        inp[f'router_group_{i}'] = nrm((D, MOE_GROUPS), D ** -0.5)
        inp[f'router_group_b_{i}'] = nrm((MOE_GROUPS,), 0.01)
        inp[f'router_expert_{i}'] = nrm((D, MOE_EXPERTS), D ** -0.5)
        inp[f'router_expert_b_{i}'] = nrm((MOE_EXPERTS,), 0.01)
        inp[f'moe_w1_{i}'] = nrm((MOE_EXPERTS, D, MOE_HIDDEN), D ** -0.5)
        inp[f'moe_w3_{i}'] = nrm((MOE_EXPERTS, D, MOE_HIDDEN), D ** -0.5)
        inp[f'moe_w2_{i}'] = nrm((MOE_EXPERTS, MOE_HIDDEN, D), MOE_HIDDEN ** -0.5)

    add_moe(0)
    inp['mix_norm_1'] = gain(D)
    inp['w_in_1'] = nrm((D, ODD_IN), D ** -0.5)
    inp['nsa_cmp_pos_1'] = nrm((2, CMP_LEN, NSA_DH), 0.1)
    inp['nsa_cmp_k1_1'] = nrm((CMP_LEN * NSA_DH, CMP_HIDDEN), (CMP_LEN * NSA_DH) ** -0.5)
    inp['nsa_cmp_k2_1'] = nrm((CMP_HIDDEN, NSA_DH), CMP_HIDDEN ** -0.5)
    inp['nsa_cmp_v1_1'] = nrm((CMP_LEN * NSA_DH, CMP_HIDDEN), (CMP_LEN * NSA_DH) ** -0.5)
    inp['nsa_cmp_v2_1'] = nrm((CMP_HIDDEN, NSA_DH), CMP_HIDDEN ** -0.5)
    inp['w_out_1'] = nrm((NSA_W, D), NSA_W ** -0.5)
    add_moe(1)
    inp['final_norm'] = gain(D)
    return inp

def reference(x, mix_norm_0, w_in_0, mlstm_conv_0, mlstm_gate_b_0, mlstm_head_norm_0, w_out_0,
              ffn_norm_0, router_group_0, router_group_b_0, router_expert_0, router_expert_b_0,
              moe_w1_0, moe_w3_0, moe_w2_0,
              mix_norm_1, w_in_1, nsa_cmp_pos_1, nsa_cmp_k1_1, nsa_cmp_k2_1, nsa_cmp_v1_1, nsa_cmp_v2_1, w_out_1,
              ffn_norm_1, router_group_1, router_group_b_1, router_expert_1, router_expert_b_1,
              moe_w1_1, moe_w3_1, moe_w2_1,
              final_norm):
    mix_norms = (mix_norm_0, mix_norm_1)
    mixers = ((even_mixer, (w_in_0, mlstm_conv_0, mlstm_gate_b_0, mlstm_head_norm_0, w_out_0)),
              (odd_mixer, (w_in_1, nsa_cmp_pos_1, nsa_cmp_k1_1, nsa_cmp_k2_1, nsa_cmp_v1_1, nsa_cmp_v2_1, w_out_1)))
    ffn_norms = (ffn_norm_0, ffn_norm_1)
    moes = ((router_group_0, router_group_b_0, router_expert_0, router_expert_b_0, moe_w1_0, moe_w3_0, moe_w2_0),
            (router_group_1, router_group_b_1, router_expert_1, router_expert_b_1, moe_w1_1, moe_w3_1, moe_w2_1))
    h = x
    for layer in range(DEPTH):
        mixer, params = mixers[layer]
        h = h + mixer(rms_norm(h, mix_norms[layer]), *params)
        h = h + hier_moe(rms_norm(h, ffn_norms[layer]), *moes[layer])
    return rms_norm(h, final_norm)


_drawn_inputs = setup_inputs


def setup_inputs(seed=0):
    import zlib

    import numpy as np

    out = dict(_drawn_inputs(seed))
    spreads = {}
    factors = {'router_group_b_0': 2.775,
     'mix_norm_1': 3.152,
     'router_group_b_1': 44.259,
     'router_expert_b_1': 29.394,
     'final_norm': 7.584,
     'ffn_norm_1': 5.269}
    for name, (base, spread) in spreads.items():
        noise = np.random.default_rng([zlib.crc32(name.encode()), seed]).standard_normal(out[name].shape)
        drawn = base * np.exp(spread * noise) if base else spread * noise
        out[name] = jnp.asarray(drawn.astype(out[name].dtype))
    for name, factor in factors.items():
        out[name] = (out[name] * factor).astype(out[name].dtype)
    return out
```

```python
import concourse.bass as bass
from concourse import mybir
from contextlib import ExitStack

P = 128
T = 256
TT = T // P
D = 1024
KD = D // P
DH = 128
SCALE = float(DH) ** -0.5
EPS = 1e-6
NEG = -1e30
MH = 4
GATE_CAP = 15.0
CONV = 4
NG, REP, NH = 2, 4, 8
CMP_LEN, CMP_STRIDE, CMP_HID = 32, 16, 256
NCMP = (T - CMP_LEN) // CMP_STRIDE + 1
GROUPS, PER_GROUP = 4, 4
EXPERTS = GROUPS * PER_GROUP
HID = D // 4
CAP = 64
LOGITS = GROUPS + EXPERTS

NSLOT = 12
SLOT = 2048
UNROLL = 4
BANK = 512
ARENA = 16832
N_PARAMS, N_SMALL = 5, 16

CONST_COLS = {}
_at = 0
for _name, _n in (("ident", P), ("ones", P), ("before", P), ("swap", P), ("mask_sT", T), ("mask_ts", 384),
                  ("cos", T), ("sin", T), ("iota", CAP), ("desc", EXPERTS), ("head_row", MH * P),
                  ("cmp_add", TT * NCMP), ("cmp_keep", TT * NCMP), ("power", 8)):
    CONST_COLS[_name] = (_at, _n)
    _at += _n
NCONST = _at


class Jobs:

    def __init__(self, filled, emptied):
        self.filled_sem, self.emptied_sem = filled, emptied
        self.n_filled, self.n_emptied = [0] * 8, [0] * 8
        self.last = [None] * 8
        self.at = {}
        self.next = 0

    def plan(self, name, emptied=None, bank=None):
        if bank is None:
            bank = self.next
        self.next = (bank + 1) % 8
        self.n_filled[bank] += 1
        if emptied is None:
            self.n_emptied[bank] += 1
            emptied = (self.emptied_sem[bank], self.n_emptied[bank])
        self.at[name] = dict(bank=bank, filled=(self.filled_sem[bank], self.n_filled[bank]), emptied=emptied,
                             before=self.last[bank])
        self.last[bank] = emptied


def hybrid_kernel(nc, A, out):
    f32 = mybir.dt.float32
    i32 = mybir.dt.int32
    ALU = mybir.AluOpType
    ACT = mybir.ActivationFunctionType
    AX = mybir.AxisListType.X
    ds = bass.ds

    ctx = ExitStack()
    with ctx:
        def sb(name, shape, dt=f32):
            return ctx.enter_context(nc.sbuf_tensor(name, shape, dt))

        def sem(name):
            return ctx.enter_context(nc.semaphore(name))

        ring = sb("ring", [P, NSLOT, SLOT])
        h = sb("h", [P, TT, D])
        hs = sb("hs", [P, TT, D])
        xT = sb("xT", [P, KD, T])
        const = sb("const", [P, NCONST])
        norm_gain = sb("norm_gain", [P, 4, KD])
        final_gain = sb("final_gain", [P, D])
        head_gain = sb("head_gain", [P, MH * DH])
        cols_raw = sb("cols_raw", [96, P])
        cols = sb("cols", [P, 96])
        w_gate0 = sb("w_gate0", [P, KD, 2 * MH])
        w_gate1 = sb("w_gate1", [P, KD, 3 * NH])
        gate_bias = sb("gate_bias", [MH, 2])
        router_g = [sb(f"router_g{i}", [P, KD, GROUPS]) for i in range(2)]
        router_e = [sb(f"router_e{i}", [P, KD, EXPERTS]) for i in range(2)]
        router_w = [sb(f"router_w{i}", [P, KD, LOGITS]) for i in range(2)]
        router_b = [sb(f"router_b{i}", [P, LOGITS]) for i in range(2)]
        w_cmp2 = sb("w_cmp2", [P, 2, 2, DH])
        ssq = sb("ssq", [P, 5, TT])
        rstd = sb("rstd", [P, 5, TT])
        arena = sb("arena", [P, ARENA])

        def C(name, rows=P):
            a, n = CONST_COLS[name]
            return const[0:rows, a:a + n]

        ident = C("ident")
        top = [0]

        def view(n, shape=None, parts=P, at=None):
            if at is None:
                at = top[0]
                top[0] += n
                assert top[0] <= ARENA, top[0]
            a = arena[0:parts, at:at + n]
            if shape is None:
                return a
            names = "abcd"[:len(shape)]
            return a.rearrange(f"p ({' '.join(names)}) -> p {' '.join(names)}", **dict(zip(names, shape)))

        yT = view(KD * T, (KD, T))
        NPROB, NPT = 4, 3
        probs = [view(384) for _ in range(NPROB)]
        probsT = [view(384) for _ in range(NPT)]
        amax = view(NPROB * 2, (NPROB, 2))
        abias = view(NPROB * 2, (NPROB, 2))
        asum = view(NPROB * 2, (NPROB, 2))
        arec = view(NPROB * 2, (NPROB, 2))
        mark = top[0]
        qkT = view(8 * T, (8, T))
        rope_raw = view(8 * T, (8, T))
        rope_out = view(8 * T, (8, T))
        rope_cos = [hs[:, 0, i * 2 * T:(i + 1) * 2 * T] for i in range(2)]
        rope_sin = [hs[:, 1, i * 2 * T:(i + 1) * 2 * T] for i in range(2)]
        v_ext = view(TT * MH * (DH + 1), (TT, MH, DH + 1))
        v_b = view(TT * MH * DH, (TT, MH * DH))
        og = view(TT * MH * DH, (TT, MH * DH))
        rows0 = [view(2 * T, parts=MH) for _ in range(2)]
        row = [view(T, parts=MH) for _ in range(6)]
        acols = view(16, (4, MH))
        arg = [xT[:, 2 * i:2 * i + 2, :].rearrange("p a b -> p (a b)")[:, 0:384] for i in range(2)]
        lstm_pT = [xT[:, 4 + 2 * i:6 + 2 * i, :].rearrange("p a b -> p (a b)")[:, 0:384] for i in range(2)]
        junk = [xT[:, 2 * i + 1, T - DH:T] for i in range(TT)]
        small0 = view(64, (8, 8))
        num = view(TT * MH * (DH + 1), (TT, MH, DH + 1), at=mark + 8 * T * 1)
        top[0] = mark
        lg = view(TT * LOGITS, (TT, LOGITS))
        g4 = [view(TT * GROUPS, (TT, GROUPS)) for _ in range(3)]
        e16 = [view(TT * EXPERTS, (TT, EXPERTS)) for _ in range(5)]
        t1 = [view(TT) for _ in range(10)]
        rexp = [g4[1], t1[6]]
        posm = view(TT * EXPERTS, (TT, EXPERTS))
        comb = view(TT * EXPERTS, (TT, EXPERTS))
        sel = view(TT * EXPERTS, (TT, EXPERTS))
        pick = [view(TT * CAP, (TT, CAP)) for _ in range(2)]
        wpick = [view(TT * 2 * CAP, (TT, 2 * CAP)) for _ in range(2)]
        scatT = [view(T) for _ in range(2)]
        xg = [view(KD * CAP, (KD, CAP)) for _ in range(2)]
        silu_t = view(2 * CAP)
        hdn = [view(2 * CAP, (2, CAP)) for _ in range(2)]
        y_sb = [view(D) for _ in range(2)]
        top[0] = mark
        q_raw = view(NH * T, (NH, T))
        kk_raw = view(4 * T, (4, T))
        q_rot = view(NH * T, (NH, T))
        kk_rot = view(4 * T, (4, T))
        v_sw = view(2 * TT * NG * DH, (2, TT, NG * DH))
        blocks = [view(CMP_LEN * NG * NCMP, (CMP_LEN, NG, NCMP)) for _ in range(2)]
        gelu_t = [view(2 * NG * NCMP, (2, NG * NCMP)) for _ in range(2)]
        kcmpT = view(NG * NCMP)
        vcmp = view(NG * DH, parts=NCMP)
        gates = view(TT * 3 * NH, (TT, NH, 3))
        pc = view(TT * NH * NCMP, (TT, NH, NCMP))
        pcs = [view(TT * NH, (TT, NH)) for _ in range(3)]
        pcT = [view(2 * T, parts=NCMP) for _ in range(4)]
        count_f = [sb(f"count_f{i}", [1, 4]) for i in range(2)]
        count_i = [sb(f"count_i{i}", [1, 1], i32) for i in range(2)]

        psum = ctx.enter_context(nc.psum_tensor("psum", [P, 8 * BANK], f32))

        def bank_ap(b, n=1):
            return psum[:, b * BANK:(b + n) * BANK]

        bank_filled = [sem(f"bank_filled{b}") for b in range(8)]
        bank_emptied = [sem(f"bank_emptied{b}") for b in range(8)]
        slot_loaded = [sem(f"slot_loaded{s}") for s in range(NSLOT)]
        x_loaded, const_loaded, params_loaded = sem("x_loaded"), sem("const_loaded"), sem("params_loaded")
        small_loaded = sem("small_loaded")
        vec_step, act_step, pool_step = sem("vec_step"), sem("act_step"), sem("pool_step")
        sq_done, rstd_ready = sem("sq_done"), sem("rstd_ready")
        hsA_ready, hsV_ready = sem("hsA_ready"), sem("hsV_ready")
        h_updated, h_copiedA, h_copiedV = sem("h_updated"), sem("h_copiedA"), sem("h_copiedV")
        wout_used, cmp_used = sem("wout_used"), sem("cmp_used")
        ones_set, bias_scaled = sem("ones_set"), sem("bias_scaled")
        conv_seeded, qk_ready = sem("conv_seeded"), sem("qk_ready")
        cos_done, rope_ready = sem("cos_done"), sem("rope_ready")
        og_ready = sem("og_ready")
        tanh_done, logf_done, nm_ready, expnm_ready, m_ready = (sem("tanh_done"), sem("logf_done"), sem("nm_ready"),
                                                                sem("expnm_ready"), sem("m_ready"))
        arg_ready, decay_ready = sem("arg_ready"), sem("decay_ready")
        lstm_sq, denom_sq, lstm_rstd, lstm_y = sem("lstm_sq"), sem("denom_sq"), sem("lstm_rstd"), sem("lstm_y")
        abias_ready, aexp_done, arec_ready, aprob_ready = (sem("abias_ready"), sem("aexp_done"), sem("arec_ready"),
                                                           sem("aprob_ready"))
        gates_ready, blocks_ready, gelu_done, pc_exp_in, pc_exp_out, pc_ready = (
            sem("gates_ready"), sem("blocks_ready"), sem("gelu_done"), sem("pc_exp_in"), sem("pc_exp_out"),
            sem("pc_ready"))
        r_exp_in, r_exp_out, sel_ready, count_ready = (sem("r_exp_in"), sem("r_exp_out"), sem("sel_ready"),
                                                       sem("count_ready"))
        picked, wpicked, xg_filled, xg_ready = sem("picked"), sem("wpicked"), sem("xg_filled"), sem("xg_ready")
        w1_used, hid_filled, silu_done, hdn_ready = sem("w1_used"), sem("hid_filled"), sem("silu_done"), sem("hdn_ready")
        scatT_ready, y_filled, yA_ready, yV_ready, scattered = (sem("scatT_ready"), sem("y_filled"), sem("yA_ready"),
                                                                sem("yV_ready"), sem("scattered"))
        more_loaded = [sem(f"more_loaded{i}") for i in range(2)]
        more_pe = [sem(f"more_pe{i}") for i in range(2)]
        more_vec = [sem(f"more_vec{i}") for i in range(2)]
        more_act = [sem(f"more_act{i}") for i in range(2)]
        more_done = [sem(f"more_done{i}") for i in range(2)]
        more_base = [sem(f"more_base{i}") for i in range(2)]
        router_packed, out_stored = sem("router_packed"), sem("out_stored")

        w_in_0 = A["w_in_0"].rearrange("(p k) n -> p k n", k=KD)
        w_in_1 = A["w_in_1"].rearrange("(p k) n -> p k n", k=KD)
        W0 = MH * DH
        Z0 = ([("qk", i, 256 * i) for i in range(4)]
              + [("rope", i, 4 * W0 + 2 * MH + 256 * i) for i in range(4)]
              + [("om", i, 3 * W0 + 256 * i) for i in range(2)]
              + [("vm", i, 2 * W0 + 256 * i) for i in range(2)]
              + [("vb", i, 6 * W0 + 2 * MH + 256 * i) for i in range(2)])
        QW, KW = NH * DH, NG * DH
        Z1 = ([("cmp", 0, QW), ("cmp", 1, QW + KW)]
              + [("rope", i, 256 * i) for i in range(4)]
              + [("rope", 4, QW + 2 * KW), ("rope", 5, QW + 4 * KW)]
              + [("vsw", 0, QW + 3 * KW), ("vsw", 1, QW + 5 * KW)])
        N_Z0, N_Z1, N_MOE = len(Z0), len(Z1), 3 * EXPERTS
        FIRST = {"z0": 0, "o0": N_Z0, "moe0": N_Z0 + 4}
        FIRST["z1"] = FIRST["moe0"] + N_MOE
        FIRST["cmp"] = FIRST["z1"] + N_Z1
        FIRST["o1"] = FIRST["cmp"] + 8
        FIRST["moe1"] = FIRST["o1"] + 4

        def slot_of(n):
            return n % NSLOT

        def loads_before(n):
            return n // NSLOT

        jobs = Jobs(bank_filled, bank_emptied)
        jobs.plan("cols")

        def plan_norm(n):
            for j in range(4):
                jobs.plan(("x", n, j))

        def plan_out(layer):
            for i in range(4):
                jobs.plan(("o", layer, i), emptied=(h_updated, 4 * layer + i + 1))

        plan_norm(0)
        jobs.plan("gate0")
        Z0_ORDER = []
        for i, z in enumerate(Z0):
            Z0_ORDER.append(("z", i))
            if z[0] == "rope" and z[1] >= 1:
                Z0_ORDER.append(("swap", z[1] - 1))
            if z[0] == "om" and z[1] == 0:
                Z0_ORDER.append(("swap", 3))
        for kind, i in Z0_ORDER:
            jobs.plan((kind, 0, i))
        jobs.plan("acols")
        for hd in range(MH):
            if hd % 2 == 0:
                jobs.plan(("mB", hd // 2), emptied=(arg_ready, hd + 2))
            jobs.plan(("mS", hd))
            jobs.plan(("aS", 0, hd))
            if hd >= 1:
                jobs.plan(("mN", hd - 1), emptied=(lstm_sq, hd))
                jobs.plan(("aT", 0, hd - 1))
                jobs.plan(("aO", 0, hd - 1))
        jobs.plan(("mN", MH - 1), emptied=(lstm_sq, MH))
        jobs.plan(("aT", 0, MH - 1))
        jobs.plan(("aO", 0, MH - 1))
        for i in range(2):
            jobs.plan(("yt", i))
        plan_out(0)

        def plan_moe(layer):
            n = 1 + 2 * layer
            for j in range(4):
                jobs.plan(("x", n, j), bank=j)
            jobs.plan(("logits", layer), bank=2)
            jobs.plan(("pos", layer), bank=3)
            jobs.next = 0

        plan_moe(0)
        BEFORE_ACC = [list(jobs.last)]
        plan_norm(2)
        Z1_ORDER = []
        for i, z in enumerate(Z1):
            Z1_ORDER.append(("z", i))
            if z[0] == "rope" and z[1] >= 1:
                Z1_ORDER.append(("swap", z[1] - 1))
            if z[0] == "vsw" and z[1] == 0:
                Z1_ORDER.append(("swap", 5))
        for kind, i in Z1_ORDER:
            jobs.plan((kind, 1, i))
        jobs.plan("gate1")
        for kv in range(2):
            for ht in range(2):
                jobs.plan(("cmp1", kv, ht), emptied=(gelu_done, 2 * kv + ht + 1))
        jobs.plan("kcmp")
        jobs.plan("vcmp")
        jobs.plan("cS")
        jobs.plan(("aS", 1, 0))
        jobs.plan(("aS", 1, 1))
        for i in range(4):
            jobs.plan(("cT", i))
        for hd in range(NH):
            if hd + 1 < NH:
                jobs.plan(("aS", 1, 2 * hd + 2))
                jobs.plan(("aS", 1, 2 * hd + 3))
            jobs.plan(("aT", 1, 2 * hd))
            jobs.plan(("aT", 1, 2 * hd + 1))
            jobs.plan(("aO", 1, hd))
        plan_out(1)
        plan_moe(1)
        BEFORE_ACC.append(list(jobs.last))

        def bank(name):
            return bank_ap(jobs.at[name]["bank"])

        def open_bank(pe, name):
            if jobs.at[name]["before"] is not None:
                pe.wait_ge(*jobs.at[name]["before"])
            return bank(name)

        def fill(ins, name):
            ins.then_inc(jobs.at[name]["filled"][0], 1)

        def wait_filled(eng, name):
            eng.wait_ge(*jobs.at[name]["filled"])
            return bank(name)

        def emptied(ins, name):
            ins.then_inc(jobs.at[name]["emptied"][0], 1)

        def wait_emptied(eng, name):
            eng.wait_ge(*jobs.at[name]["emptied"])

        def mm(o, lhsT, rhs, first=True, last=True):
            return nc.tensor.matmul(o, lhsT, rhs, start=first, stop=last)

        def flip(o, i):
            n = i.shape[0]
            return nc.tensor.transpose(o, i, ident[0:n, 0:n])

        NX = 5

        def wait_h(eng, n, tile):
            if n == 0:
                eng.wait_ge(x_loaded, 16)
            elif n in (1, 3):
                eng.wait_ge(h_updated, 4 * (n // 2) + 2 * tile + 2)
            elif tile == 0:
                eng.wait_ge(h_copiedA, n // 2)
            else:
                eng.wait_ge(h_copiedV, n // 2)

        def unit(layer, u):
            if layer == 0:
                return (rope_out[:, u, :], rope_out[:, MH + u, :],
                        [v_b[:, t, u * DH:(u + 1) * DH] for t in range(TT)], None)
            hd, br = u // 2, u % 2
            g = hd // REP
            return (q_rot[:, hd, :], kk_rot[:, 2 * br + g, :],
                    [v_sw[:, br, t, g * DH:(g + 1) * DH] for t in range(TT)],
                    [gates[:, t, hd, 1 + br:2 + br] for t in range(TT)])

        def useq(layer, u):
            return u + 1 + (MH if layer else 0)

        block = ctx.enter_context(nc.Block())

        @block.sync
        def _(sp):
            sp.dma_start(h[:, :, :], A["x"][0].rearrange("(t p) d -> p t d", p=P)).then_inc(x_loaded, 16)

            def load(n, dst, src):
                sp.dma_start(dst, src).then_inc(slot_loaded[slot_of(n)], 16)

            def wait_used(n):
                m = n - NSLOT
                if m < 0:
                    return
                for name in ("moe1", "o1", "cmp", "z1", "moe0", "o0", "z0"):
                    if m >= FIRST[name]:
                        i = m - FIRST[name]
                        break
                layer = int(name[-1] == "1")
                if name[0] == "z":
                    sp.wait_ge(*jobs.at[("z", layer, i)]["filled"])
                elif name[0] == "o":
                    if i < 3:
                        sp.wait_ge(wout_used, 3 * layer + i + 1)
                    else:
                        sp.wait_ge(*jobs.at[("o", layer, 3)]["filled"])
                elif name == "cmp":
                    if i % 4 < 3:
                        sp.wait_ge(cmp_used, 3 * (i // 4) + i % 4 + 1)
                    else:
                        sp.wait_ge(*jobs.at[("cmp1", i // 4, 1)]["filled"])
                else:
                    e = i // 3 + EXPERTS * layer
                    sp.wait_ge((w1_used, hid_filled, y_filled)[i % 3], e + 1)

            def slot(n, shape):
                a = ring[:, slot_of(n), :]
                return a.rearrange("p (a b) -> p a b", a=shape)

            def load_z(layer, Z, w):
                for i, (_, _, col) in enumerate(Z):
                    n = FIRST[f"z{layer}"] + i
                    wait_used(n)
                    load(n, slot(n, KD), w[:, :, col:col + 256])

            def load_out(layer):
                w = A[f"w_out_{layer}"].rearrange("(j k p) n -> p j k n", p=P, k=2)
                for j in range(4):
                    n = FIRST[f"o{layer}"] + j
                    wait_used(n)
                    load(n, slot(n, 2), w[:, j])

            def expert(layer, n, e):
                for c, (name, k) in enumerate((("moe_w1", KD), ("moe_w3", KD), ("moe_w2", 2))):
                    w = A[f"{name}_{layer}"]
                    if k == KD:
                        src = w.rearrange("e (p k) n -> p e (k n)", k=k)[:, ds(e, 1), :]
                        dst = ring[:, slot_of(n + c):slot_of(n + c) + 1, :]
                    else:
                        src = w.rearrange("e (k p) n -> p e k n", k=k)[:, ds(e, 1), :, :]
                        dst = ring[:, slot_of(n + c):slot_of(n + c) + 1, :].rearrange("p e (k n) -> p e k n", k=k)
                    yield c, dst, src

            def load_moe(layer):
                n0 = FIRST[f"moe{layer}"]
                for e in range(UNROLL):
                    for c, dst, src in expert(layer, n0 + 3 * e, e):
                        wait_used(n0 + 3 * e + c)
                        load(n0 + 3 * e + c, dst, src)
                with sp.Fori(1, EXPERTS // UNROLL) as it:
                    for j in range(UNROLL):
                        e = it * UNROLL + j
                        for c, dst, src in expert(layer, n0 + 3 * j, e):
                            sp.wait_ge((w1_used, hid_filled, y_filled)[c],
                                       EXPERTS * layer + e - UNROLL + 1)
                            load(n0 + 3 * j + c, dst, src)
                sp.wait_ge(count_ready, layer + 1)
                nx = sp.value_load(count_i[layer][0:1, 0:1], min_val=0, max_val=T // CAP - 1)
                with sp.If(nx > 0):
                    sp.wait_ge(y_filled, EXPERTS * (layer + 1))
                    with sp.Fori(0, nx) as r:
                        with sp.Fori(0, EXPERTS) as e:
                            sp.wait_ge(more_pe[layer], (r * EXPERTS + e) * 4 + 1)
                            for c, dst, src in expert(layer, n0, e):
                                sp.dma_start(dst, src).then_inc(more_loaded[layer], 16)
                    sp.wait_ge(more_done[layer], 1)

            load_z(0, Z0, w_in_0)
            load_out(0)
            load_moe(0)
            load_z(1, Z1, w_in_1)
            for kv, w in enumerate((A["nsa_cmp_k1_1"], A["nsa_cmp_v1_1"])):
                wl = w.rearrange("(l p) n -> p l n", p=P)
                for i in range(4):
                    n = FIRST["cmp"] + 4 * kv + i
                    wait_used(n)
                    load(n, slot(n, 8), wl[:, 8 * i:8 * i + 8, :])
            load_out(1)
            load_moe(1)
            ov = out[0].rearrange("(t p) d -> p t d", p=P)
            for t in range(TT):
                sp.wait_ge(h_copiedV, 3 + t)
                sp.dma_start(ov[:, t, :], h[:, t, :]).then_inc(out_stored, 16)
            sp.wait_ge(out_stored, 16 * TT)

        @block.gpsimd
        def _(pool):
            steps = [0]

            def step(ins):
                steps[0] += 1
                ins.then_inc(pool_step, 1)
                pool.wait_ge(pool_step, steps[0])

            nc.gpsimd.memset(v_ext[:, :, :, DH:DH + 1], 1.0).then_inc(ones_set, 1)
            nc.gpsimd.memset(row[5], 1.0).then_inc(ones_set, 1)
            pool.wait_ge(params_loaded, 16 * N_PARAMS)
            nc.gpsimd.tensor_scalar(gate_bias[:, :], gate_bias[:, :], 1.0 / GATE_CAP, 1.0, ALU.mult,
                                    ALU.mult).then_inc(bias_scaled, 1)

            def norm(n):
                pool.wait_ge(sq_done, 2 * (n + 1))
                if n == 0:
                    pool.wait_ge(const_loaded, 16)
                step(nc.gpsimd.tensor_scalar(rstd[:, n, :], ssq[:, n, :], 1.0 / D, EPS, ALU.mult, ALU.add))
                nc.gpsimd.tensor_tensor(rstd[:, n, :], rstd[:, n, :], C("power")[:, 0:TT], ALU.pow)\
                    .then_inc(rstd_ready, 1)

            def rope(layer, i, raw, cosd):
                z = [k for k, zz in enumerate((Z0, Z1)[layer]) if zz[0] == "rope"][i]
                wait_emptied(pool, ("z", layer, z))
                done = 4 * layer + i
                if i >= 2:
                    pool.wait_ge(rope_ready, done - 1)
                c = C("cos").unsqueeze(1).to_broadcast([P, 2, T])
                nc.gpsimd.tensor_tensor(cosd[i % 2].rearrange("p (a b) -> p a b", a=2), raw, c, ALU.mult)\
                    .then_inc(cos_done, 1)

            norm(0)
            for i in range(4):
                rope(0, i, rope_raw[:, 2 * i:2 * i + 2, :], rope_cos)
            pool.wait_ge(small_loaded, 16 * N_SMALL)
            for i in range(2):
                nc.gpsimd.tensor_copy(router_w[i][:, :, 0:GROUPS], router_g[i][:, :, :])
                nc.gpsimd.tensor_copy(router_w[i][:, :, GROUPS:LOGITS], router_e[i][:, :, :]).then_inc(router_packed, 1)
            for i in range(2):
                wait_emptied(pool, ("z", 0, [k for k, z in enumerate(Z0) if z[0] == "om"][i]))
                o = og[:, :, 256 * i:256 * i + 256]
                g = head_gain[:, 256 * i:256 * i + 256].unsqueeze(1).to_broadcast([P, TT, 256])
                nc.gpsimd.tensor_tensor(o, o, g, ALU.mult).then_inc(og_ready, 1)

            def normalise(layer, u):
                _, _, _, gate = unit(layer, u)
                k = useq(layer, u)
                pool.wait_ge(arec_ready, k)
                p = probs[u % NPROB]
                for t, (a, b) in enumerate(((0, 128), (128, 384))):
                    ins = nc.gpsimd.tensor_scalar(p[:, a:b], p[:, a:b], arec[:, u % NPROB, t:t + 1],
                                                  1.0 if gate is None else gate[t], ALU.mult, ALU.mult)
                ins.then_inc(aprob_ready, 1)

            for u in range(MH):
                normalise(0, u)
            pool.wait_ge(denom_sq, 1)
            step(nc.gpsimd.tensor_scalar(small0[:, 3, :], small0[:, 3, :], 1.0 / DH, EPS, ALU.mult, ALU.add))
            nc.gpsimd.tensor_tensor(small0[:, 4, :], small0[:, 3, :], C("power"), ALU.pow).then_inc(lstm_rstd, 1)
            norm(1)
            norm(2)
            for i in range(6):
                raw = q_raw[:, 2 * i:2 * i + 2, :] if i < 4 else kk_raw[:, 2 * i - 8:2 * i - 6, :]
                rope(1, i, raw, rope_cos)
            for u in range(2 * NH):
                normalise(1, u)
            norm(3)
            norm(4)

        @block.scalar
        def _(act):
            steps = [0]

            def step(ins):
                steps[0] += 1
                ins.then_inc(act_step, 1)
                act.wait_ge(act_step, steps[0])

            act.dma_start(const[:, :], A["const"]).then_inc(const_loaded, 16)
            act.dma_start(norm_gain[:, 0, :], A["mix_norm_0"].rearrange("(p k) -> p k", k=KD)).then_inc(params_loaded, 16)
            act.dma_start(gate_bias[:, :], A["mlstm_gate_b_0"].rearrange("(a h) -> h a", a=2),
                          allow_slow_non_contiguous=True).then_inc(params_loaded, 16)
            act.dma_start(w_gate0[:, :, :], w_in_0[:, :, 4 * W0:4 * W0 + 2 * MH]).then_inc(params_loaded, 16)
            act.dma_start(cols_raw[0:32, :], A["mlstm_conv_0"].rearrange("j (c p) -> (j c) p", p=P)).then_inc(params_loaded, 16)
            act.dma_start(cols_raw[32:96, :], A["nsa_cmp_pos_1"].rearrange("a l d -> (a l) d")).then_inc(params_loaded, 16)
            small = [(norm_gain[:, 1, :], A["ffn_norm_0"].rearrange("(p k) -> p k", k=KD)),
                     (norm_gain[:, 2, :], A["mix_norm_1"].rearrange("(p k) -> p k", k=KD)),
                     (norm_gain[:, 3, :], A["ffn_norm_1"].rearrange("(p k) -> p k", k=KD)),
                     (head_gain[:, :], A["mlstm_head_norm_0"].partition_broadcast(P)),
                     (w_gate1[:, :, :], w_in_1[:, :, QW + 6 * KW:QW + 6 * KW + 3 * NH]),
                     (final_gain[:, :], A["final_norm"].partition_broadcast(P))]
            for i in range(2):
                small += [(router_g[i][:, :, :], A[f"router_group_{i}"].rearrange("(p k) n -> p k n", k=KD)),
                          (router_e[i][:, :, :], A[f"router_expert_{i}"].rearrange("(p k) n -> p k n", k=KD)),
                          (router_b[i][:, 0:GROUPS], A[f"router_group_b_{i}"].partition_broadcast(P)),
                          (router_b[i][:, GROUPS:LOGITS], A[f"router_expert_b_{i}"].partition_broadcast(P))]
            assert len(small) == N_SMALL - 2
            small2 = [(w_cmp2[:, 0, :, :], A["nsa_cmp_k2_1"].rearrange("(k p) n -> p k n", p=P)),
                      (w_cmp2[:, 1, :, :], A["nsa_cmp_v2_1"].rearrange("(k p) n -> p k n", p=P))]

            def square(n, tile):
                nc.scalar.activation(hs[:, tile, :], h[:, tile, :], ACT.Square,
                                     accum_out=ssq[:, n, tile:tile + 1]).then_inc(sq_done, 1)

            def norm(n):
                for tile in range(TT):
                    wait_h(act, n, tile)
                    square(n, tile)
                act.wait_ge(rstd_ready, n + 1)
                nc.scalar.activation(hs[:, 0, :], h[:, 0, :], ACT.Copy, scale=rstd[:, n, 0:1]).then_inc(hsA_ready, 1)

            def norm_evac(n):
                if n == 0:
                    act.wait_ge(params_loaded, 16 * N_PARAMS)
                if n == 1:
                    act.wait_ge(small_loaded, 16 * N_SMALL)
                for j in (1, 3):
                    b = wait_filled(act, ("x", n, j))
                    for k in (2 * j, 2 * j + 1):
                        a = (k - 2 * j) * T
                        ins = nc.scalar.activation(xT[:, k, :], b[:, a:a + T], ACT.Copy, scale=norm_gain[:, n, k:k + 1])
                    emptied(ins, ("x", n, j))

            def copy_out(dst, name, src=None):
                b = wait_filled(act, name)
                emptied(nc.scalar.activation(dst, b if src is None else src(b), ACT.Copy), name)

            norm(0)
            for dst, src in small + small2:
                act.dma_start(dst, src).then_inc(small_loaded, 16)
            norm_evac(0)

            b = wait_filled(act, "gate0")
            act.wait_ge(bias_scaled, 1)
            for i in range(2):
                ins = nc.scalar.activation(rows0[0][:, i * T:(i + 1) * T], b[0:MH, i * T:(i + 1) * T], ACT.Tanh,
                                           bias=gate_bias[:, i:i + 1], scale=1.0 / GATE_CAP)
            emptied(ins, "gate0")
            wait_emptied(act, "cols")

            def conv_seed(i):
                b = wait_filled(act, ("z", 0, i))
                for k in (2 * i, 2 * i + 1):
                    a = (k - 2 * i) * T
                    tap = cols[:, (CONV - 1) * 8 + k:(CONV - 1) * 8 + k + 1]
                    ins = nc.scalar.activation(qkT[:, k, :], b[:, a:a + T], ACT.Copy, scale=tap)
                ins.then_inc(conv_seeded, 1)

            def conv_silu(i):
                wait_emptied(act, ("z", 0, i))
                nc.scalar.activation(qkT[:, 2 * i:2 * i + 2, :], qkT[:, 2 * i:2 * i + 2, :], ACT.Silu)\
                    .then_inc(qk_ready, 1)

            for i in range(4):
                conv_seed(i)
                if i >= 1:
                    conv_silu(i - 1)
            for k, (kind, i, _) in enumerate(Z0):
                name = ("z", 0, k)
                if kind == "rope":
                    copy_out(rope_raw[:, 2 * i:2 * i + 2, :].rearrange("p a b -> p (a b)"), name)
                    if i == 0:
                        conv_silu(3)
                elif kind == "om":
                    b = wait_filled(act, name)
                    o = og[:, :, 256 * i:256 * i + 256]
                    act_ins = nc.scalar.activation(o, b.rearrange("p (t n) -> p t n", t=TT), ACT.Sigmoid)
                    emptied(act_ins, name)
                    if i == 1:
                        step(nc.scalar.activation(rows0[1][:, 0:T], rows0[0][:, T:2 * T], ACT.Exp, scale=-GATE_CAP))
                        nc.scalar.activation(rows0[1][:, T:2 * T], rows0[1][:, 0:T], ACT.Ln, bias=1.0)\
                            .then_inc(logf_done, 1)
                elif kind == "vm":
                    if i == 0:
                        act.wait_ge(ones_set, 2)
                        act.wait_ge(nm_ready, 1)
                        nc.scalar.activation(row[4], row[3], ACT.Exp).then_inc(expnm_ready, 1)
                    copy_out(v_ext[:, :, 2 * i:2 * i + 2, 0:DH], name,
                             lambda b: b.rearrange("p (t a e) -> p t a e", t=TT, a=2))
                elif kind == "vb":
                    copy_out(v_b[:, :, 256 * i:256 * i + 256], name, lambda b: b.rearrange("p (t n) -> p t n", t=TT))

            def attn_exp(layer, u):
                k = useq(layer, u)
                act.wait_ge(abias_ready, k)
                p = probs[u % NPROB]
                for t, (a, b) in enumerate(((0, 128), (128, 384))):
                    ins = nc.scalar.activation(p[:, a:b], p[:, a:b], ACT.Exp, bias=abias[:, u % NPROB, t:t + 1],
                                               scale=SCALE, accum_out=asum[:, u % NPROB, t:t + 1])
                ins.then_inc(aexp_done, 1)

            def lstm_decay(hd):
                act.wait_ge(arg_ready, hd + 1)
                nc.scalar.activation(arg[hd % 2], arg[hd % 2], ACT.Exp).then_inc(decay_ready, 1)

            def lstm_num(hd):
                b = wait_filled(act, ("mN", hd))
                if hd:
                    act.wait_ge(lstm_sq, hd)
                for t in range(TT):
                    c = t * (DH + 1)
                    nc.scalar.activation(junk[t], b[:, c:c + DH], ACT.Square,
                                         accum_out=small0[:, 0, t * MH + hd:t * MH + hd + 1])
                nc.scalar.activation(num[:, :, hd, :], b[:, 0:TT * (DH + 1)].rearrange("p (t e) -> p t e", t=TT),
                                     ACT.Copy).then_inc(lstm_sq, 1)

            for hd in range(MH + 1):
                if hd < MH:
                    lstm_decay(hd)
                    attn_exp(0, hd)
                if hd >= 1:
                    copy_out(probsT[(hd - 1) % NPT], ("aT", 0, hd - 1), lambda b: b[:, 0:384])
                    lstm_num(hd - 1)
                    copy_out(yT[:, MH + hd - 1, :], ("aO", 0, hd - 1), lambda b: b[:, 0:T])
            copy_out(yT[:, 2:4, :].rearrange("p a b -> p (a b)"), ("yt", 1))

            def moe(layer):
                norm(1 + 2 * layer)
                norm_evac(1 + 2 * layer)
                for i in range(2):
                    act.wait_ge(r_exp_in, 2 * layer + i + 1)
                    a = rexp[i]
                    nc.scalar.activation(a, a, ACT.Exp).then_inc(r_exp_out, 1)
                b0 = EXPERTS * layer

                def body(it, j):
                    e, pair = it * UNROLL + j, it * (UNROLL // 2) + j // 2
                    act.wait_ge(hid_filled, b0 + e + 1)
                    act.wait_ge(hdn_ready, layer + 1 + b0 + e)
                    nc.scalar.activation(silu_t, bank_ap(1)[:, 0:2 * CAP], ACT.Silu).then_inc(silu_done, 1)
                    q = CAP * (j % 2)
                    act.wait_ge(y_filled, b0 + e + 1)
                    if j % 2 == 0:
                        act.wait_ge(scattered, 10 * layer + pair + 1)
                    nc.scalar.activation(y_sb[j // 2][q:q + CAP, 0:BANK], bank_ap(2)[q:q + CAP, :], ACT.Copy)\
                        .then_inc(yA_ready, 1)

                with act.Fori(0, EXPERTS // UNROLL) as it:
                    for j in range(UNROLL):
                        body(it, j)
                act.wait_ge(count_ready, layer + 1)
                nx = act.value_load(count_i[layer][0:1, 0:1], min_val=0, max_val=T // CAP - 1)
                with act.If(nx > 0):
                    with act.Fori(0, nx) as r:
                        with act.Fori(0, EXPERTS) as e:
                            act.wait_ge(more_pe[layer], (r * EXPERTS + e) * 4 + 3)
                            nc.scalar.activation(silu_t, bank_ap(1)[:, 0:2 * CAP], ACT.Silu)\
                                .then_inc(more_act[layer], 1)
                    act.wait_ge(more_done[layer], 1)
                act.wait_ge(scattered, 10 * (layer + 1))
                nc.scalar.activation(h[:, 0, :], bank_ap(4, 2), ACT.Copy).then_inc(h_copiedA, 1)

            moe(0)

            norm(2)
            norm_evac(2)
            for k, (kind, i, _) in enumerate(Z1):
                if kind == "rope":
                    dst = q_raw[:, 2 * i:2 * i + 2, :] if i < 4 else kk_raw[:, 2 * i - 8:2 * i - 6, :]
                    copy_out(dst.rearrange("p a b -> p (a b)"), ("z", 1, k))
                elif kind == "vsw":
                    copy_out(v_sw[:, i].rearrange("p t n -> p (t n)"), ("z", 1, k))
            b = wait_filled(act, "gate1")
            emptied(nc.scalar.activation(gates.rearrange("p t h c -> p (t h c)"), b[:, 0:TT * 3 * NH], ACT.Sigmoid),
                    "gate1")
            for kv in range(2):
                for ht in range(2):
                    b = wait_filled(act, ("cmp1", kv, ht))
                    nc.scalar.activation(gelu_t[kv][:, ht, :], b[:, 0:NG * NCMP], ACT.Gelu_apprx_tanh)\
                        .then_inc(gelu_done, 1)
            copy_out(kcmpT, "kcmp", lambda b: b[:, 0:NG * NCMP])
            copy_out(vcmp, "vcmp", lambda b: b[0:NCMP, 0:NG * DH])
            act.wait_ge(pc_exp_in, 1)
            nc.scalar.activation(pc, pc, ACT.Exp, scale=SCALE).then_inc(pc_exp_out, 1)
            for u in range(2):
                attn_exp(1, u)
            for i in range(4):
                copy_out(pcT[i], ("cT", i), lambda b: b[0:NCMP, :])
            for hd in range(NH):
                if hd + 1 < NH:
                    attn_exp(1, 2 * hd + 2)
                    attn_exp(1, 2 * hd + 3)
                for u in (2 * hd, 2 * hd + 1):
                    copy_out(probsT[u % NPT], ("aT", 1, u), lambda b: b[:, 0:384])
                copy_out(yT[:, hd, :], ("aO", 1, hd), lambda b: b[:, 0:T])
            moe(1)
            for tile in range(TT):
                wait_h(act, 4, tile)
                square(4, tile)

        @block.vector
        def _(vec):
            steps = [0]

            def step(ins):
                steps[0] += 1
                ins.then_inc(vec_step, 1)
                vec.wait_ge(vec_step, steps[0])

            V = nc.vector

            def norm(n):
                vec.wait_ge(rstd_ready, n + 1)
                V.tensor_scalar(hs[:, 1, :], h[:, 1, :], rstd[:, n, 1:2], None, ALU.mult).then_inc(hsV_ready, 1)
                for j in (0, 2):
                    b = wait_filled(vec, ("x", n, j))
                    if n == 0 and j == 0:
                        vec.wait_ge(params_loaded, 16 * N_PARAMS)
                    if n == 1 and j == 0:
                        vec.wait_ge(small_loaded, 16 * N_SMALL)
                    for k in (2 * j, 2 * j + 1):
                        a = (k - 2 * j) * T
                        ins = V.tensor_scalar(xT[:, k, :], b[:, a:a + T], norm_gain[:, n, k:k + 1], None, ALU.mult)
                    emptied(ins, ("x", n, j))

            def swap(layer, i):
                b = wait_filled(vec, ("swap", layer, i))
                s = C("sin").unsqueeze(1).to_broadcast([P, 2, T])
                sn = rope_sin[i % 2]
                emptied(V.tensor_tensor(sn.rearrange("p (a b) -> p a b", a=2), b.rearrange("p (a b) -> p a b", a=2), s,
                                        ALU.mult), ("swap", layer, i))
                wait_emptied(vec, ("swap", layer, i))
                vec.wait_ge(cos_done, 4 * layer + i + 1)
                if layer == 0:
                    dst = rope_out[:, 2 * i:2 * i + 2, :]
                else:
                    dst = q_rot[:, 2 * i:2 * i + 2, :] if i < 4 else kk_rot[:, 2 * i - 8:2 * i - 6, :]
                V.tensor_tensor(dst.rearrange("p a b -> p (a b)"), sn, rope_cos[i % 2], ALU.add).then_inc(rope_ready, 1)

            def scores(layer, u):
                k, r = useq(layer, u), u % NPROB
                b = wait_filled(vec, ("aS", layer, u))
                if u >= NPROB:
                    vec.wait_ge(*jobs.at[("aT", layer, u - NPROB)]["filled"])
                for t, (a, z) in enumerate(((0, 128), (128, 384))):
                    ins = V.tensor_tensor_reduce(out=probs[r][:, a:z], in0=b[:, a:z], in1=C("mask_ts")[:, a:z],
                                                 scale=1.0, scalar=-3e38, op0=ALU.add, op1=ALU.max,
                                                 accum_out=amax[:, r, t:t + 1])
                emptied(ins, ("aS", layer, u))
                wait_emptied(vec, ("aS", layer, u))
                V.tensor_scalar(abias[:, r, :], amax[:, r, :], -SCALE, None, ALU.mult).then_inc(abias_ready, 1)

            def sums(layer, u):
                k, r = useq(layer, u), u % NPROB
                vec.wait_ge(aexp_done, k)
                V.reciprocal(arec[:, r, :], asum[:, r, :]).then_inc(arec_ready, 1)

            norm(0)
            b = wait_filled(vec, "cols")
            emptied(V.tensor_copy(cols[:, :], b[:, 0:96]), "cols")
            wait_emptied(vec, "cols")

            for i in range(4):
                vec.wait_ge(conv_seeded, i + 1)
                b = bank(("z", 0, i))
                for j in range(CONV - 2, -1, -1):
                    s = CONV - 1 - j
                    for k in (2 * i, 2 * i + 1):
                        a = (k - 2 * i) * T
                        ins = V.scalar_tensor_tensor(out=qkT[:, k, s:T], in0=b[:, a:a + T - s],
                                                     scalar=cols[:, j * 8 + k:j * 8 + k + 1], in1=qkT[:, k, s:T],
                                                     op0=ALU.mult, op1=ALU.add)
                        if j:
                            ins.then_inc(vec_step, 1)
                            steps[0] += 1
                    if j:
                        vec.wait_ge(vec_step, steps[0])
                emptied(ins, ("z", 0, i))
            for i in range(4):
                swap(0, i)
            neg_f, a_row, m_row, nm_row, _, one_row = row
            vec.wait_ge(logf_done, 1)
            vec.wait_ge(ones_set, 2)
            step(V.tensor_tensor_scan(neg_f, one_row, rows0[1][:, T:2 * T], 0.0, ALU.mult, ALU.add))
            step(V.scalar_tensor_tensor(out=a_row, in0=rows0[0][:, 0:T], scalar=GATE_CAP, in1=neg_f,
                                        op0=ALU.mult, op1=ALU.add))
            V.tensor_tensor_scan(m_row, a_row, a_row, 0.0, ALU.max, ALU.max).then_inc(m_ready, 1)
            vec.wait_ge(m_ready, 1)
            V.tensor_tensor(nm_row, neg_f, m_row, ALU.subtract).then_inc(nm_ready, 1)
            b = wait_filled(vec, "acols")
            emptied(V.tensor_copy(acols.rearrange("p a b -> p (a b)"), b[:, 0:16]), "acols")
            wait_emptied(vec, "acols")

            def lstm_arg(hd):
                b = wait_filled(vec, ("mB", hd // 2))
                a = (hd % 2) * T
                V.scalar_tensor_tensor(out=arg[hd % 2][:, 0:T], in0=C("mask_sT"), scalar=acols[:, 0, hd:hd + 1],
                                       in1=b[:, a:a + T], op0=ALU.add, op1=ALU.subtract)
                V.scalar_tensor_tensor(out=arg[hd % 2][:, T:384], in0=C("mask_sT")[:, 0:P],
                                       scalar=acols[:, 1, hd:hd + 1], in1=b[:, a + P:a + T],
                                       op0=ALU.add, op1=ALU.subtract).then_inc(arg_ready, 1)

            def lstm_weights(hd):
                b = wait_filled(vec, ("mS", hd))
                vec.wait_ge(decay_ready, hd + 1)
                if hd >= 2:
                    vec.wait_ge(*jobs.at[("mN", hd - 2)]["filled"])
                emptied(V.scalar_tensor_tensor(out=lstm_pT[hd % 2], in0=b[:, 0:384], scalar=SCALE, in1=arg[hd % 2],
                                               op0=ALU.mult, op1=ALU.mult), ("mS", hd))

            for hd in range(MH):
                lstm_arg(hd)
                scores(0, hd)
                lstm_weights(hd)
                sums(0, hd)
            vec.wait_ge(lstm_sq, MH)
            den = num[:, :, :, DH]
            th = [small0[:, i, :].rearrange("p (t h) -> p t h", t=TT) for i in range(8)]
            step(V.scalar_tensor_tensor(out=th[1], in0=den, scalar=-1.0, in1=den, op0=ALU.mult, op1=ALU.max))
            step(V.tensor_tensor(th[1], th[1], acols[:, 2:4, :], ALU.max))
            step(V.reciprocal(small0[:, 2, :], small0[:, 1, :]))
            step(V.tensor_tensor(small0[:, 3, :], small0[:, 0, :], small0[:, 2, :], ALU.mult))
            V.tensor_tensor(small0[:, 3, :], small0[:, 3, :], small0[:, 2, :], ALU.mult).then_inc(denom_sq, 1)
            vec.wait_ge(lstm_rstd, 1)
            step(V.tensor_tensor(small0[:, 5, :], small0[:, 4, :], small0[:, 2, :], ALU.mult))
            vec.wait_ge(og_ready, 2)
            for hd in range(MH):
                for t in range(TT):
                    o = og[:, t, hd * DH:(hd + 1) * DH]
                    ins = V.scalar_tensor_tensor(out=o, in0=num[:, t, hd, 0:DH],
                                                 scalar=small0[:, 5, t * MH + hd:t * MH + hd + 1], in1=o,
                                                 op0=ALU.mult, op1=ALU.mult)
                if hd % 2:
                    ins.then_inc(lstm_y, 1)
            b = wait_filled(vec, ("yt", 0))
            emptied(V.tensor_copy(yT[:, 0:2, :].rearrange("p a b -> p (a b)"), b), ("yt", 0))

            def add_out(layer):
                for i in range(4):
                    b = wait_filled(vec, ("o", layer, i))
                    piece = h[:, i // 2, (i % 2) * BANK:(i % 2 + 1) * BANK]
                    V.tensor_tensor(piece, b, piece, ALU.add).then_inc(h_updated, 1)

            add_out(0)

            def moe(layer):
                b0, b8 = EXPERTS * layer, EXPERTS // 2 * layer
                norm(1 + 2 * layer)

                def wide(a, n):
                    return a.unsqueeze(2).to_broadcast([P, TT, n])

                gl, el = lg[:, :, 0:GROUPS], lg[:, :, GROUPS:LOGITS]
                desc = C("desc").unsqueeze(1).to_broadcast([P, TT, EXPERTS])
                b = wait_filled(vec, ("logits", layer))
                bias = router_b[layer][:, :].unsqueeze(1).to_broadcast([P, TT, LOGITS])
                emptied(V.tensor_tensor(lg, b[:, 0:TT * LOGITS].rearrange("p (t n) -> p t n", t=TT), bias, ALU.add),
                        ("logits", layer))
                wait_emptied(vec, ("logits", layer))
                gmax, gsum, gw, m1, m2, wm, dif, w1, w2, _ = t1

                def first_of_max(hot, vals, mx, n, tmp):
                    step(V.tensor_reduce(mx, vals, AX, ALU.max))
                    step(V.tensor_tensor(tmp, vals, wide(mx, n), ALU.is_equal))
                    step(V.tensor_tensor(tmp, tmp, desc[:, :, EXPERTS - n:EXPERTS], ALU.mult))
                    step(V.tensor_reduce(wm, tmp, AX, ALU.max))
                    step(V.tensor_tensor(hot, tmp, wide(wm, n), ALU.is_equal))

                first_of_max(g4[0], gl, gmax, GROUPS, g4[2])
                V.tensor_tensor(g4[1], gl, wide(gmax, GROUPS), ALU.subtract).then_inc(r_exp_in, 1)
                step(V.tensor_scalar(g4[2], g4[0], 1.0, -NEG, ALU.subtract, ALU.mult))
                pen = g4[2].unsqueeze(3).to_broadcast([P, TT, GROUPS, PER_GROUP])
                for t in range(TT):
                    ins = V.tensor_tensor(e16[0][:, t, :].rearrange("p (g x) -> p g x", g=GROUPS),
                                          el[:, t, :].rearrange("p (g x) -> p g x", g=GROUPS), pen[:, t], ALU.add)
                step(ins)
                first_of_max(e16[1], e16[0], m1, EXPERTS, e16[4])
                step(V.scalar_tensor_tensor(out=e16[0], in0=e16[1], scalar=2 * NEG, in1=e16[0],
                                            op0=ALU.mult, op1=ALU.add))
                first_of_max(e16[2], e16[0], m2, EXPERTS, e16[4])
                V.tensor_tensor(sel, e16[1], e16[2], ALU.add).then_inc(sel_ready, 1)
                V.tensor_tensor(dif, m2, m1, ALU.subtract).then_inc(r_exp_in, 1)
                vec.wait_ge(r_exp_out, 2 * layer + 1)
                step(V.tensor_reduce(gsum, g4[1], AX, ALU.add))
                step(V.reciprocal(gw, gsum))
                vec.wait_ge(r_exp_out, 2 * layer + 2)
                step(V.tensor_scalar(w1, dif, 1.0, None, ALU.add))
                step(V.reciprocal(w2, w1))
                step(V.tensor_tensor(w1, w2, gw, ALU.mult))
                step(V.tensor_tensor(w2, w1, dif, ALU.mult))
                step(V.tensor_tensor(e16[1], e16[1], wide(w1, EXPERTS), ALU.mult))
                step(V.tensor_tensor(e16[2], e16[2], wide(w2, EXPERTS), ALU.mult))
                step(V.tensor_tensor(comb, e16[1], e16[2], ALU.add))
                b = wait_filled(vec, ("pos", layer))
                step(V.scalar_tensor_tensor(out=posm, in0=b[:, 0:TT * EXPERTS].rearrange("p (t n) -> p t n", t=TT),
                                            scalar=1.0, in1=sel, op0=ALU.add, op1=ALU.mult))
                cf = count_f[layer]
                step(V.tensor_reduce(cf[0:1, 0:1], b[0:1, 2 * EXPERTS:3 * EXPERTS], AX, ALU.max))
                step(V.tensor_scalar(posm, posm, -1.0, None, ALU.add))
                emptied(V.tensor_scalar(cf[0:1, 1:2], cf[0:1, 0:1], float(CAP), None, ALU.is_gt), ("pos", layer))

                def build_pick(e, buf):
                    for t in range(TT):
                        ins = V.tensor_scalar(pick[buf][:, t, :], C("iota"), posm[:, t, ds(e, 1)], None, ALU.is_equal)
                    return ins

                def build_wpick(e, buf, at):
                    for t in range(TT):
                        ins = V.tensor_scalar(wpick[buf][:, t, at:at + CAP], C("iota"), posm[:, t, ds(e, 1)],
                                              comb[:, t, ds(e, 1)], ALU.is_equal, ALU.mult)
                    return ins

                def gathered(buf):
                    g = norm_gain[:, 1 + 2 * layer, :].unsqueeze(2).to_broadcast([P, KD, CAP])
                    return V.tensor_tensor(xg[buf], bank_ap(0).rearrange("p (k s) -> p k s", k=KD), g, ALU.mult)

                build_pick(0, 0).then_inc(picked, 1)
                V.memset(t1[9][:, 0:1], 0.0).then_inc(hdn_ready, 1)
                V.memset(t1[9][:, 1:2], 0.0).then_inc(scatT_ready, 1)
                wait_emptied(vec, ("pos", layer))
                step(V.scalar_tensor_tensor(out=cf[0:1, 2:3], in0=cf[0:1, 0:1], scalar=2.0 * CAP, in1=cf[0:1, 1:2],
                                            op0=ALU.is_gt, op1=ALU.add))
                V.scalar_tensor_tensor(out=count_i[layer][0:1, 0:1], in0=cf[0:1, 0:1], scalar=3.0 * CAP,
                                       in1=cf[0:1, 2:3], op0=ALU.is_gt, op1=ALU.add).then_inc(count_ready, 1)
                vec.wait_ge(xg_filled, b0 + 1)
                gathered(0).then_inc(xg_ready, 1)

                def body(it, j, last=False):
                    e, pair = it * UNROLL + j, it * (UNROLL // 2) + j // 2
                    build_wpick(e, j // 2, (j % 2) * CAP).then_inc(wpicked, 1)
                    if not last:
                        build_pick(e + 1, (j + 1) % 2).then_inc(picked, 1)
                    vec.wait_ge(silu_done, b0 + e + 1)
                    V.tensor_tensor(hdn[j % 2].rearrange("p c s -> p (c s)"), bank_ap(1)[:, 2 * CAP:4 * CAP], silu_t,
                                    ALU.mult).then_inc(hdn_ready, 1)
                    if j % 2:
                        vec.wait_ge(scattered, 10 * layer + pair + 1)
                        V.tensor_copy(scatT[j // 2], bank_ap(1)[:, T:2 * T]).then_inc(scatT_ready, 1)

                    def y_out():
                        q = CAP * (j % 2)
                        vec.wait_ge(y_filled, b0 + e + 1)
                        if j % 2 == 0:
                            vec.wait_ge(scattered, 10 * layer + pair + 1)
                        V.tensor_copy(y_sb[j // 2][q:q + CAP, BANK:D], bank_ap(3)[q:q + CAP, :]).then_inc(yV_ready, 1)

                    def x_next():
                        if not last:
                            vec.wait_ge(xg_filled, b0 + e + 2)
                            gathered((j + 1) % 2).then_inc(xg_ready, 1)

                    if j == UNROLL - 1:
                        y_out()
                        x_next()
                    else:
                        x_next()
                        y_out()

                with vec.Fori(0, EXPERTS // UNROLL - 1) as it:
                    for j in range(UNROLL):
                        body(it, j)
                for j in range(UNROLL):
                    body(EXPERTS // UNROLL - 1, j, last=j == UNROLL - 1)
                vec.wait_ge(count_ready, layer + 1)
                nx = vec.value_load(count_i[layer][0:1, 0:1], min_val=0, max_val=T // CAP - 1)
                with vec.If(nx > 0):
                    vec.wait_ge(scattered, 10 * (layer + 1))
                    with vec.Fori(0, nx) as r:
                        V.tensor_scalar(posm, posm, -float(CAP), None, ALU.add).then_inc(more_base[layer], 1)
                        with vec.Fori(0, EXPERTS) as e:
                            k4 = (r * EXPERTS + e) * 4
                            vec.wait_ge(more_pe[layer], k4 + 1)
                            vec.wait_ge(more_base[layer], r + 1)
                            build_pick(e, 0)
                            build_wpick(e, 0, 0).then_inc(more_vec[layer], 1)
                            vec.wait_ge(more_pe[layer], k4 + 2)
                            gathered(0).then_inc(more_vec[layer], 1)
                            vec.wait_ge(more_act[layer], r * EXPERTS + e + 1)
                            V.tensor_tensor(hdn[0].rearrange("p c s -> p (c s)"), bank_ap(1)[:, 2 * CAP:4 * CAP], silu_t,
                                            ALU.mult)
                            V.tensor_copy(scatT[0][0:CAP, :], bank_ap(1)[0:CAP, T:2 * T]).then_inc(more_vec[layer], 1)
                            vec.wait_ge(more_pe[layer], k4 + 4)
                            V.tensor_copy(y_sb[0][0:CAP, :], bank_ap(2, 2)[0:CAP, :]).then_inc(more_vec[layer], 1)
                    vec.wait_ge(more_done[layer], 1)
                vec.wait_ge(scattered, 10 * (layer + 1))
                V.tensor_copy(h[:, 1, :], bank_ap(6, 2)).then_inc(h_copiedV, 1)

            moe(0)

            norm(2)
            for kv in range(2):
                b = wait_filled(vec, ("z", 1, kv)).rearrange("p (g n b) -> p b g n", g=NG, b=CMP_STRIDE)
                for half in range(CMP_LEN // CMP_STRIDE):
                    c = MH * 8 + kv * CMP_LEN + half * CMP_STRIDE
                    for g in range(NG):
                        pos = cols[:, c:c + CMP_STRIDE].unsqueeze(2).to_broadcast([P, CMP_STRIDE, NCMP])
                        ins = V.tensor_tensor(blocks[kv][:, half * CMP_STRIDE:(half + 1) * CMP_STRIDE, g, :],
                                              b[:, :, g, half:half + NCMP], pos, ALU.add)
                emptied(ins, ("z", 1, kv))
            for i in range(6):
                swap(1, i)

            b = wait_filled(vec, "cS")
            add = C("cmp_add").rearrange("p (t n) -> p t n", t=TT)
            keep = C("cmp_keep").rearrange("p (t n) -> p t n", t=TT)
            bv = b[:, 0:TT * NH * NCMP].rearrange("p (t h n) -> p t h n", t=TT, h=NH)
            for t in range(TT):
                ins = V.tensor_tensor(pc[:, t], bv[:, t], add[:, t].unsqueeze(1).to_broadcast([P, NH, NCMP]), ALU.add)
            emptied(ins, "cS")
            wait_emptied(vec, "cS")
            pcr = pc.rearrange("p t h n -> p (t h) n")
            s0, s1, s2 = [a.rearrange("p t h -> p (t h)") for a in pcs]

            def per_head(a):
                return a.unsqueeze(2).to_broadcast([P, TT * NH, NCMP])

            step(V.tensor_reduce(s0, pcr, AX, ALU.max))
            V.tensor_tensor(pcr, pcr, per_head(s0), ALU.subtract).then_inc(pc_exp_in, 1)
            vec.wait_ge(pc_exp_out, 1)
            for t in range(TT):
                ins = V.tensor_tensor(pc[:, t], pc[:, t], keep[:, t].unsqueeze(1).to_broadcast([P, NH, NCMP]), ALU.mult)
            step(ins)
            step(V.tensor_reduce(s0, pcr, AX, ALU.add))
            step(V.tensor_scalar(s1, s0, 1e-30, None, ALU.max))
            step(V.reciprocal(s2, s1))
            wait_emptied(vec, "gate1")
            step(V.tensor_tensor(pcs[2], pcs[2], gates[:, :, :, 0], ALU.mult))
            V.tensor_tensor(pcr, pcr, per_head(s2), ALU.mult).then_inc(pc_ready, 1)
            for u in range(2):
                scores(1, u)
                sums(1, u)
            for hd in range(NH - 1):
                for u in (2 * hd + 2, 2 * hd + 3):
                    scores(1, u)
                    sums(1, u)
            add_out(1)
            moe(1)
            vec.wait_ge(rstd_ready, NX)
            for t in range(TT):
                if t == 0:
                    vec.wait_ge(h_copiedA, 2)
                V.scalar_tensor_tensor(out=h[:, t, :], in0=h[:, t, :], scalar=rstd[:, NX - 1, t:t + 1],
                                       in1=final_gain[:, :], op0=ALU.mult, op1=ALU.mult).then_inc(h_copiedV, 1)

        @block.tensor
        def _(pe):
            def slot(n, k):
                return ring[:, slot_of(n), :].rearrange("p (a b) -> p a b", a=k)

            def wait_slot(n, more=0):
                pe.wait_ge(slot_loaded[slot_of(n)], (more + (loads_before(n) + 1)) * 16)

            def norm(n):
                pe.wait_ge(hsA_ready, n + 1)
                pe.wait_ge(hsV_ready, n + 1)
                for j in range(4):
                    b = open_bank(pe, ("x", n, j))
                    for k in (2 * j, 2 * j + 1):
                        for t in range(TT):
                            a = (k - 2 * j) * T + t * P
                            ins = flip(b[:, a:a + P], hs[:, t, k:D:KD])
                    fill(ins, ("x", n, j))

            def wait_xT(n):
                for j in range(4):
                    wait_emptied(pe, ("x", n, j))

            def project(layer, i, natural):
                n = FIRST[f"z{layer}"] + i
                name = ("z", layer, i)
                wait_slot(n)
                w = slot(n, KD)
                b = open_bank(pe, name)
                for c in range(2):
                    for k in range(KD):
                        if natural:
                            ins = mm(b[:, c * 256:c * 256 + 256], xT[:, k, c * P:(c + 1) * P], w[:, k, :],
                                     k == 0, k == KD - 1)
                        else:
                            ins = mm(b[:, c * T:(c + 1) * T], w[:, k, c * P:(c + 1) * P], xT[:, k, :],
                                     k == 0, k == KD - 1)
                fill(ins, name)

            def swap(layer, i):
                Z = (Z0, Z1)[layer]
                z = [k for k, zz in enumerate(Z) if zz[0] == "rope"][i]
                wait_emptied(pe, ("z", layer, z))
                if layer == 0:
                    raw = rope_raw[:, 2 * i:2 * i + 2, :]
                else:
                    raw = q_raw[:, 2 * i:2 * i + 2, :] if i < 4 else kk_raw[:, 2 * i - 8:2 * i - 6, :]
                b = open_bank(pe, ("swap", layer, i))
                fill(mm(b, C("swap"), raw.rearrange("p a b -> p (a b)")), ("swap", layer, i))

            def attn_scores(layer, u):
                q, k, _, _ = unit(layer, u)
                b = open_bank(pe, ("aS", layer, u))
                mm(b[:, 0:P], q[:, 0:P], k[:, 0:P])
                fill(mm(b[:, P:384], q[:, P:T], k[:, 0:T]), ("aS", layer, u))

            def attn_flip(layer, u):
                pe.wait_ge(aprob_ready, useq(layer, u))
                b = open_bank(pe, ("aT", layer, u))
                for i in range(3):
                    ins = flip(b[:, i * P:(i + 1) * P], probs[u % NPROB][:, i * P:(i + 1) * P])
                fill(ins, ("aT", layer, u))

            def attn_values(b, layer, u, first, last):
                wait_emptied(pe, ("aT", layer, u))
                _, _, v, _ = unit(layer, u)
                mm(b[:, 0:T], v[0], probsT[u % NPT][:, 0:T], first, False)
                return mm(b[:, P:T], v[1], probsT[u % NPT][:, T:384], False, last)

            def out_proj(layer):
                for j in range(4):
                    n = FIRST[f"o{layer}"] + j
                    wait_slot(n)
                    w = slot(n, 2)
                    for i in range(4):
                        t, half = i // 2, i % 2
                        b = open_bank(pe, ("o", layer, i)) if j == 0 else bank(("o", layer, i))
                        for k in range(2):
                            ins = mm(b, yT[:, 2 * j + k, t * P:(t + 1) * P], w[:, k, half * BANK:(half + 1) * BANK],
                                     j == 0 and k == 0, j == 3 and k == 1)
                        if j == 3:
                            fill(ins, ("o", layer, i))
                    if j < 3:
                        ins.then_inc(wout_used, 1)

            pe.wait_ge(const_loaded, 16)
            pe.wait_ge(params_loaded, 16 * N_PARAMS)
            b = open_bank(pe, "cols")
            fill(flip(b[:, 0:96], cols_raw[:, :]), "cols")

            norm(0)
            wait_xT(0)
            b = open_bank(pe, "gate0")
            for i in range(2):
                for k in range(KD):
                    ins = mm(b[0:MH, i * T:(i + 1) * T], w_gate0[:, k, i * MH:(i + 1) * MH], xT[:, k, :],
                             k == 0, k == KD - 1)
            fill(ins, "gate0")
            for kind, i in Z0_ORDER:
                if kind == "z":
                    project(0, i, Z0[i][0] in ("om", "vm", "vb"))
                else:
                    swap(0, i)
            pe.wait_ge(m_ready, 1)
            pe.wait_ge(expnm_ready, 1)
            b = open_bank(pe, "acols")
            for i, r in enumerate((row[1], row[4])):
                for t in range(TT):
                    c = (2 * i + t) * MH
                    ins = flip(b[:, c:c + MH], r[:, t * P:(t + 1) * P])
            fill(ins, "acols")
            for i in range(4):
                pe.wait_ge(qk_ready, i + 1)

            def lstm_values(hd):
                wait_emptied(pe, ("mS", hd))
                b = open_bank(pe, ("mN", hd))
                w = lstm_pT[hd % 2]
                E1 = DH + 1
                mm(b[:, 0:E1], w[:, 0:P], v_ext[:, 0, hd, :])
                mm(b[:, E1:2 * E1], w[:, P:T], v_ext[:, 0, hd, :], True, False)
                fill(mm(b[:, E1:2 * E1], w[:, T:384], v_ext[:, 1, hd, :], False, True), ("mN", hd))

            def head_out(hd):
                lstm_values(hd)
                attn_flip(0, hd)
                b = open_bank(pe, ("aO", 0, hd))
                fill(attn_values(b, 0, hd, True, True), ("aO", 0, hd))

            pe.wait_ge(rope_ready, 4)
            for i, z in enumerate(Z0):
                if z[0] in ("vm", "vb"):
                    wait_emptied(pe, ("z", 0, i))
            for hd in range(MH):
                if hd % 2 == 0:
                    b = open_bank(pe, ("mB", hd // 2))
                    for i in range(2):
                        ins = mm(b[:, i * T:(i + 1) * T], C("head_row", MH)[:, (hd + i) * P:(hd + i + 1) * P], row[2])
                    fill(ins, ("mB", hd // 2))
                b = open_bank(pe, ("mS", hd))
                q, k = qkT[:, hd, :], qkT[:, MH + hd, :]
                mm(b[:, 0:T], k[:, 0:P], q)
                fill(mm(b[:, T:384], k[:, P:T], q[:, P:T]), ("mS", hd))
                attn_scores(0, hd)
                if hd >= 1:
                    head_out(hd - 1)
            head_out(MH - 1)
            for i in range(2):
                pe.wait_ge(lstm_y, i + 1)
                b = open_bank(pe, ("yt", i))
                for a in range(2):
                    for t in range(TT):
                        hd = 2 * i + a
                        ins = flip(b[:, a * T + t * P:a * T + (t + 1) * P], og[:, t, hd * DH:(hd + 1) * DH])
                fill(ins, ("yt", i))
            for hd in range(MH):
                wait_emptied(pe, ("aO", 0, hd))
            for i in range(2):
                wait_emptied(pe, ("yt", i))
            out_proj(0)

            def moe(layer):
                n0 = FIRST[f"moe{layer}"]
                b0 = EXPERTS * layer
                norm(1 + 2 * layer)
                pe.wait_ge(h_updated, 4 * (layer + 1))
                for i in range(4):
                    if BEFORE_ACC[layer][4 + i] is not None:
                        pe.wait_ge(*BEFORE_ACC[layer][4 + i])
                    ins = mm(bank_ap(4 + i), ident, h[:, i // 2, (i % 2) * BANK:(i % 2 + 1) * BANK])
                    if i in (0, 3):
                        ins.then_inc(scattered, 1)
                wait_xT(1 + 2 * layer)
                pe.wait_ge(router_packed, layer + 1)
                b = open_bank(pe, ("logits", layer))
                for t in range(TT):
                    for k in range(KD):
                        ins = mm(b[:, t * LOGITS:(t + 1) * LOGITS], xT[:, k, t * P:(t + 1) * P],
                                 router_w[layer][:, k, :], k == 0, k == KD - 1)
                fill(ins, ("logits", layer))
                pe.wait_ge(sel_ready, layer + 1)
                b = open_bank(pe, ("pos", layer))
                mm(b[:, 0:EXPERTS], C("before"), sel[:, 0, :])
                mm(b[:, EXPERTS:2 * EXPERTS], C("ones"), sel[:, 0, :], True, False)
                mm(b[:, EXPERTS:2 * EXPERTS], C("before"), sel[:, 1, :], False, True)
                mm(b[:, 2 * EXPERTS:3 * EXPERTS], C("ones"), sel[:, 0, :], True, False)
                fill(mm(b[:, 2 * EXPERTS:3 * EXPERTS], C("ones"), sel[:, 1, :], False, True), ("pos", layer))

                def gather(buf):
                    b = bank_ap(0)
                    for k in range(KD):
                        for t in range(TT):
                            ins = mm(b[:, k * CAP:(k + 1) * CAP], hs[:, t, k:D:KD], pick[buf][:, t, :],
                                     t == 0, t == TT - 1)
                    return ins

                def hidden(w, x, at):
                    b = bank_ap(1)
                    for c in range(2):
                        for k in range(KD):
                            ins = mm(b[:, at + c * CAP:at + (c + 1) * CAP], w[:, k, c * P:(c + 1) * P], x[:, k, :],
                                     k == 0, k == KD - 1)
                    return ins

                def down(w, hd, q):
                    for half in range(2):
                        for c in range(2):
                            ins = mm(bank_ap(2 + half)[q:q + CAP, :], hd[:, c, :], w[:, c, half * BANK:(half + 1) * BANK],
                                     c == 0, c == 1)
                    return ins

                def scatter(rows, buf, last=False):
                    for i in range(4):
                        ins = nc.tensor.matmul(bank_ap(4 + i), scatT[buf][0:rows, (i // 2) * P:(i // 2 + 1) * P],
                                               y_sb[buf][0:rows, (i % 2) * BANK:(i % 2 + 1) * BANK],
                                               start=False, stop=last, skip_group_check=True)
                    return ins

                for bb in (("x", 1 + 2 * layer, 0), ("pos", layer), ("logits", layer)):
                    wait_emptied(pe, bb)
                pe.wait_ge(picked, b0 + 1)
                gather(0).then_inc(xg_filled, 1)

                def body(it, j, last=False):
                    e, pair = it * UNROLL + j, it * (UNROLL // 2) + j // 2
                    n = n0 + 3 * j
                    more = 0 if isinstance(it, int) else it
                    if isinstance(it, int):
                        n += it * NSLOT
                    pe.wait_ge(xg_ready, b0 + e + 1)
                    pe.wait_ge(hdn_ready, layer + 1 + b0 + e)
                    if j % 2 == 0:
                        pe.wait_ge(scatT_ready, layer + 1 + EXPERTS // 2 * layer + pair)
                    wait_slot(n, more)
                    hidden(slot(n, KD), xg[j % 2], 0).then_inc(w1_used, 1)
                    wait_slot(n + 1, more)
                    ins = hidden(slot(n + 1, KD), xg[j % 2], 2 * CAP)
                    if j % 2:
                        pe.wait_ge(wpicked, b0 + e + 1)
                        for t in range(TT):
                            ins = flip(bank_ap(1)[:, T + t * P:T + (t + 1) * P], wpick[j // 2][:, t, :])
                    ins.then_inc(hid_filled, 1)

                    def next_gather():
                        if not last:
                            pe.wait_ge(picked, b0 + e + 2)
                            gather((j + 1) % 2).then_inc(xg_filled, 1)

                    def scatter_pair(p):
                        k = it * UNROLL + 2 * p + 2
                        pe.wait_ge(yA_ready, b0 + k)
                        pe.wait_ge(yV_ready, b0 + k)
                        pe.wait_ge(scatT_ready, layer + 1 + EXPERTS // 2 * layer + it * 2 + p + 1)
                        scatter(P, p, last and p == 1).then_inc(scattered, 1)

                    if j < UNROLL - 1:
                        next_gather()
                    else:
                        scatter_pair(0)
                    pe.wait_ge(hdn_ready, layer + 1 + b0 + e + 1)
                    wait_slot(n + 2, more)
                    down(slot(n + 2, 2), hdn[j % 2], CAP * (j % 2)).then_inc(y_filled, 1)
                    if j == UNROLL - 1:
                        next_gather()
                        scatter_pair(1)

                with pe.Fori(0, EXPERTS // UNROLL - 1) as it:
                    for j in range(UNROLL):
                        body(it, j)
                for j in range(UNROLL):
                    body(EXPERTS // UNROLL - 1, j, last=j == UNROLL - 1)
                pe.wait_ge(count_ready, layer + 1)
                nx = pe.value_load(count_i[layer][0:1, 0:1], min_val=0, max_val=T // CAP - 1)
                with pe.If(nx > 0):
                    mm(bank_ap(0)[:, 0:EXPERTS], C("ones"), sel[:, 0, :]).then_inc(more_pe[layer], 1)
                    with pe.Fori(0, nx) as r:
                        with pe.Fori(0, EXPERTS) as e:
                            k = r * EXPERTS + e
                            pe.wait_ge(more_vec[layer], k * 4 + 1)
                            gather(0).then_inc(more_pe[layer], 1)
                            pe.wait_ge(more_vec[layer], k * 4 + 2)
                            pe.wait_ge(more_loaded[layer], (k + 1) * 48)
                            hidden(slot(n0, KD), xg[0], 0)
                            hidden(slot(n0 + 1, KD), xg[0], 2 * CAP)
                            for t in range(TT):
                                ins = flip(bank_ap(1)[0:CAP, T + t * P:T + (t + 1) * P], wpick[0][:, t, 0:CAP])
                            ins.then_inc(more_pe[layer], 1)
                            pe.wait_ge(more_vec[layer], k * 4 + 3)
                            down(slot(n0 + 2, 2), hdn[0], 0).then_inc(more_pe[layer], 1)
                            pe.wait_ge(more_vec[layer], k * 4 + 4)
                            scatter(CAP, 0).then_inc(more_pe[layer], 1)
                    mm(bank_ap(0)[:, 0:EXPERTS], C("ones"), sel[:, 0, :]).then_inc(more_done[layer], 1)

            moe(0)

            norm(2)
            wait_xT(2)
            for kind, i in Z1_ORDER:
                if kind == "z":
                    project(1, i, Z1[i][0] == "vsw")
                else:
                    swap(1, i)
            b = open_bank(pe, "gate1")
            for t in range(TT):
                for k in range(KD):
                    ins = mm(b[:, t * 3 * NH:(t + 1) * 3 * NH], xT[:, k, t * P:(t + 1) * P], w_gate1[:, k, :],
                             k == 0, k == KD - 1)
            fill(ins, "gate1")
            for kv in range(2):
                wait_emptied(pe, ("z", 1, kv))
                for i in range(4):
                    n = FIRST["cmp"] + 4 * kv + i
                    wait_slot(n)
                    w = slot(n, 8)
                    for ht in range(2):
                        name = ("cmp1", kv, ht)
                        b = open_bank(pe, name) if i == 0 else bank(name)
                        for l in range(8):
                            ins = mm(b[:, 0:NG * NCMP], w[:, l, ht * P:(ht + 1) * P],
                                     blocks[kv][:, 8 * i + l].rearrange("p g n -> p (g n)"),
                                     i == 0 and l == 0, i == 3 and l == 7)
                            if i == 3 and l == 7:
                                if ht == 0:
                                    fill(ins, name)
                    if i < 3:
                        ins.then_inc(cmp_used, 1)
                    else:
                        fill(ins, name)
            pe.wait_ge(gelu_done, 2)
            b = open_bank(pe, "kcmp")
            for c in range(2):
                ins = mm(b[:, 0:NG * NCMP], w_cmp2[:, 0, c, :], gelu_t[0][:, c, :], c == 0, c == 1)
            fill(ins, "kcmp")
            pe.wait_ge(gelu_done, 4)
            b = open_bank(pe, "vcmp")
            for g in range(NG):
                for c in range(2):
                    ins = mm(b[0:NCMP, g * DH:(g + 1) * DH], gelu_t[1][:, c, g * NCMP:(g + 1) * NCMP],
                             w_cmp2[:, 1, c, :], c == 0, c == 1)
            fill(ins, "vcmp")
            wait_emptied(pe, "kcmp")
            b = open_bank(pe, "cS")
            for t in range(TT):
                for hd in range(NH):
                    c = (t * NH + hd) * NCMP
                    g = hd // REP
                    ins = mm(b[:, c:c + NCMP], q_raw[:, hd, t * P:(t + 1) * P], kcmpT[:, g * NCMP:(g + 1) * NCMP])
            fill(ins, "cS")
            pe.wait_ge(rope_ready, 10)
            attn_scores(1, 0)
            attn_scores(1, 1)
            pe.wait_ge(pc_ready, 1)
            for i in range(4):
                b = open_bank(pe, ("cT", i))
                for a in range(2):
                    for t in range(TT):
                        ins = flip(b[0:NCMP, a * T + t * P:a * T + (t + 1) * P], pc[:, t, 2 * i + a, :])
                fill(ins, ("cT", i))
            wait_emptied(pe, "vcmp")
            for i, z in enumerate(Z1):
                if z[0] == "vsw":
                    wait_emptied(pe, ("z", 1, i))
            for hd in range(NH):
                if hd + 1 < NH:
                    attn_scores(1, 2 * hd + 2)
                    attn_scores(1, 2 * hd + 3)
                attn_flip(1, 2 * hd)
                attn_flip(1, 2 * hd + 1)
                b = open_bank(pe, ("aO", 1, hd))
                wait_emptied(pe, ("cT", hd // 2))
                attn_values(b, 1, 2 * hd, True, False)
                attn_values(b, 1, 2 * hd + 1, False, False)
                g = hd // REP
                fill(mm(b[:, 0:T], vcmp[:, g * DH:(g + 1) * DH], pcT[hd // 2][:, (hd % 2) * T:(hd % 2 + 1) * T],
                        False, True), ("aO", 1, hd))
            for hd in range(NH):
                wait_emptied(pe, ("aO", 1, hd))
            out_proj(1)
            moe(1)


def _constants():
    import numpy as np
    r = np.arange(P)
    t = {}
    t["ident"] = np.eye(P)
    t["ones"] = np.ones((P, P))
    t["before"] = r[:, None] < r[None, :]
    t["swap"] = r[:, None] == (r[None, :] + DH // 2) % DH
    tri = np.where(r[:, None] > r[None, :], NEG, 0.0)
    zero = np.zeros((P, P))
    t["mask_sT"] = np.concatenate([tri, zero], 1)
    t["mask_ts"] = np.concatenate([tri.T, zero, tri.T], 1)
    half = DH // 2
    inv = np.float32(10000.0) ** (-(np.arange(half, dtype=np.float32) / np.float32(half)))
    ang = np.arange(T, dtype=np.float32)[None, :] * inv.astype(np.float32)[:, None]
    t["cos"] = np.concatenate([np.cos(ang), np.cos(ang)], 0)
    t["sin"] = np.concatenate([-np.sin(ang), np.sin(ang)], 0)
    t["iota"] = np.tile(np.arange(CAP), (P, 1))
    t["desc"] = np.tile(np.arange(EXPERTS, 0, -1), (P, 1))
    t["head_row"] = np.repeat(r[:, None] == np.arange(MH)[None, :], P, 1)
    end = np.arange(NCMP) * CMP_STRIDE + CMP_LEN - 1
    ok = end[None, :] <= np.arange(T)[:, None]
    ok = np.concatenate([ok[i * P:(i + 1) * P] for i in range(TT)], 1)
    t["cmp_add"] = np.where(ok, 0.0, NEG)
    t["cmp_keep"] = ok
    t["power"] = np.full((P, 8), -0.5)
    return np.concatenate([np.asarray(t[n], np.float32) for n in CONST_COLS], 1)


_INS = ["x", "mix_norm_0", "w_in_0", "mlstm_conv_0", "mlstm_gate_b_0", "mlstm_head_norm_0", "w_out_0", "ffn_norm_0",
        "router_group_0", "router_group_b_0", "router_expert_0", "router_expert_b_0", "moe_w1_0", "moe_w3_0",
        "moe_w2_0", "mix_norm_1", "w_in_1", "nsa_cmp_pos_1", "nsa_cmp_k1_1", "nsa_cmp_k2_1", "nsa_cmp_v1_1",
        "nsa_cmp_v2_1", "w_out_1", "ffn_norm_1", "router_group_1", "router_group_b_1", "router_expert_1",
        "router_expert_b_1", "moe_w1_1", "moe_w3_1", "moe_w2_1", "final_norm"]


def kernel(**inputs):
    import numpy as _np
    import concourse.bacc as _bacc
    from concourse import mybir as _mybir
    from concourse.bass_utils import run_bass_kernel_spmd as _run

    nc = _bacc.Bacc("TRN2", target_bir_lowering=False, num_devices=1)
    arrays, A = {}, {}
    for name in _INS + ["const"]:
        a = _constants() if name == "const" else _np.ascontiguousarray(inputs[name])
        arrays[f"in_{name}_dram"] = a
        A[name] = nc.dram_tensor(f"in_{name}_dram", a.shape, _mybir.dt.from_np(a.dtype), kind="ExternalInput").ap()
    out = nc.dram_tensor("out_0_dram", (1, T, D), _mybir.dt.float32, kind="ExternalOutput").ap()
    hybrid_kernel(nc, A, out)
    r = _run(nc, [arrays], core_ids=[0])
    return r.results[0]["out_0_dram"]
```

```python
import concourse.bass as bass
from concourse import mybir
from contextlib import ExitStack

P = 128
T = 256
TT = T // P
D = 1024
KD = D // P
DH = 128
SCALE = float(DH) ** -0.5
EPS = 1e-6
NEG = -1e30
MH = 4
GATE_CAP = 15.0
CONV = 4
NG, REP, NH = 2, 4, 8
CMP_LEN, CMP_STRIDE, CMP_HID = 32, 16, 256
NCMP = (T - CMP_LEN) // CMP_STRIDE + 1
QUARTER = P // 4
GROUPS, PER_GROUP = 4, 4
EXPERTS = GROUPS * PER_GROUP
HID = D // 4
CAP = 64
LOGITS = GROUPS + EXPERTS

NSLOT = 12
SLOT = 2048
PAIRS = EXPERTS // 2
PAIR_LOADS = 6
S2 = 2 * CAP
BANK = 512
ARENA = 16768
N_PARAMS, N_GATE0, N_SMALL = 3, 2, 16

CONST_COLS = {}
_at = 0
for _name, _n in (("ident", P), ("power", 8), ("ones", P), ("before", P), ("swap", P), ("mask_sT", T), ("mask_ts", 384),
                  ("cos", T), ("sin", T), ("iota", CAP), ("desc", EXPERTS), ("head_row", MH * P),
                  ("cmp_add", TT * NCMP), ("cmp_keep", TT * NCMP), ("fold", NG * NCMP)):
    CONST_COLS[_name] = (_at, _n)
    _at += _n
NCONST = _at
N_FIRST = CONST_COLS["ones"][0]


class Jobs:

    def __init__(self, filled, emptied):
        self.filled_sem, self.emptied_sem = filled, emptied
        self.n_filled, self.n_emptied = [0] * 8, [0] * 8
        self.last = [None] * 8
        self.at = {}
        self.next = 0

    def plan(self, name, emptied=None, bank=None):
        if bank is None:
            bank = self.next
        self.next = (bank + 1) % 8
        self.n_filled[bank] += 1
        if emptied is None:
            self.n_emptied[bank] += 1
            emptied = (self.emptied_sem[bank], self.n_emptied[bank])
        self.at[name] = dict(bank=bank, filled=(self.filled_sem[bank], self.n_filled[bank]), emptied=emptied,
                             before=self.last[bank])
        self.last[bank] = emptied


def hybrid_kernel(nc, A, out):
    f32 = mybir.dt.float32
    i32 = mybir.dt.int32
    ALU = mybir.AluOpType
    ACT = mybir.ActivationFunctionType
    AX = mybir.AxisListType.X
    ds = bass.ds

    ctx = ExitStack()
    with ctx:
        def sb(name, shape, dt=f32):
            return ctx.enter_context(nc.sbuf_tensor(name, shape, dt))

        def sem(name):
            return ctx.enter_context(nc.semaphore(name))

        ring = sb("ring", [P, NSLOT, SLOT])
        h = sb("h", [P, TT, D])
        hs = sb("hs", [P, TT, D])
        xT = sb("xT", [P, KD, T])
        const = sb("const", [P, NCONST])
        norm_gain = sb("norm_gain", [P, 4, KD])
        final_gain = sb("final_gain", [P, D])
        head_gain = sb("head_gain", [P, MH * DH])
        cols_raw = sb("cols_raw", [96, P])
        cols = sb("cols", [P, 96])
        w_gate0 = sb("w_gate0", [P, KD, 2 * MH])
        w_gate1 = sb("w_gate1", [P, KD, 3 * NH])
        gate_bias = sb("gate_bias", [MH, 2])
        router_g = [sb(f"router_g{i}", [P, KD, GROUPS]) for i in range(2)]
        router_e = [sb(f"router_e{i}", [P, KD, EXPERTS]) for i in range(2)]
        router_w = [sb(f"router_w{i}", [P, KD, LOGITS]) for i in range(2)]
        router_b = [sb(f"router_b{i}", [P, LOGITS]) for i in range(2)]
        w_cmp2 = sb("w_cmp2", [P, 2, 2, DH])
        ssq = sb("ssq", [P, 5, TT])
        rstd = sb("rstd", [P, 5, TT])
        arena = sb("arena", [P, ARENA])

        def C(name, rows=P):
            a, n = CONST_COLS[name]
            return const[0:rows, a:a + n]

        ident = C("ident")
        top = [0]

        def view(n, shape=None, parts=P, at=None):
            if at is None:
                at = top[0]
                top[0] += n
                assert top[0] <= ARENA, top[0]
            a = arena[0:parts, at:at + n]
            if shape is None:
                return a
            names = "abcd"[:len(shape)]
            return a.rearrange(f"p ({' '.join(names)}) -> p {' '.join(names)}", **dict(zip(names, shape)))

        yT = view(KD * T, (KD, T))
        NPROB, NPT = 4, 3
        probs = [view(384) for _ in range(NPROB)]
        probsT = [view(384) for _ in range(NPT)]
        amax = view(NPROB * 2, (NPROB, 2))
        abias = view(NPROB * 2, (NPROB, 2))
        asum = view(NPROB * 2, (NPROB, 2))
        arec = view(NPROB * 2, (NPROB, 2))
        mark = top[0]
        qkT = view(8 * T, (8, T))
        rope_raw = view(8 * T, (8, T))
        rope_out = view(8 * T, (8, T))
        rope_cos = [hs[:, 0, i * 2 * T:(i + 1) * 2 * T] for i in range(2)]
        rope_sin = [hs[:, 1, i * 2 * T:(i + 1) * 2 * T] for i in range(2)]
        v_ext = view(TT * MH * (DH + 1), (TT, MH, DH + 1))
        v_b = view(TT * MH * DH, (TT, MH * DH))
        og = view(TT * MH * DH, (TT, MH * DH))
        rows0 = [view(2 * T, parts=MH) for _ in range(2)]
        row = [view(T, parts=MH) for _ in range(6)]
        acols = view(16, (4, MH))
        arg = [xT[:, 2 * i:2 * i + 2, :].rearrange("p a b -> p (a b)")[:, 0:384] for i in range(2)]
        lstm_pT = [xT[:, 4 + 2 * i:6 + 2 * i, :].rearrange("p a b -> p (a b)")[:, 0:384] for i in range(2)]
        junk = [xT[:, 2 * i + 1, T - DH:T] for i in range(TT)]
        small0 = view(64, (8, 8))
        num = view(TT * MH * (DH + 1), (TT, MH, DH + 1), at=mark + 8 * T * 1)
        top[0] = mark
        lg = view(TT * LOGITS, (TT, LOGITS))
        g4 = [view(TT * GROUPS, (TT, GROUPS)) for _ in range(3)]
        e16 = [view(TT * EXPERTS, (TT, EXPERTS)) for _ in range(5)]
        t1 = [view(TT) for _ in range(10)]
        rexp = [g4[1], t1[6]]
        posm = view(TT * EXPERTS, (TT, EXPERTS))
        comb = view(TT * EXPERTS, (TT, EXPERTS))
        sel = view(TT * EXPERTS, (TT, EXPERTS))
        pick = [view(TT * S2, (TT, S2)) for _ in range(2)]
        wpick = [view(TT * S2, (TT, S2)) for _ in range(2)]
        xg = [view(KD * S2, (KD, S2)) for _ in range(2)]
        silu_t = view(HID)
        hdn = view(HID)
        turned = [view(HID + T) for _ in range(2)]
        y_sb = [view(D) for _ in range(2)]
        top[0] = mark
        q_raw = view(NH * T, (NH, T))
        kk_raw = view(4 * T, (4, T))
        q_rot = view(NH * T, (NH, T))
        kk_rot = view(4 * T, (4, T))
        v_sw = view(2 * TT * NG * DH, (2, TT, NG * DH))
        blocks = [view(CMP_LEN * QUARTER, (CMP_LEN, QUARTER)) for _ in range(2)]
        cmp_part = [q_rot[:, NH - 2 + kv, :] for kv in range(2)]
        probsT1 = probsT + [view(384)]
        gelu_t = [view(2 * NG * NCMP, (2, NG * NCMP)) for _ in range(2)]
        kcmpT = view(NG * NCMP)
        vcmp = view(NG * DH, parts=NCMP)
        gates = view(TT * 3 * NH, (TT, NH, 3))
        pc = view(TT * NH * NCMP, (TT, NH, NCMP))
        pcs = [view(TT * NH, (TT, NH)) for _ in range(3)]
        pcT = [blocks[i // 2].rearrange("p l q -> p (l q)")[0:NCMP, i % 2 * 2 * T:(i % 2 + 1) * 2 * T]
               for i in range(4)]
        count_f = [sb(f"count_f{i}", [1, 4]) for i in range(2)]
        count_i = [sb(f"count_i{i}", [1, 1], i32) for i in range(2)]

        psum = ctx.enter_context(nc.psum_tensor("psum", [P, 8 * BANK], f32))

        def bank_ap(b, n=1):
            return psum[:, b * BANK:(b + n) * BANK]

        bank_filled = [sem(f"bank_filled{b}") for b in range(8)]
        bank_emptied = [sem(f"bank_emptied{b}") for b in range(8)]
        slot_loaded = [sem(f"slot_loaded{s}") for s in range(NSLOT)]
        x_loaded = [sem(f"x_loaded{t}") for t in range(TT)]
        first_loaded, const_loaded, params_loaded = sem("first_loaded"), sem("const_loaded"), sem("params_loaded")
        gate0_loaded = sem("gate0_loaded")
        small_loaded = sem("small_loaded")
        vec_step, act_step, pool_step = sem("vec_step"), sem("act_step"), sem("pool_step")
        sq_done, rstd_ready = sem("sq_done"), sem("rstd_ready")
        hsA_ready, hsV_ready = sem("hsA_ready"), sem("hsV_ready")
        h_updated, h_copiedA, h_copiedV = sem("h_updated"), sem("h_copiedA"), sem("h_copiedV")
        wout_used, cmp_used = sem("wout_used"), sem("cmp_used")
        ones_set, bias_scaled = sem("ones_set"), sem("bias_scaled")
        conv_seeded, qk_ready = sem("conv_seeded"), sem("qk_ready")
        cos_done, rope_ready = sem("cos_done"), sem("rope_ready")
        og_ready = sem("og_ready")
        tanh_done, logf_done, nm_ready, expnm_ready, m_ready = (sem("tanh_done"), sem("logf_done"), sem("nm_ready"),
                                                                sem("expnm_ready"), sem("m_ready"))
        arg_ready, decay_ready = sem("arg_ready"), sem("decay_ready")
        lstm_sq, denom_sq, lstm_rstd, lstm_y = sem("lstm_sq"), sem("denom_sq"), sem("lstm_rstd"), sem("lstm_y")
        abias_ready, aexp_done, arec_ready, aprob_ready = (sem("abias_ready"), sem("aexp_done"), sem("arec_ready"),
                                                           sem("aprob_ready"))
        gates_ready, pads_zeroed, gelu_done, pc_exp_in, pc_exp_out, pc_ready = (
            sem("gates_ready"), sem("pads_zeroed"), sem("gelu_done"), sem("pc_exp_in"), sem("pc_exp_out"),
            sem("pc_ready"))
        r_exp_in, r_exp_out, sel_ready, count_ready = (sem("r_exp_in"), sem("r_exp_out"), sem("sel_ready"),
                                                       sem("count_ready"))
        picked, wpicked, xg_filled, xg_ready = sem("picked"), sem("wpicked"), sem("xg_filled"), sem("xg_ready")
        w1_used, hid_filled, silu_done, hdn_ready = sem("w1_used"), sem("hid_filled"), sem("silu_done"), sem("hdn_ready")
        turn_filled, turned_ready = sem("turn_filled"), sem("turned_ready")
        y_filled, yA_ready, yV_ready, scattered = sem("y_filled"), sem("yA_ready"), sem("yV_ready"), sem("scattered")
        more_loaded = [sem(f"more_loaded{i}") for i in range(2)]
        more_pe = [sem(f"more_pe{i}") for i in range(2)]
        more_vec = [sem(f"more_vec{i}") for i in range(2)]
        more_act = [sem(f"more_act{i}") for i in range(2)]
        more_done = [sem(f"more_done{i}") for i in range(2)]
        more_base = [sem(f"more_base{i}") for i in range(2)]
        router_packed, out_stored = sem("router_packed"), sem("out_stored")

        w_in_0 = A["w_in_0"].rearrange("(p k) n -> p k n", k=KD)
        w_in_1 = A["w_in_1"].rearrange("(p k) n -> p k n", k=KD)
        W0 = MH * DH
        Z0 = ([("qk", i, 256 * i) for i in range(4)]
              + [("rope", i, 4 * W0 + 2 * MH + 256 * i) for i in range(4)]
              + [("om", i, 3 * W0 + 256 * i) for i in range(2)]
              + [("vm", i, 2 * W0 + 256 * i) for i in range(2)]
              + [("vb", i, 6 * W0 + 2 * MH + 256 * i) for i in range(2)])
        QW, KW = NH * DH, NG * DH
        Z1 = ([("cmp", 0, QW), ("cmp", 1, QW + KW)]
              + [("rope", i, 256 * i) for i in range(4)]
              + [("rope", 4, QW + 2 * KW), ("rope", 5, QW + 4 * KW)]
              + [("vsw", 0, QW + 3 * KW), ("vsw", 1, QW + 5 * KW)])
        N_Z0, N_Z1, N_MOE = len(Z0), len(Z1), 3 * EXPERTS
        FIRST = {"z0": 0, "o0": N_Z0, "moe0": N_Z0 + 4}
        FIRST["z1"] = FIRST["moe0"] + N_MOE
        N_BEFORE_CMP = 3
        FIRST["cmp"] = FIRST["z1"] + N_BEFORE_CMP
        FIRST["z1b"] = FIRST["cmp"] + 8
        FIRST["o1"] = FIRST["z1"] + N_Z1 + 8
        FIRST["moe1"] = FIRST["o1"] + 4

        def z_load(layer, i):
            return FIRST[f"z{layer}"] + i + (8 if layer == 1 and i >= N_BEFORE_CMP else 0)

        def slot_of(n):
            return n % NSLOT

        def loads_before(n):
            return n // NSLOT

        jobs = Jobs(bank_filled, bank_emptied)

        def plan_norm(n):
            for j in range(4):
                jobs.plan(("x", n, j))

        def plan_out(layer):
            for i in range(4):
                jobs.plan(("o", layer, i), emptied=(h_updated, 4 * layer + i + 1))

        plan_norm(0)
        jobs.plan("cols")
        jobs.plan("gate0")
        Z0_ORDER = []
        for i, z in enumerate(Z0):
            Z0_ORDER.append(("z", i))
            if z[0] == "rope" and z[1] >= 1:
                Z0_ORDER.append(("swap", z[1] - 1))
            if z[0] == "om" and z[1] == 0:
                Z0_ORDER.append(("swap", 3))
        for kind, i in Z0_ORDER:
            jobs.plan((kind, 0, i))
        jobs.plan("acols")
        for hd in range(MH):
            if hd % 2 == 0:
                jobs.plan(("mB", hd // 2), emptied=(arg_ready, hd + 2))
            jobs.plan(("mS", hd))
            jobs.plan(("aS", 0, hd))
            if hd >= 1:
                jobs.plan(("mN", hd - 1), emptied=(lstm_sq, hd))
                jobs.plan(("aT", 0, hd - 1))
                jobs.plan(("aO", 0, hd - 1))
        jobs.plan(("mN", MH - 1), emptied=(lstm_sq, MH))
        jobs.plan(("aT", 0, MH - 1))
        jobs.plan(("aO", 0, MH - 1))
        for i in range(2):
            jobs.plan(("yt", i))
        plan_out(0)

        def plan_moe(layer):
            n = 1 + 2 * layer
            for j in range(4):
                jobs.plan(("x", n, j), bank=j)
            jobs.plan(("logits", layer), bank=2)
            jobs.plan(("pos", layer), bank=3)
            jobs.next = 0

        plan_moe(0)
        BEFORE_ACC = [list(jobs.last)]
        plan_norm(2)
        Z1_ORDER = [("z", 0), ("z", 1), ("z", 2), ("cmp1", 0), ("cmp1", 1), ("fold", 0), ("fold", 1),
                    ("z", 3), ("swap", 0), ("kcmp",), ("vcmp",), ("z", 4), ("swap", 1), ("z", 5), ("swap", 2),
                    ("z", 6), ("swap", 3), ("cS",), ("z", 7), ("swap", 4), ("gate1",), ("swap", 5), ("z", 8),
                    ("aS", 0), ("aS", 1), ("z", 9)]
        for kind, *i in Z1_ORDER:
            if kind in ("z", "swap", "aS"):
                jobs.plan((kind, 1, *i))
            elif kind == "fold":
                jobs.plan((kind, *i), emptied=(gelu_done, i[0] + 1))
            else:
                jobs.plan((kind, *i) if i else kind)
        for i in range(4):
            jobs.plan(("cT", i))
        for hd in range(NH + 1):
            if hd + 1 < NH:
                jobs.plan(("aS", 1, 2 * hd + 2))
                jobs.plan(("aS", 1, 2 * hd + 3))
            if hd < NH:
                jobs.plan(("aT", 1, 2 * hd))
                jobs.plan(("aT", 1, 2 * hd + 1))
            if hd >= 1:
                jobs.plan(("aO", 1, hd - 1))
        plan_out(1)
        plan_moe(1)
        BEFORE_ACC.append(list(jobs.last))

        def bank(name):
            return bank_ap(jobs.at[name]["bank"])

        def open_bank(pe, name):
            if jobs.at[name]["before"] is not None:
                pe.wait_ge(*jobs.at[name]["before"])
            return bank(name)

        def fill(ins, name):
            ins.then_inc(jobs.at[name]["filled"][0], 1)

        def wait_filled(eng, name):
            eng.wait_ge(*jobs.at[name]["filled"])
            return bank(name)

        def emptied(ins, name):
            ins.then_inc(jobs.at[name]["emptied"][0], 1)

        def wait_emptied(eng, name):
            eng.wait_ge(*jobs.at[name]["emptied"])

        def mm(o, lhsT, rhs, first=True, last=True):
            return nc.tensor.matmul(o, lhsT, rhs, start=first, stop=last)

        def flip(o, i):
            n = i.shape[0]
            return nc.tensor.transpose(o, i, ident[0:n, 0:n])

        MORE_STEPS = 5
        NX = 5

        def wait_h(eng, n, tile):
            if n == 0:
                eng.wait_ge(x_loaded[tile], 16)
            elif n in (1, 3):
                eng.wait_ge(h_updated, 4 * (n // 2) + 2 * tile + 2)
            elif tile == 0:
                eng.wait_ge(h_copiedA, n // 2)
            else:
                eng.wait_ge(h_copiedV, n // 2)

        def unit(layer, u):
            if layer == 0:
                return (rope_out[:, u, :], rope_out[:, MH + u, :],
                        [v_b[:, t, u * DH:(u + 1) * DH] for t in range(TT)], None)
            hd, br = u // 2, u % 2
            g = hd // REP
            return (q_rot[:, hd, :], kk_rot[:, 2 * br + g, :],
                    [v_sw[:, br, t, g * DH:(g + 1) * DH] for t in range(TT)],
                    [gates[:, t, hd, 1 + br:2 + br] for t in range(TT)])

        def useq(layer, u):
            return u + 1 + (MH if layer else 0)

        block = ctx.enter_context(nc.Block())

        @block.sync
        def _(sp):
            xv = A["x"][0].rearrange("(t p) d -> p t d", p=P)
            for t in range(TT):
                sp.dma_start(h[:, t, :], xv[:, t, :]).then_inc(x_loaded[t], 16)
            sp.dma_start(const[:, 0:N_FIRST], A["const"][:, 0:N_FIRST]).then_inc(first_loaded, 16)
            sp.dma_start(norm_gain[:, 0, :], A["mix_norm_0"].rearrange("(p k) -> p k", k=KD)).then_inc(params_loaded, 16)
            sp.dma_start(cols_raw[0:32, :], A["mlstm_conv_0"].rearrange("j (c p) -> (j c) p", p=P)).then_inc(params_loaded, 16)
            sp.dma_start(cols_raw[32:96, :], A["nsa_cmp_pos_1"].rearrange("a l d -> (a l) d")).then_inc(params_loaded, 16)

            def load(n, dst, src):
                sp.dma_start(dst, src).then_inc(slot_loaded[slot_of(n)], 16)

            def wait_used(n):
                m = n - NSLOT
                if m < 0:
                    return
                for name in ("moe1", "o1", "z1b", "cmp", "z1", "moe0", "o0", "z0"):
                    if m >= FIRST[name]:
                        i = m - FIRST[name] + (N_BEFORE_CMP if name == "z1b" else 0)
                        break
                layer = int(name[-1] != "0")
                if name[0] == "z":
                    sp.wait_ge(*jobs.at[("z", layer, i)]["filled"])
                elif name[0] == "o":
                    if i < 3:
                        sp.wait_ge(wout_used, 3 * layer + i + 1)
                    else:
                        sp.wait_ge(*jobs.at[("o", layer, 3)]["filled"])
                elif name == "cmp":
                    if i % 4 < 3:
                        sp.wait_ge(cmp_used, 3 * (i // 4) + i % 4 + 1)
                    else:
                        sp.wait_ge(*jobs.at[("cmp1", i // 4)]["filled"])
                else:
                    pair = i // PAIR_LOADS + PAIRS * layer
                    sp.wait_ge((w1_used, hid_filled, y_filled)[i % PAIR_LOADS // 2], pair + 1)

            def slot(n, shape):
                a = ring[:, slot_of(n), :]
                return a.rearrange("p (a b) -> p a b", a=shape)

            def load_z(layer, i):
                col, w = (Z0, Z1)[layer][i][2], (w_in_0, w_in_1)[layer]
                n = z_load(layer, i)
                wait_used(n)
                load(n, slot(n, KD), w[:, :, col:col + 256])

            def load_out(layer):
                w = A[f"w_out_{layer}"].rearrange("(j k p) n -> p j k n", p=P, k=2)
                for j in range(4):
                    n = FIRST[f"o{layer}"] + j
                    wait_used(n)
                    load(n, slot(n, 2), w[:, j])

            def pair_loads(layer, n, pair):
                for c in range(PAIR_LOADS):
                    name, k = (("moe_w1", KD), ("moe_w3", KD), ("moe_w2", 2))[c // 2]
                    w = A[f"{name}_{layer}"]
                    e = pair * 2 + c % 2
                    dst = ring[:, slot_of(n + c):slot_of(n + c) + 1, :]
                    if k == KD:
                        src = w.rearrange("e (p k) n -> p e (k n)", k=k)[:, ds(e, 1), :]
                    else:
                        src = w.rearrange("e (k p) n -> p e k n", k=k)[:, ds(e, 1), :, :]
                        dst = dst.rearrange("p e (k n) -> p e k n", k=k)
                    yield c, dst, src

            def load_moe(layer):
                n0 = FIRST[f"moe{layer}"]
                for pair in range(2):
                    for c, dst, src in pair_loads(layer, n0 + PAIR_LOADS * pair, pair):
                        wait_used(n0 + PAIR_LOADS * pair + c)
                        load(n0 + PAIR_LOADS * pair + c, dst, src)
                with sp.Fori(1, PAIRS // 2) as it:
                    for b in range(2):
                        pair = it * 2 + b
                        for c, dst, src in pair_loads(layer, n0 + PAIR_LOADS * b, pair):
                            sp.wait_ge((w1_used, hid_filled, y_filled)[c // 2], PAIRS * layer + pair - 2 + 1)
                            load(n0 + PAIR_LOADS * b + c, dst, src)
                sp.wait_ge(count_ready, layer + 1)
                nx = sp.value_load(count_i[layer][0:1, 0:1], min_val=0, max_val=T // CAP - 1)
                with sp.If(nx > 0):
                    sp.wait_ge(y_filled, PAIRS * (layer + 1))
                    with sp.Fori(0, nx) as r:
                        with sp.Fori(0, PAIRS) as pair:
                            sp.wait_ge(more_pe[layer], (r * PAIRS + pair) * MORE_STEPS + 1)
                            for c, dst, src in pair_loads(layer, n0, pair):
                                sp.dma_start(dst, src).then_inc(more_loaded[layer], 16)
                    sp.wait_ge(more_done[layer], 1)

            for i in range(N_Z0):
                load_z(0, i)
                if i == 0:
                    sp.dma_start(w_gate0[:, :, :], w_in_0[:, :, 4 * W0:4 * W0 + 2 * MH]).then_inc(gate0_loaded, 16)
                    sp.dma_start(gate_bias[:, :], A["mlstm_gate_b_0"].rearrange("(a h) -> h a", a=2),
                                 allow_slow_non_contiguous=True).then_inc(gate0_loaded, 16)
                if i == 1:
                    sp.dma_start(const[:, N_FIRST:NCONST], A["const"][:, N_FIRST:NCONST]).then_inc(const_loaded, 16)
            load_out(0)
            load_moe(0)
            for i in range(N_BEFORE_CMP):
                load_z(1, i)
            for kv, w in enumerate((A["nsa_cmp_k1_1"], A["nsa_cmp_v1_1"])):
                wl = w.rearrange("(l p) n -> p l n", p=P)
                for i in range(4):
                    n = FIRST["cmp"] + 4 * kv + i
                    wait_used(n)
                    load(n, slot(n, 8), wl[:, 8 * i:8 * i + 8, :])
            for i in range(N_BEFORE_CMP, N_Z1):
                load_z(1, i)
            load_out(1)
            load_moe(1)
            ov = out[0].rearrange("(t p) d -> p t d", p=P)
            for t in range(TT):
                sp.wait_ge(h_copiedV, 3 + t)
                sp.dma_start(ov[:, t, :], h[:, t, :]).then_inc(out_stored, 16)
            sp.wait_ge(out_stored, 16 * TT)

        @block.gpsimd
        def _(pool):
            steps = [0]

            def step(ins):
                steps[0] += 1
                ins.then_inc(pool_step, 1)
                pool.wait_ge(pool_step, steps[0])

            nc.gpsimd.memset(v_ext[:, :, :, DH:DH + 1], 1.0).then_inc(ones_set, 1)
            nc.gpsimd.memset(row[5], 1.0).then_inc(ones_set, 1)
            def norm(n):
                pool.wait_ge(sq_done, 2 * (n + 1))
                if n == 0:
                    pool.wait_ge(first_loaded, 16)
                step(nc.gpsimd.tensor_scalar(rstd[:, n, :], ssq[:, n, :], 1.0 / D, EPS, ALU.mult, ALU.add))
                nc.gpsimd.tensor_tensor(rstd[:, n, :], rstd[:, n, :], C("power")[:, 0:TT], ALU.pow)\
                    .then_inc(rstd_ready, 1)

            def rope(layer, i, raw, cosd):
                z = [k for k, zz in enumerate((Z0, Z1)[layer]) if zz[0] == "rope"][i]
                wait_emptied(pool, ("z", layer, z))
                done = 4 * layer + i
                if i >= 2:
                    pool.wait_ge(rope_ready, done - 1)
                c = C("cos").unsqueeze(1).to_broadcast([P, 2, T])
                nc.gpsimd.tensor_tensor(cosd[i % 2].rearrange("p (a b) -> p a b", a=2), raw, c, ALU.mult)\
                    .then_inc(cos_done, 1)

            norm(0)
            pool.wait_ge(gate0_loaded, 16 * N_GATE0)
            nc.gpsimd.tensor_scalar(gate_bias[:, :], gate_bias[:, :], 1.0 / GATE_CAP, 1.0, ALU.mult,
                                    ALU.mult).then_inc(bias_scaled, 1)
            pool.wait_ge(const_loaded, 16)
            for i in range(4):
                rope(0, i, rope_raw[:, 2 * i:2 * i + 2, :], rope_cos)
            pool.wait_ge(small_loaded, 16 * N_SMALL)
            for i in range(2):
                nc.gpsimd.tensor_copy(router_w[i][:, :, 0:GROUPS], router_g[i][:, :, :])
                nc.gpsimd.tensor_copy(router_w[i][:, :, GROUPS:LOGITS], router_e[i][:, :, :]).then_inc(router_packed, 1)
            for i in range(2):
                wait_emptied(pool, ("z", 0, [k for k, z in enumerate(Z0) if z[0] == "om"][i]))
                o = og[:, :, 256 * i:256 * i + 256]
                g = head_gain[:, 256 * i:256 * i + 256].unsqueeze(1).to_broadcast([P, TT, 256])
                nc.gpsimd.tensor_tensor(o, o, g, ALU.mult).then_inc(og_ready, 1)

            def normalise(layer, u):
                _, _, _, gate = unit(layer, u)
                k = useq(layer, u)
                pool.wait_ge(arec_ready, k)
                p = probs[u % NPROB]
                for t, (a, b) in enumerate(((0, 128), (128, 384))):
                    ins = nc.gpsimd.tensor_scalar(p[:, a:b], p[:, a:b], arec[:, u % NPROB, t:t + 1],
                                                  1.0 if gate is None else gate[t], ALU.mult, ALU.mult)
                ins.then_inc(aprob_ready, 1)

            for u in range(MH):
                normalise(0, u)
            pool.wait_ge(denom_sq, 1)
            step(nc.gpsimd.tensor_scalar(small0[:, 3, :], small0[:, 3, :], 1.0 / DH, EPS, ALU.mult, ALU.add))
            nc.gpsimd.tensor_tensor(small0[:, 4, :], small0[:, 3, :], C("power"), ALU.pow).then_inc(lstm_rstd, 1)
            norm(1)
            norm(2)
            for kv in range(2):
                nc.gpsimd.memset(blocks[kv][:, :, NG * NCMP:QUARTER], 0.0).then_inc(pads_zeroed, 1)
            for i in range(6):
                raw = q_raw[:, 2 * i:2 * i + 2, :] if i < 4 else kk_raw[:, 2 * i - 8:2 * i - 6, :]
                rope(1, i, raw, rope_cos)
            for u in range(2 * NH):
                normalise(1, u)
            norm(3)
            norm(4)

        @block.scalar
        def _(act):
            steps = [0]

            def step(ins):
                steps[0] += 1
                ins.then_inc(act_step, 1)
                act.wait_ge(act_step, steps[0])

            small = [(norm_gain[:, 1, :], A["ffn_norm_0"].rearrange("(p k) -> p k", k=KD)),
                     (norm_gain[:, 2, :], A["mix_norm_1"].rearrange("(p k) -> p k", k=KD)),
                     (norm_gain[:, 3, :], A["ffn_norm_1"].rearrange("(p k) -> p k", k=KD)),
                     (head_gain[:, :], A["mlstm_head_norm_0"].partition_broadcast(P)),
                     (w_gate1[:, :, :], w_in_1[:, :, QW + 6 * KW:QW + 6 * KW + 3 * NH]),
                     (final_gain[:, :], A["final_norm"].partition_broadcast(P))]
            for i in range(2):
                small += [(router_g[i][:, :, :], A[f"router_group_{i}"].rearrange("(p k) n -> p k n", k=KD)),
                          (router_e[i][:, :, :], A[f"router_expert_{i}"].rearrange("(p k) n -> p k n", k=KD)),
                          (router_b[i][:, 0:GROUPS], A[f"router_group_b_{i}"].partition_broadcast(P)),
                          (router_b[i][:, GROUPS:LOGITS], A[f"router_expert_b_{i}"].partition_broadcast(P))]
            assert len(small) == N_SMALL - 2
            small2 = [(w_cmp2[:, 0, :, :], A["nsa_cmp_k2_1"].rearrange("(k p) n -> p k n", p=P)),
                      (w_cmp2[:, 1, :, :], A["nsa_cmp_v2_1"].rearrange("(k p) n -> p k n", p=P))]

            def square(n, tile):
                nc.scalar.activation(hs[:, tile, :], h[:, tile, :], ACT.Square,
                                     accum_out=ssq[:, n, tile:tile + 1]).then_inc(sq_done, 1)

            def norm(n):
                for tile in range(TT):
                    wait_h(act, n, tile)
                    square(n, tile)
                act.wait_ge(rstd_ready, n + 1)
                nc.scalar.activation(hs[:, 0, :], h[:, 0, :], ACT.Copy, scale=rstd[:, n, 0:1]).then_inc(hsA_ready, 1)

            def norm_evac(n):
                if n == 0:
                    act.wait_ge(params_loaded, 16 * N_PARAMS)
                if n == 1:
                    act.wait_ge(small_loaded, 16 * N_SMALL)
                for j in (1, 3):
                    b = wait_filled(act, ("x", n, j))
                    for k in (2 * j, 2 * j + 1):
                        a = (k - 2 * j) * T
                        ins = nc.scalar.activation(xT[:, k, :], b[:, a:a + T], ACT.Copy, scale=norm_gain[:, n, k:k + 1])
                    emptied(ins, ("x", n, j))

            def copy_out(dst, name, src=None):
                b = wait_filled(act, name)
                emptied(nc.scalar.activation(dst, b if src is None else src(b), ACT.Copy), name)

            norm(0)
            for dst, src in small + small2:
                act.dma_start(dst, src).then_inc(small_loaded, 16)
            norm_evac(0)

            b = wait_filled(act, "gate0")
            act.wait_ge(bias_scaled, 1)
            for i in range(2):
                ins = nc.scalar.activation(rows0[0][:, i * T:(i + 1) * T], b[0:MH, i * T:(i + 1) * T], ACT.Tanh,
                                           bias=gate_bias[:, i:i + 1], scale=1.0 / GATE_CAP)
            emptied(ins, "gate0")
            wait_emptied(act, "cols")

            def conv_seed(i):
                b = wait_filled(act, ("z", 0, i))
                for k in (2 * i, 2 * i + 1):
                    a = (k - 2 * i) * T
                    tap = cols[:, (CONV - 1) * 8 + k:(CONV - 1) * 8 + k + 1]
                    ins = nc.scalar.activation(qkT[:, k, :], b[:, a:a + T], ACT.Copy, scale=tap)
                ins.then_inc(conv_seeded, 1)

            def conv_silu(i):
                wait_emptied(act, ("z", 0, i))
                nc.scalar.activation(qkT[:, 2 * i:2 * i + 2, :], qkT[:, 2 * i:2 * i + 2, :], ACT.Silu)\
                    .then_inc(qk_ready, 1)

            for i in range(4):
                conv_seed(i)
                if i >= 1:
                    conv_silu(i - 1)
            for k, (kind, i, _) in enumerate(Z0):
                name = ("z", 0, k)
                if kind == "rope":
                    copy_out(rope_raw[:, 2 * i:2 * i + 2, :].rearrange("p a b -> p (a b)"), name)
                    if i == 0:
                        conv_silu(3)
                elif kind == "om":
                    b = wait_filled(act, name)
                    o = og[:, :, 256 * i:256 * i + 256]
                    act_ins = nc.scalar.activation(o, b.rearrange("p (t n) -> p t n", t=TT), ACT.Sigmoid)
                    emptied(act_ins, name)
                    if i == 1:
                        step(nc.scalar.activation(rows0[1][:, 0:T], rows0[0][:, T:2 * T], ACT.Exp, scale=-GATE_CAP))
                        nc.scalar.activation(rows0[1][:, T:2 * T], rows0[1][:, 0:T], ACT.Ln, bias=1.0)\
                            .then_inc(logf_done, 1)
                elif kind == "vm":
                    if i == 0:
                        act.wait_ge(ones_set, 2)
                        act.wait_ge(nm_ready, 1)
                        nc.scalar.activation(row[4], row[3], ACT.Exp).then_inc(expnm_ready, 1)
                    copy_out(v_ext[:, :, 2 * i:2 * i + 2, 0:DH], name,
                             lambda b: b.rearrange("p (t a e) -> p t a e", t=TT, a=2))
                elif kind == "vb":
                    copy_out(v_b[:, :, 256 * i:256 * i + 256], name, lambda b: b.rearrange("p (t n) -> p t n", t=TT))

            def attn_exp(layer, u):
                k = useq(layer, u)
                act.wait_ge(abias_ready, k)
                p = probs[u % NPROB]
                for t, (a, b) in enumerate(((0, 128), (128, 384))):
                    ins = nc.scalar.activation(p[:, a:b], p[:, a:b], ACT.Exp, bias=abias[:, u % NPROB, t:t + 1],
                                               scale=SCALE, accum_out=asum[:, u % NPROB, t:t + 1])
                ins.then_inc(aexp_done, 1)

            def lstm_decay(hd):
                act.wait_ge(arg_ready, hd + 1)
                nc.scalar.activation(arg[hd % 2], arg[hd % 2], ACT.Exp).then_inc(decay_ready, 1)

            def lstm_num(hd):
                b = wait_filled(act, ("mN", hd))
                if hd:
                    act.wait_ge(lstm_sq, hd)
                for t in range(TT):
                    c = t * (DH + 1)
                    nc.scalar.activation(junk[t], b[:, c:c + DH], ACT.Square,
                                         accum_out=small0[:, 0, t * MH + hd:t * MH + hd + 1])
                nc.scalar.activation(num[:, :, hd, :], b[:, 0:TT * (DH + 1)].rearrange("p (t e) -> p t e", t=TT),
                                     ACT.Copy).then_inc(lstm_sq, 1)

            for hd in range(MH + 1):
                if hd < MH:
                    lstm_decay(hd)
                    attn_exp(0, hd)
                if hd >= 1:
                    copy_out(probsT[(hd - 1) % NPT], ("aT", 0, hd - 1), lambda b: b[:, 0:384])
                    lstm_num(hd - 1)
                    copy_out(yT[:, MH + hd - 1, :], ("aO", 0, hd - 1), lambda b: b[:, 0:T])
            copy_out(yT[:, 2:4, :].rearrange("p a b -> p (a b)"), ("yt", 1))

            def moe(layer):
                norm(1 + 2 * layer)
                norm_evac(1 + 2 * layer)
                for i in range(2):
                    act.wait_ge(r_exp_in, 2 * layer + i + 1)
                    a = rexp[i]
                    nc.scalar.activation(a, a, ACT.Exp).then_inc(r_exp_out, 1)
                b0 = PAIRS * layer

                def silu():
                    return nc.scalar.activation(silu_t, bank_ap(2)[:, 0:HID], ACT.Silu)

                def pair_steps(p, b):
                    act.wait_ge(hid_filled, b0 + p + 1)
                    silu().then_inc(silu_done, 1)
                    act.wait_ge(turn_filled, b0 + p + 1)
                    nc.scalar.activation(turned[b], bank_ap(3), ACT.Copy).then_inc(turned_ready, 1)
                    act.wait_ge(y_filled, b0 + p + 1)
                    nc.scalar.activation(y_sb[b][:, 0:BANK], bank_ap(0), ACT.Copy).then_inc(yA_ready, 1)

                pair_steps(0, 0)
                with act.Fori(0, PAIRS // 2 - 1) as it:
                    for b in (1, 0):
                        pair_steps(it * 2 + 2 - b, b)
                pair_steps(PAIRS - 1, 1)
                act.wait_ge(count_ready, layer + 1)
                nx = act.value_load(count_i[layer][0:1, 0:1], min_val=0, max_val=T // CAP - 1)
                with act.If(nx > 0):
                    with act.Fori(0, nx) as r:
                        with act.Fori(0, PAIRS) as pair:
                            act.wait_ge(more_pe[layer], (r * PAIRS + pair) * MORE_STEPS + 3)
                            silu().then_inc(more_act[layer], 1)
                    act.wait_ge(more_done[layer], 1)
                act.wait_ge(scattered, PAIRS * (layer + 1))
                nc.scalar.activation(h[:, 0, :], bank_ap(4, 2), ACT.Copy).then_inc(h_copiedA, 1)

            moe(0)

            norm(2)
            norm_evac(2)

            def copy_raw(i):
                dst = q_raw[:, 2 * i:2 * i + 2, :] if i < 4 else kk_raw[:, 2 * i - 8:2 * i - 6, :]
                copy_out(dst.rearrange("p a b -> p (a b)"), ("z", 1, 2 + i))

            def copy_v(i):
                copy_out(v_sw[:, i].rearrange("p t n -> p (t n)"), ("z", 1, 8 + i))

            copy_raw(0)
            for kv in range(2):
                copy_out(cmp_part[kv], ("cmp1", kv), lambda b: b[:, 0:CMP_HID])
            for kv in range(2):
                b = wait_filled(act, ("fold", kv))
                nc.scalar.activation(gelu_t[kv].rearrange("p a b -> p (a b)"), b[:, 0:2 * NG * NCMP],
                                     ACT.Gelu_apprx_tanh).then_inc(gelu_done, 1)
            copy_raw(1)
            copy_out(kcmpT, "kcmp", lambda b: b[:, 0:NG * NCMP])
            copy_out(vcmp, "vcmp", lambda b: b[0:NCMP, 0:NG * DH])
            for i in range(2, 5):
                copy_raw(i)
            act.wait_ge(pc_exp_in, 1)
            nc.scalar.activation(pc, pc, ACT.Exp, scale=SCALE).then_inc(pc_exp_out, 1)
            copy_raw(5)
            b = wait_filled(act, "gate1")
            emptied(nc.scalar.activation(gates.rearrange("p t h c -> p (t h c)"), b[:, 0:TT * 3 * NH], ACT.Sigmoid),
                    "gate1")
            copy_v(0)
            for u in range(2):
                attn_exp(1, u)
            copy_v(1)
            for i in range(4):
                copy_out(pcT[i], ("cT", i), lambda b: b[0:NCMP, :])
            for hd in range(NH + 1):
                if hd + 1 < NH:
                    attn_exp(1, 2 * hd + 2)
                    attn_exp(1, 2 * hd + 3)
                if hd < NH:
                    copy_out(probsT1[2 * hd % 4], ("aT", 1, 2 * hd), lambda b: b[:, 0:384])
                if hd >= 1:
                    copy_out(yT[:, hd - 1, :], ("aO", 1, hd - 1), lambda b: b[:, 0:T])
            moe(1)
            for tile in range(TT):
                wait_h(act, 4, tile)
                square(4, tile)

        @block.vector
        def _(vec):
            steps = [0]

            def step(ins):
                steps[0] += 1
                ins.then_inc(vec_step, 1)
                vec.wait_ge(vec_step, steps[0])

            V = nc.vector

            def norm(n):
                vec.wait_ge(rstd_ready, n + 1)
                V.tensor_scalar(hs[:, 1, :], h[:, 1, :], rstd[:, n, 1:2], None, ALU.mult).then_inc(hsV_ready, 1)
                for j in (0, 2):
                    b = wait_filled(vec, ("x", n, j))
                    if n == 0 and j == 0:
                        vec.wait_ge(params_loaded, 16 * N_PARAMS)
                    if n == 1 and j == 0:
                        vec.wait_ge(small_loaded, 16 * N_SMALL)
                    for k in (2 * j, 2 * j + 1):
                        a = (k - 2 * j) * T
                        ins = V.tensor_scalar(xT[:, k, :], b[:, a:a + T], norm_gain[:, n, k:k + 1], None, ALU.mult)
                    emptied(ins, ("x", n, j))

            def swap(layer, i):
                b = wait_filled(vec, ("swap", layer, i))
                s = C("sin").unsqueeze(1).to_broadcast([P, 2, T])
                sn = rope_sin[i % 2]
                emptied(V.tensor_tensor(sn.rearrange("p (a b) -> p a b", a=2), b.rearrange("p (a b) -> p a b", a=2), s,
                                        ALU.mult), ("swap", layer, i))
                wait_emptied(vec, ("swap", layer, i))
                vec.wait_ge(cos_done, 4 * layer + i + 1)
                if layer == 0:
                    dst = rope_out[:, 2 * i:2 * i + 2, :]
                else:
                    dst = q_rot[:, 2 * i:2 * i + 2, :] if i < 4 else kk_rot[:, 2 * i - 8:2 * i - 6, :]
                V.tensor_tensor(dst.rearrange("p a b -> p (a b)"), sn, rope_cos[i % 2], ALU.add).then_inc(rope_ready, 1)

            def scores(layer, u):
                k, r = useq(layer, u), u % NPROB
                b = wait_filled(vec, ("aS", layer, u))
                if u >= NPROB:
                    vec.wait_ge(*jobs.at[("aT", layer, u - NPROB)]["filled"])
                for t, (a, z) in enumerate(((0, 128), (128, 384))):
                    ins = V.tensor_tensor_reduce(out=probs[r][:, a:z], in0=b[:, a:z], in1=C("mask_ts")[:, a:z],
                                                 scale=1.0, scalar=-3e38, op0=ALU.add, op1=ALU.max,
                                                 accum_out=amax[:, r, t:t + 1])
                emptied(ins, ("aS", layer, u))
                wait_emptied(vec, ("aS", layer, u))
                V.tensor_scalar(abias[:, r, :], amax[:, r, :], -SCALE, None, ALU.mult).then_inc(abias_ready, 1)

            def sums(layer, u):
                k, r = useq(layer, u), u % NPROB
                vec.wait_ge(aexp_done, k)
                V.reciprocal(arec[:, r, :], asum[:, r, :]).then_inc(arec_ready, 1)

            norm(0)
            b = wait_filled(vec, "cols")
            emptied(V.tensor_copy(cols[:, :], b[:, 0:96]), "cols")
            wait_emptied(vec, "cols")

            for i in range(4):
                vec.wait_ge(conv_seeded, i + 1)
                b = bank(("z", 0, i))
                for j in range(CONV - 2, -1, -1):
                    s = CONV - 1 - j
                    for k in (2 * i, 2 * i + 1):
                        a = (k - 2 * i) * T
                        ins = V.scalar_tensor_tensor(out=qkT[:, k, s:T], in0=b[:, a:a + T - s],
                                                     scalar=cols[:, j * 8 + k:j * 8 + k + 1], in1=qkT[:, k, s:T],
                                                     op0=ALU.mult, op1=ALU.add)
                        if j:
                            ins.then_inc(vec_step, 1)
                            steps[0] += 1
                    if j:
                        vec.wait_ge(vec_step, steps[0])
                emptied(ins, ("z", 0, i))
            for i in range(4):
                swap(0, i)
            neg_f, a_row, m_row, nm_row, _, one_row = row
            vec.wait_ge(logf_done, 1)
            vec.wait_ge(ones_set, 2)
            step(V.tensor_tensor_scan(neg_f, one_row, rows0[1][:, T:2 * T], 0.0, ALU.mult, ALU.add))
            step(V.scalar_tensor_tensor(out=a_row, in0=rows0[0][:, 0:T], scalar=GATE_CAP, in1=neg_f,
                                        op0=ALU.mult, op1=ALU.add))
            V.tensor_tensor_scan(m_row, a_row, a_row, 0.0, ALU.max, ALU.max).then_inc(m_ready, 1)
            vec.wait_ge(m_ready, 1)
            V.tensor_tensor(nm_row, neg_f, m_row, ALU.subtract).then_inc(nm_ready, 1)
            b = wait_filled(vec, "acols")
            emptied(V.tensor_copy(acols.rearrange("p a b -> p (a b)"), b[:, 0:16]), "acols")
            wait_emptied(vec, "acols")

            def lstm_arg(hd):
                b = wait_filled(vec, ("mB", hd // 2))
                a = (hd % 2) * T
                V.scalar_tensor_tensor(out=arg[hd % 2][:, 0:T], in0=C("mask_sT"), scalar=acols[:, 0, hd:hd + 1],
                                       in1=b[:, a:a + T], op0=ALU.add, op1=ALU.subtract)
                V.scalar_tensor_tensor(out=arg[hd % 2][:, T:384], in0=C("mask_sT")[:, 0:P],
                                       scalar=acols[:, 1, hd:hd + 1], in1=b[:, a + P:a + T],
                                       op0=ALU.add, op1=ALU.subtract).then_inc(arg_ready, 1)

            def lstm_weights(hd):
                b = wait_filled(vec, ("mS", hd))
                vec.wait_ge(decay_ready, hd + 1)
                if hd >= 2:
                    vec.wait_ge(*jobs.at[("mN", hd - 2)]["filled"])
                emptied(V.scalar_tensor_tensor(out=lstm_pT[hd % 2], in0=b[:, 0:384], scalar=SCALE, in1=arg[hd % 2],
                                               op0=ALU.mult, op1=ALU.mult), ("mS", hd))

            for hd in range(MH):
                lstm_arg(hd)
                scores(0, hd)
                lstm_weights(hd)
                sums(0, hd)
            vec.wait_ge(lstm_sq, MH)
            den = num[:, :, :, DH]
            th = [small0[:, i, :].rearrange("p (t h) -> p t h", t=TT) for i in range(8)]
            step(V.scalar_tensor_tensor(out=th[1], in0=den, scalar=-1.0, in1=den, op0=ALU.mult, op1=ALU.max))
            step(V.tensor_tensor(th[1], th[1], acols[:, 2:4, :], ALU.max))
            step(V.reciprocal(small0[:, 2, :], small0[:, 1, :]))
            step(V.tensor_tensor(small0[:, 3, :], small0[:, 0, :], small0[:, 2, :], ALU.mult))
            V.tensor_tensor(small0[:, 3, :], small0[:, 3, :], small0[:, 2, :], ALU.mult).then_inc(denom_sq, 1)
            vec.wait_ge(lstm_rstd, 1)
            step(V.tensor_tensor(small0[:, 5, :], small0[:, 4, :], small0[:, 2, :], ALU.mult))
            vec.wait_ge(og_ready, 2)
            for hd in range(MH):
                for t in range(TT):
                    o = og[:, t, hd * DH:(hd + 1) * DH]
                    ins = V.scalar_tensor_tensor(out=o, in0=num[:, t, hd, 0:DH],
                                                 scalar=small0[:, 5, t * MH + hd:t * MH + hd + 1], in1=o,
                                                 op0=ALU.mult, op1=ALU.mult)
                if hd % 2:
                    ins.then_inc(lstm_y, 1)
            b = wait_filled(vec, ("yt", 0))
            emptied(V.tensor_copy(yT[:, 0:2, :].rearrange("p a b -> p (a b)"), b), ("yt", 0))

            def add_out(layer):
                for i in range(4):
                    b = wait_filled(vec, ("o", layer, i))
                    piece = h[:, i // 2, (i % 2) * BANK:(i % 2 + 1) * BANK]
                    V.tensor_tensor(piece, b, piece, ALU.add).then_inc(h_updated, 1)

            add_out(0)

            def moe(layer):
                b0 = PAIRS * layer
                norm(1 + 2 * layer)

                def wide(a, n):
                    return a.unsqueeze(2).to_broadcast([P, TT, n])

                gl, el = lg[:, :, 0:GROUPS], lg[:, :, GROUPS:LOGITS]
                desc = C("desc").unsqueeze(1).to_broadcast([P, TT, EXPERTS])
                b = wait_filled(vec, ("logits", layer))
                bias = router_b[layer][:, :].unsqueeze(1).to_broadcast([P, TT, LOGITS])
                emptied(V.tensor_tensor(lg, b[:, 0:TT * LOGITS].rearrange("p (t n) -> p t n", t=TT), bias, ALU.add),
                        ("logits", layer))
                wait_emptied(vec, ("logits", layer))
                gmax, gsum, gw, m1, m2, wm, dif, w1, w2, _ = t1

                def first_of_max(hot, vals, mx, n, tmp):
                    step(V.tensor_reduce(mx, vals, AX, ALU.max))
                    step(V.tensor_tensor(tmp, vals, wide(mx, n), ALU.is_equal))
                    step(V.tensor_tensor(tmp, tmp, desc[:, :, EXPERTS - n:EXPERTS], ALU.mult))
                    step(V.tensor_reduce(wm, tmp, AX, ALU.max))
                    step(V.tensor_tensor(hot, tmp, wide(wm, n), ALU.is_equal))

                first_of_max(g4[0], gl, gmax, GROUPS, g4[2])
                V.tensor_tensor(g4[1], gl, wide(gmax, GROUPS), ALU.subtract).then_inc(r_exp_in, 1)
                step(V.tensor_scalar(g4[2], g4[0], 1.0, -NEG, ALU.subtract, ALU.mult))
                pen = g4[2].unsqueeze(3).to_broadcast([P, TT, GROUPS, PER_GROUP])
                for t in range(TT):
                    ins = V.tensor_tensor(e16[0][:, t, :].rearrange("p (g x) -> p g x", g=GROUPS),
                                          el[:, t, :].rearrange("p (g x) -> p g x", g=GROUPS), pen[:, t], ALU.add)
                step(ins)
                first_of_max(e16[1], e16[0], m1, EXPERTS, e16[4])
                step(V.scalar_tensor_tensor(out=e16[0], in0=e16[1], scalar=2 * NEG, in1=e16[0],
                                            op0=ALU.mult, op1=ALU.add))
                first_of_max(e16[2], e16[0], m2, EXPERTS, e16[4])
                V.tensor_tensor(sel, e16[1], e16[2], ALU.add).then_inc(sel_ready, 1)
                V.tensor_tensor(dif, m2, m1, ALU.subtract).then_inc(r_exp_in, 1)
                vec.wait_ge(r_exp_out, 2 * layer + 1)
                step(V.tensor_reduce(gsum, g4[1], AX, ALU.add))
                step(V.reciprocal(gw, gsum))
                vec.wait_ge(r_exp_out, 2 * layer + 2)
                step(V.tensor_scalar(w1, dif, 1.0, None, ALU.add))
                step(V.reciprocal(w2, w1))
                step(V.tensor_tensor(w1, w2, gw, ALU.mult))
                step(V.tensor_tensor(w2, w1, dif, ALU.mult))
                step(V.tensor_tensor(e16[1], e16[1], wide(w1, EXPERTS), ALU.mult))
                step(V.tensor_tensor(e16[2], e16[2], wide(w2, EXPERTS), ALU.mult))
                step(V.tensor_tensor(comb, e16[1], e16[2], ALU.add))
                b = wait_filled(vec, ("pos", layer))
                step(V.scalar_tensor_tensor(out=posm, in0=b[:, 0:TT * EXPERTS].rearrange("p (t n) -> p t n", t=TT),
                                            scalar=1.0, in1=sel, op0=ALU.add, op1=ALU.mult))
                cf = count_f[layer]
                step(V.tensor_reduce(cf[0:1, 0:1], b[0:1, 2 * EXPERTS:3 * EXPERTS], AX, ALU.max))
                step(V.tensor_scalar(posm, posm, -1.0, None, ALU.add))
                emptied(V.tensor_scalar(cf[0:1, 1:2], cf[0:1, 0:1], float(CAP), None, ALU.is_gt), ("pos", layer))

                def build_pick(pair, b):
                    for t in range(TT):
                        for i in range(2):
                            ins = V.tensor_scalar(pick[b][:, t, i * CAP:(i + 1) * CAP], C("iota"),
                                                  posm[:, t, ds(pair * 2 + i, 1)], None, ALU.is_equal)
                    return ins

                def build_wpick(pair, b):
                    for t in range(TT):
                        for i in range(2):
                            e = pair * 2 + i
                            ins = V.tensor_scalar(wpick[b][:, t, i * CAP:(i + 1) * CAP], C("iota"),
                                                  posm[:, t, ds(e, 1)], comb[:, t, ds(e, 1)], ALU.is_equal, ALU.mult)
                    return ins

                def gathered(b):
                    g = norm_gain[:, 1 + 2 * layer, :].unsqueeze(2).to_broadcast([P, KD, S2])
                    return V.tensor_tensor(xg[b], bank_ap(0, 2).rearrange("p (k s) -> p k s", k=KD), g, ALU.mult)

                def gated():
                    return V.tensor_tensor(hdn, bank_ap(2)[:, HID:2 * HID], silu_t, ALU.mult)

                build_pick(0, 0).then_inc(picked, 1)
                wait_emptied(vec, ("pos", layer))
                step(V.scalar_tensor_tensor(out=cf[0:1, 2:3], in0=cf[0:1, 0:1], scalar=2.0 * CAP, in1=cf[0:1, 1:2],
                                            op0=ALU.is_gt, op1=ALU.add))
                V.scalar_tensor_tensor(out=count_i[layer][0:1, 0:1], in0=cf[0:1, 0:1], scalar=3.0 * CAP,
                                       in1=cf[0:1, 2:3], op0=ALU.is_gt, op1=ALU.add).then_inc(count_ready, 1)
                vec.wait_ge(xg_filled, b0 + 1)
                gathered(0).then_inc(xg_ready, 1)

                def pair_steps(p, b, last=False):
                    build_wpick(p, b).then_inc(wpicked, 1)
                    if not last:
                        build_pick(p + 1, 1 - b).then_inc(picked, 1)
                    vec.wait_ge(silu_done, b0 + p + 1)
                    gated().then_inc(hdn_ready, 1)
                    if not last:
                        vec.wait_ge(xg_filled, b0 + p + 2)
                        gathered(1 - b).then_inc(xg_ready, 1)
                    vec.wait_ge(y_filled, b0 + p + 1)
                    V.tensor_copy(y_sb[b][:, BANK:D], bank_ap(1)).then_inc(yV_ready, 1)

                pair_steps(0, 0)
                with vec.Fori(0, PAIRS // 2 - 1) as it:
                    for b in (1, 0):
                        pair_steps(it * 2 + 2 - b, b)
                pair_steps(PAIRS - 1, 1, last=True)
                vec.wait_ge(count_ready, layer + 1)
                nx = vec.value_load(count_i[layer][0:1, 0:1], min_val=0, max_val=T // CAP - 1)
                with vec.If(nx > 0):
                    vec.wait_ge(scattered, PAIRS * (layer + 1))
                    with vec.Fori(0, nx) as r:
                        V.tensor_scalar(posm, posm, -float(CAP), None, ALU.add).then_inc(more_base[layer], 1)
                        with vec.Fori(0, PAIRS) as pair:
                            k = (r * PAIRS + pair) * MORE_STEPS
                            vec.wait_ge(more_pe[layer], k + 1)
                            vec.wait_ge(more_base[layer], r + 1)
                            build_pick(pair, 0)
                            build_wpick(pair, 0).then_inc(more_vec[layer], 1)
                            vec.wait_ge(more_pe[layer], k + 2)
                            gathered(0).then_inc(more_vec[layer], 1)
                            vec.wait_ge(more_act[layer], r * PAIRS + pair + 1)
                            gated().then_inc(more_vec[layer], 1)
                            vec.wait_ge(more_pe[layer], k + 4)
                            V.tensor_copy(turned[0], bank_ap(3)).then_inc(more_vec[layer], 1)
                            vec.wait_ge(more_pe[layer], k + 5)
                            V.tensor_copy(y_sb[0], bank_ap(0, 2)).then_inc(more_vec[layer], 1)
                    vec.wait_ge(more_done[layer], 1)
                vec.wait_ge(scattered, PAIRS * (layer + 1))
                V.tensor_copy(h[:, 1, :], bank_ap(6, 2)).then_inc(h_copiedV, 1)

            moe(0)

            norm(2)
            for kv in range(2):
                b = wait_filled(vec, ("z", 1, kv)).rearrange("p (g n b) -> p b g n", g=NG, b=CMP_STRIDE)
                for half in range(CMP_LEN // CMP_STRIDE):
                    c = MH * 8 + kv * CMP_LEN + half * CMP_STRIDE
                    for g in range(NG):
                        pos = cols[:, c:c + CMP_STRIDE].unsqueeze(2).to_broadcast([P, CMP_STRIDE, NCMP])
                        ins = V.tensor_tensor(blocks[kv][:, half * CMP_STRIDE:(half + 1) * CMP_STRIDE,
                                                         g * NCMP:(g + 1) * NCMP],
                                              b[:, :, g, half:half + NCMP], pos, ALU.add)
                emptied(ins, ("z", 1, kv))
            for i in range(4):
                swap(1, i)

            b = wait_filled(vec, "cS")
            add = C("cmp_add").rearrange("p (t n) -> p t n", t=TT)
            keep = C("cmp_keep").rearrange("p (t n) -> p t n", t=TT)
            bv = b[:, 0:TT * NH * NCMP].rearrange("p (t h n) -> p t h n", t=TT, h=NH)
            for t in range(TT):
                ins = V.tensor_tensor(pc[:, t], bv[:, t], add[:, t].unsqueeze(1).to_broadcast([P, NH, NCMP]), ALU.add)
            emptied(ins, "cS")
            wait_emptied(vec, "cS")
            pcr = pc.rearrange("p t h n -> p (t h) n")
            s0, s1, s2 = [a.rearrange("p t h -> p (t h)") for a in pcs]

            def per_head(a):
                return a.unsqueeze(2).to_broadcast([P, TT * NH, NCMP])

            step(V.tensor_reduce(s0, pcr, AX, ALU.max))
            V.tensor_tensor(pcr, pcr, per_head(s0), ALU.subtract).then_inc(pc_exp_in, 1)
            swap(1, 4)
            vec.wait_ge(pc_exp_out, 1)
            for t in range(TT):
                ins = V.tensor_tensor(pc[:, t], pc[:, t], keep[:, t].unsqueeze(1).to_broadcast([P, NH, NCMP]), ALU.mult)
            step(ins)
            step(V.tensor_reduce(s0, pcr, AX, ALU.add))
            step(V.tensor_scalar(s1, s0, 1e-30, None, ALU.max))
            step(V.reciprocal(s2, s1))
            swap(1, 5)
            wait_emptied(vec, "gate1")
            step(V.tensor_tensor(pcs[2], pcs[2], gates[:, :, :, 0], ALU.mult))
            V.tensor_tensor(pcr, pcr, per_head(s2), ALU.mult).then_inc(pc_ready, 1)
            for u in range(2):
                scores(1, u)
            for u in range(2):
                sums(1, u)
            for hd in range(NH):
                if hd + 1 < NH:
                    scores(1, 2 * hd + 2)
                    scores(1, 2 * hd + 3)
                b = wait_filled(vec, ("aT", 1, 2 * hd + 1))
                emptied(V.tensor_copy(probsT1[(2 * hd + 1) % 4], b[:, 0:384]), ("aT", 1, 2 * hd + 1))
                if hd + 1 < NH:
                    sums(1, 2 * hd + 2)
                    sums(1, 2 * hd + 3)
            add_out(1)
            moe(1)
            vec.wait_ge(rstd_ready, NX)
            for t in range(TT):
                if t == 0:
                    vec.wait_ge(h_copiedA, 2)
                V.scalar_tensor_tensor(out=h[:, t, :], in0=h[:, t, :], scalar=rstd[:, NX - 1, t:t + 1],
                                       in1=final_gain[:, :], op0=ALU.mult, op1=ALU.mult).then_inc(h_copiedV, 1)

        @block.tensor
        def _(pe):
            def slot(n, k):
                return ring[:, slot_of(n), :].rearrange("p (a b) -> p a b", a=k)

            def wait_slot(n, more=0):
                pe.wait_ge(slot_loaded[slot_of(n)], (more + (loads_before(n) + 1)) * 16)

            def norm(n):
                pe.wait_ge(hsA_ready, n + 1)
                pe.wait_ge(hsV_ready, n + 1)
                for j in range(4):
                    b = open_bank(pe, ("x", n, j))
                    for k in (2 * j, 2 * j + 1):
                        for t in range(TT):
                            a = (k - 2 * j) * T + t * P
                            ins = flip(b[:, a:a + P], hs[:, t, k:D:KD])
                    fill(ins, ("x", n, j))

            def wait_xT(n):
                for j in range(4):
                    wait_emptied(pe, ("x", n, j))

            def project(layer, i, natural):
                n = z_load(layer, i)
                name = ("z", layer, i)
                wait_slot(n)
                w = slot(n, KD)
                b = open_bank(pe, name)
                for c in range(2):
                    for k in range(KD):
                        if natural:
                            ins = mm(b[:, c * 256:c * 256 + 256], xT[:, k, c * P:(c + 1) * P], w[:, k, :],
                                     k == 0, k == KD - 1)
                        else:
                            ins = mm(b[:, c * T:(c + 1) * T], w[:, k, c * P:(c + 1) * P], xT[:, k, :],
                                     k == 0, k == KD - 1)
                fill(ins, name)

            def swap(layer, i):
                Z = (Z0, Z1)[layer]
                z = [k for k, zz in enumerate(Z) if zz[0] == "rope"][i]
                wait_emptied(pe, ("z", layer, z))
                if layer == 0:
                    raw = rope_raw[:, 2 * i:2 * i + 2, :]
                else:
                    raw = q_raw[:, 2 * i:2 * i + 2, :] if i < 4 else kk_raw[:, 2 * i - 8:2 * i - 6, :]
                b = open_bank(pe, ("swap", layer, i))
                fill(mm(b, C("swap"), raw.rearrange("p a b -> p (a b)")), ("swap", layer, i))

            def attn_scores(layer, u):
                q, k, _, _ = unit(layer, u)
                b = open_bank(pe, ("aS", layer, u))
                mm(b[:, 0:P], q[:, 0:P], k[:, 0:P])
                fill(mm(b[:, P:384], q[:, P:T], k[:, 0:T]), ("aS", layer, u))

            def attn_flip(layer, u):
                pe.wait_ge(aprob_ready, useq(layer, u))
                b = open_bank(pe, ("aT", layer, u))
                for i in range(3):
                    ins = flip(b[:, i * P:(i + 1) * P], probs[u % NPROB][:, i * P:(i + 1) * P])
                fill(ins, ("aT", layer, u))

            def attn_values(b, layer, u, first, last):
                wait_emptied(pe, ("aT", layer, u))
                _, _, v, _ = unit(layer, u)
                pT = probsT1[u % 4] if layer else probsT[u % NPT]
                mm(b[:, 0:T], v[0], pT[:, 0:T], first, False)
                return mm(b[:, P:T], v[1], pT[:, T:384], False, last)

            def out_proj(layer):
                for j in range(4):
                    n = FIRST[f"o{layer}"] + j
                    wait_slot(n)
                    w = slot(n, 2)
                    for i in range(4):
                        t, half = i // 2, i % 2
                        b = open_bank(pe, ("o", layer, i)) if j == 0 else bank(("o", layer, i))
                        for k in range(2):
                            ins = mm(b, yT[:, 2 * j + k, t * P:(t + 1) * P], w[:, k, half * BANK:(half + 1) * BANK],
                                     j == 0 and k == 0, j == 3 and k == 1)
                        if j == 3:
                            fill(ins, ("o", layer, i))
                    if j < 3:
                        ins.then_inc(wout_used, 1)

            pe.wait_ge(first_loaded, 16)
            norm(0)
            pe.wait_ge(params_loaded, 16 * N_PARAMS)
            b = open_bank(pe, "cols")
            fill(flip(b[:, 0:96], cols_raw[:, :]), "cols")
            wait_xT(0)
            pe.wait_ge(gate0_loaded, 16 * N_GATE0)
            pe.wait_ge(const_loaded, 16)
            b = open_bank(pe, "gate0")
            for i in range(2):
                for k in range(KD):
                    ins = mm(b[0:MH, i * T:(i + 1) * T], w_gate0[:, k, i * MH:(i + 1) * MH], xT[:, k, :],
                             k == 0, k == KD - 1)
            fill(ins, "gate0")
            for kind, i in Z0_ORDER:
                if kind == "z":
                    project(0, i, Z0[i][0] in ("om", "vm", "vb"))
                else:
                    swap(0, i)
            pe.wait_ge(m_ready, 1)
            pe.wait_ge(expnm_ready, 1)
            b = open_bank(pe, "acols")
            for i, r in enumerate((row[1], row[4])):
                for t in range(TT):
                    c = (2 * i + t) * MH
                    ins = flip(b[:, c:c + MH], r[:, t * P:(t + 1) * P])
            fill(ins, "acols")
            for i in range(4):
                pe.wait_ge(qk_ready, i + 1)

            def lstm_values(hd):
                wait_emptied(pe, ("mS", hd))
                b = open_bank(pe, ("mN", hd))
                w = lstm_pT[hd % 2]
                E1 = DH + 1
                mm(b[:, 0:E1], w[:, 0:P], v_ext[:, 0, hd, :])
                mm(b[:, E1:2 * E1], w[:, P:T], v_ext[:, 0, hd, :], True, False)
                fill(mm(b[:, E1:2 * E1], w[:, T:384], v_ext[:, 1, hd, :], False, True), ("mN", hd))

            def head_out(hd):
                lstm_values(hd)
                attn_flip(0, hd)
                b = open_bank(pe, ("aO", 0, hd))
                fill(attn_values(b, 0, hd, True, True), ("aO", 0, hd))

            pe.wait_ge(rope_ready, 4)
            for i, z in enumerate(Z0):
                if z[0] in ("vm", "vb"):
                    wait_emptied(pe, ("z", 0, i))
            for hd in range(MH):
                if hd % 2 == 0:
                    b = open_bank(pe, ("mB", hd // 2))
                    for i in range(2):
                        ins = mm(b[:, i * T:(i + 1) * T], C("head_row", MH)[:, (hd + i) * P:(hd + i + 1) * P], row[2])
                    fill(ins, ("mB", hd // 2))
                b = open_bank(pe, ("mS", hd))
                q, k = qkT[:, hd, :], qkT[:, MH + hd, :]
                mm(b[:, 0:T], k[:, 0:P], q)
                fill(mm(b[:, T:384], k[:, P:T], q[:, P:T]), ("mS", hd))
                attn_scores(0, hd)
                if hd >= 1:
                    head_out(hd - 1)
            head_out(MH - 1)
            for i in range(2):
                pe.wait_ge(lstm_y, i + 1)
                b = open_bank(pe, ("yt", i))
                for a in range(2):
                    for t in range(TT):
                        hd = 2 * i + a
                        ins = flip(b[:, a * T + t * P:a * T + (t + 1) * P], og[:, t, hd * DH:(hd + 1) * DH])
                fill(ins, ("yt", i))
            for hd in range(MH):
                wait_emptied(pe, ("aO", 0, hd))
            for i in range(2):
                wait_emptied(pe, ("yt", i))
            out_proj(0)

            def moe(layer):
                n0 = FIRST[f"moe{layer}"]
                b0 = PAIRS * layer
                norm(1 + 2 * layer)

                def seed(i):
                    if BEFORE_ACC[layer][4 + i] is not None:
                        pe.wait_ge(*BEFORE_ACC[layer][4 + i])
                    mm(bank_ap(4 + i), ident, h[:, i // 2, (i % 2) * BANK:(i % 2 + 1) * BANK])

                pe.wait_ge(h_updated, 4 * (layer + 1))
                seed(0)
                wait_xT(1 + 2 * layer)
                pe.wait_ge(router_packed, layer + 1)
                b = open_bank(pe, ("logits", layer))
                for t in range(TT):
                    for k in range(KD):
                        ins = mm(b[:, t * LOGITS:(t + 1) * LOGITS], xT[:, k, t * P:(t + 1) * P],
                                 router_w[layer][:, k, :], k == 0, k == KD - 1)
                fill(ins, ("logits", layer))
                for i in range(1, 4):
                    seed(i)
                pe.wait_ge(sel_ready, layer + 1)
                b = open_bank(pe, ("pos", layer))
                mm(b[:, 0:EXPERTS], C("before"), sel[:, 0, :])
                mm(b[:, EXPERTS:2 * EXPERTS], C("ones"), sel[:, 0, :], True, False)
                mm(b[:, EXPERTS:2 * EXPERTS], C("before"), sel[:, 1, :], False, True)
                mm(b[:, 2 * EXPERTS:3 * EXPERTS], C("ones"), sel[:, 0, :], True, False)
                fill(mm(b[:, 2 * EXPERTS:3 * EXPERTS], C("ones"), sel[:, 1, :], False, True), ("pos", layer))

                def gather(b):
                    for k in range(KD):
                        for t in range(TT):
                            ins = mm(bank_ap(0, 2)[:, k * S2:(k + 1) * S2], hs[:, t, k:D:KD], pick[b][:, t, :],
                                     t == 0, t == TT - 1)
                    return ins

                def hidden(n, b, at):
                    for k in range(KD):
                        for i in range(2):
                            rows = slice(i * CAP, (i + 1) * CAP)
                            ins = mm(bank_ap(2)[rows, at:at + HID], xg[b][:, k, rows], slot(n + i, KD)[:, k, :],
                                     k == 0, k == KD - 1)
                    return ins

                def turn(b):
                    for c in range(2):
                        flip(bank_ap(3)[:, c * P:(c + 1) * P], hdn[:, c * P:(c + 1) * P])
                    for t in range(TT):
                        ins = flip(bank_ap(3)[:, HID + t * P:HID + (t + 1) * P], wpick[b][:, t, :])
                    return ins

                def down(n, b):
                    for half in range(2):
                        for c in range(2):
                            for i in range(2):
                                rows = slice(i * CAP, (i + 1) * CAP)
                                ins = mm(bank_ap(half)[rows, :], turned[b][:, c * P + i * CAP:c * P + (i + 1) * CAP],
                                         slot(n + i, 2)[:, c, half * BANK:(half + 1) * BANK], c == 0, c == 1)
                    return ins

                def scatter(b):
                    for i in range(4):
                        t = HID + (i // 2) * P
                        ins = nc.tensor.matmul(bank_ap(4 + i), turned[b][:, t:t + P],
                                               y_sb[b][:, (i % 2) * BANK:(i % 2 + 1) * BANK],
                                               start=False, stop=True, skip_group_check=True)
                    return ins

                for bb in (("x", 1 + 2 * layer, 0), ("x", 1 + 2 * layer, 1), ("pos", layer), ("logits", layer)):
                    wait_emptied(pe, bb)
                pe.wait_ge(picked, b0 + 1)
                gather(0).then_inc(xg_filled, 1)

                def scatter_last(p, b):
                    pe.wait_ge(yA_ready, b0 + p)
                    pe.wait_ge(yV_ready, b0 + p)
                    scatter(b).then_inc(scattered, 1)

                def steps(p, b, more, n, first=False, last=False):
                    pe.wait_ge(xg_ready, b0 + p + 1)
                    if not first:
                        pe.wait_ge(hdn_ready, b0 + p)
                    for i in range(2):
                        wait_slot(n + i, more)
                    hidden(n, b, 0).then_inc(w1_used, 1)
                    for i in range(2):
                        wait_slot(n + 2 + i, more)
                    hidden(n + 2, b, HID).then_inc(hid_filled, 1)
                    if not last:
                        pe.wait_ge(picked, b0 + p + 2)
                        if not first:
                            pe.wait_ge(yA_ready, b0 + p)
                            pe.wait_ge(yV_ready, b0 + p)
                        gather(1 - b).then_inc(xg_filled, 1)
                    pe.wait_ge(hdn_ready, b0 + p + 1)
                    pe.wait_ge(wpicked, b0 + p + 1)
                    if not first:
                        pe.wait_ge(turned_ready, b0 + p)
                    turn(b).then_inc(turn_filled, 1)
                    if not first:
                        scatter_last(p, 1 - b)
                    pe.wait_ge(turned_ready, b0 + p + 1)
                    if not last:
                        pe.wait_ge(xg_ready, b0 + p + 2)
                    for i in range(2):
                        wait_slot(n + 4 + i, more)
                    down(n + 4, b).then_inc(y_filled, 1)

                steps(0, 0, 0, n0, first=True)
                with pe.Fori(0, PAIRS // 2 - 1) as it:
                    steps(it * 2 + 1, 1, it, n0 + PAIR_LOADS)
                    steps(it * 2 + 2, 0, it, n0 + 2 * PAIR_LOADS)
                steps(PAIRS - 1, 1, 0, n0 + PAIR_LOADS * (PAIRS - 1), last=True)
                scatter_last(PAIRS, 1)
                pe.wait_ge(count_ready, layer + 1)
                nx = pe.value_load(count_i[layer][0:1, 0:1], min_val=0, max_val=T // CAP - 1)
                with pe.If(nx > 0):
                    mm(bank_ap(2)[:, 0:EXPERTS], C("ones"), sel[:, 0, :]).then_inc(more_pe[layer], 1)
                    with pe.Fori(0, nx) as r:
                        with pe.Fori(0, PAIRS) as pair:
                            k = (r * PAIRS + pair) * MORE_STEPS
                            pe.wait_ge(more_vec[layer], k + 1)
                            gather(0).then_inc(more_pe[layer], 1)
                            pe.wait_ge(more_vec[layer], k + 2)
                            pe.wait_ge(more_loaded[layer], (r * PAIRS + pair + 1) * (16 * PAIR_LOADS))
                            hidden(n0, 0, 0)
                            hidden(n0 + 2, 0, HID).then_inc(more_pe[layer], 1)
                            pe.wait_ge(more_vec[layer], k + 3)
                            turn(0).then_inc(more_pe[layer], 1)
                            pe.wait_ge(more_vec[layer], k + 4)
                            down(n0 + 4, 0).then_inc(more_pe[layer], 1)
                            pe.wait_ge(more_vec[layer], k + 5)
                            scatter(0).then_inc(more_pe[layer], 1)
                    mm(bank_ap(2)[:, 0:EXPERTS], C("ones"), sel[:, 0, :]).then_inc(more_done[layer], 1)

            moe(0)

            norm(2)
            wait_xT(2)

            def compress(kv):
                wait_emptied(pe, ("z", 1, kv))
                if kv == 0:
                    pe.wait_ge(pads_zeroed, 2)
                b = open_bank(pe, ("cmp1", kv))
                for i in range(4):
                    n = FIRST["cmp"] + 4 * kv + i
                    wait_slot(n)
                    w = slot(n, 8)
                    for l in range(8):
                        q = (l % 4) * QUARTER
                        ins = mm(b[q:q + QUARTER, 0:CMP_HID], blocks[kv][:, 8 * i + l, :], w[:, l, :],
                                 i == 0 and l < 4, i == 3 and l >= 4)
                    if i < 3:
                        ins.then_inc(cmp_used, 1)
                fill(ins, ("cmp1", kv))

            def fold(kv):
                wait_emptied(pe, ("cmp1", kv))
                b = open_bank(pe, ("fold", kv))
                for c in range(2):
                    ins = mm(b[:, c * NG * NCMP:(c + 1) * NG * NCMP], cmp_part[kv][:, c * P:(c + 1) * P], C("fold"))
                fill(ins, ("fold", kv))

            def compressed_keys():
                pe.wait_ge(gelu_done, 1)
                b = open_bank(pe, "kcmp")
                for c in range(2):
                    ins = mm(b[:, 0:NG * NCMP], w_cmp2[:, 0, c, :], gelu_t[0][:, c, :], c == 0, c == 1)
                fill(ins, "kcmp")

            def compressed_values():
                pe.wait_ge(gelu_done, 2)
                b = open_bank(pe, "vcmp")
                for g in range(NG):
                    for c in range(2):
                        ins = mm(b[0:NCMP, g * DH:(g + 1) * DH], gelu_t[1][:, c, g * NCMP:(g + 1) * NCMP],
                                 w_cmp2[:, 1, c, :], c == 0, c == 1)
                fill(ins, "vcmp")

            def compressed_scores():
                wait_emptied(pe, "kcmp")
                b = open_bank(pe, "cS")
                for t in range(TT):
                    for hd in range(NH):
                        c = (t * NH + hd) * NCMP
                        g = hd // REP
                        ins = mm(b[:, c:c + NCMP], q_raw[:, hd, t * P:(t + 1) * P], kcmpT[:, g * NCMP:(g + 1) * NCMP])
                fill(ins, "cS")

            def branch_gates():
                b = open_bank(pe, "gate1")
                for t in range(TT):
                    for k in range(KD):
                        ins = mm(b[:, t * 3 * NH:(t + 1) * 3 * NH], xT[:, k, t * P:(t + 1) * P], w_gate1[:, k, :],
                                 k == 0, k == KD - 1)
                fill(ins, "gate1")

            for kind, *i in Z1_ORDER:
                if kind == "z":
                    project(1, *i, Z1[i[0]][0] == "vsw")
                elif kind == "swap":
                    swap(1, *i)
                elif kind == "cmp1":
                    compress(*i)
                elif kind == "fold":
                    fold(*i)
                elif kind == "kcmp":
                    compressed_keys()
                elif kind == "vcmp":
                    compressed_values()
                elif kind == "cS":
                    compressed_scores()
                elif kind == "gate1":
                    branch_gates()
                elif i[0] == 0:
                    pe.wait_ge(rope_ready, 10)
                    attn_scores(1, 0)
                else:
                    attn_scores(1, 1)
            pe.wait_ge(pc_ready, 1)
            for i in range(4):
                b = open_bank(pe, ("cT", i))
                for a in range(2):
                    for t in range(TT):
                        ins = flip(b[0:NCMP, a * T + t * P:a * T + (t + 1) * P], pc[:, t, 2 * i + a, :])
                fill(ins, ("cT", i))
            wait_emptied(pe, "vcmp")
            for i, z in enumerate(Z1):
                if z[0] == "vsw":
                    wait_emptied(pe, ("z", 1, i))
            for hd in range(NH + 1):
                if hd + 1 < NH:
                    attn_scores(1, 2 * hd + 2)
                    attn_scores(1, 2 * hd + 3)
                if hd < NH:
                    attn_flip(1, 2 * hd)
                    attn_flip(1, 2 * hd + 1)
                if hd >= 1:
                    last = hd - 1
                    b = open_bank(pe, ("aO", 1, last))
                    wait_emptied(pe, ("cT", last // 2))
                    attn_values(b, 1, 2 * last, True, False)
                    attn_values(b, 1, 2 * last + 1, False, False)
                    g = last // REP
                    fill(mm(b[:, 0:T], vcmp[:, g * DH:(g + 1) * DH],
                            pcT[last // 2][:, (last % 2) * T:(last % 2 + 1) * T], False, True), ("aO", 1, last))
            for hd in range(NH):
                wait_emptied(pe, ("aO", 1, hd))
            out_proj(1)
            moe(1)


def _constants():
    import numpy as np
    r = np.arange(P)
    t = {}
    t["ident"] = np.eye(P)
    t["ones"] = np.ones((P, P))
    t["before"] = r[:, None] < r[None, :]
    t["swap"] = r[:, None] == (r[None, :] + DH // 2) % DH
    tri = np.where(r[:, None] > r[None, :], NEG, 0.0)
    zero = np.zeros((P, P))
    t["mask_sT"] = np.concatenate([tri, zero], 1)
    t["mask_ts"] = np.concatenate([tri.T, zero, tri.T], 1)
    half = DH // 2
    inv = np.float32(10000.0) ** (-(np.arange(half, dtype=np.float32) / np.float32(half)))
    ang = np.arange(T, dtype=np.float32)[None, :] * inv.astype(np.float32)[:, None]
    t["cos"] = np.concatenate([np.cos(ang), np.cos(ang)], 0)
    t["sin"] = np.concatenate([-np.sin(ang), np.sin(ang)], 0)
    t["iota"] = np.tile(np.arange(CAP), (P, 1))
    t["desc"] = np.tile(np.arange(EXPERTS, 0, -1), (P, 1))
    t["head_row"] = np.repeat(r[:, None] == np.arange(MH)[None, :], P, 1)
    end = np.arange(NCMP) * CMP_STRIDE + CMP_LEN - 1
    ok = end[None, :] <= np.arange(T)[:, None]
    ok = np.concatenate([ok[i * P:(i + 1) * P] for i in range(TT)], 1)
    t["cmp_add"] = np.where(ok, 0.0, NEG)
    t["cmp_keep"] = ok
    t["power"] = np.full((P, 8), -0.5)
    t["fold"] = r[:, None] % QUARTER == np.arange(NG * NCMP)[None, :]
    return np.concatenate([np.asarray(t[n], np.float32) for n in CONST_COLS], 1)


_INS = ["x", "mix_norm_0", "w_in_0", "mlstm_conv_0", "mlstm_gate_b_0", "mlstm_head_norm_0", "w_out_0", "ffn_norm_0",
        "router_group_0", "router_group_b_0", "router_expert_0", "router_expert_b_0", "moe_w1_0", "moe_w3_0",
        "moe_w2_0", "mix_norm_1", "w_in_1", "nsa_cmp_pos_1", "nsa_cmp_k1_1", "nsa_cmp_k2_1", "nsa_cmp_v1_1",
        "nsa_cmp_v2_1", "w_out_1", "ffn_norm_1", "router_group_1", "router_group_b_1", "router_expert_1",
        "router_expert_b_1", "moe_w1_1", "moe_w3_1", "moe_w2_1", "final_norm"]


def kernel(**inputs):
    import numpy as _np
    import concourse.bacc as _bacc
    from concourse import mybir as _mybir
    from concourse.bass_utils import run_bass_kernel_spmd as _run

    nc = _bacc.Bacc("TRN2", target_bir_lowering=False, num_devices=1)
    arrays, A = {}, {}
    for name in _INS + ["const"]:
        a = _constants() if name == "const" else _np.ascontiguousarray(inputs[name])
        arrays[f"in_{name}_dram"] = a
        A[name] = nc.dram_tensor(f"in_{name}_dram", a.shape, _mybir.dt.from_np(a.dtype), kind="ExternalInput").ap()
    out = nc.dram_tensor("out_0_dram", (1, T, D), _mybir.dt.float32, kind="ExternalOutput").ap()
    hybrid_kernel(nc, A, out)
    r = _run(nc, [arrays], core_ids=[0])
    return r.results[0]["out_0_dram"]
```

```python
import concourse.bass as bass
from concourse import mybir
from contextlib import ExitStack

P = 128
T = 256
TT = T // P
D = 1024
KD = D // P
DH = 128
SCALE = float(DH) ** -0.5
EPS = 1e-6
NEG = -1e30
MH = 4
GATE_CAP = 15.0
CONV = 4
NG, REP, NH = 2, 4, 8
CMP_LEN, CMP_STRIDE, CMP_HID = 32, 16, 256
NCMP = (T - CMP_LEN) // CMP_STRIDE + 1
QUARTER = P // 4
GROUPS, PER_GROUP = 4, 4
EXPERTS = GROUPS * PER_GROUP
HID = D // 4
CAP = 64
LOGITS = GROUPS + EXPERTS

NSLOT = 12
SLOT = 2048
PAIRS = EXPERTS // 2
PAIR_LOADS = 6
S2 = 2 * CAP
BANK = 512
ARENA = 16640
N_PARAMS, N_GATE0, N_SMALL = 3, 2, 16

CONST_COLS = {}
_at = 0
for _name, _n in (("ident", P), ("power", 8), ("fold", NG * NCMP), ("before", P), ("ones", P),
                  ("mask_sT", T), ("mask_ts", 384),
                  ("cos", T), ("sin", T), ("iota", CAP), ("desc", EXPERTS), ("head_row", MH * P),
                  ("cmp_add", TT * NCMP), ("cmp_keep", TT * NCMP)):
    CONST_COLS[_name] = (_at, _n)
    _at += _n
NCONST = _at
N_FIRST = CONST_COLS["before"][0]


class Jobs:

    def __init__(self, filled, emptied):
        self.filled_sem, self.emptied_sem = filled, emptied
        self.n_filled, self.n_emptied = [0] * 8, [0] * 8
        self.last = [None] * 8
        self.at = {}
        self.next = 0

    def plan(self, name, emptied=None, bank=None):
        if bank is None:
            bank = self.next
        self.next = (bank + 1) % 8
        self.n_filled[bank] += 1
        if emptied is None:
            self.n_emptied[bank] += 1
            emptied = (self.emptied_sem[bank], self.n_emptied[bank])
        self.at[name] = dict(bank=bank, filled=(self.filled_sem[bank], self.n_filled[bank]), emptied=emptied,
                             before=self.last[bank])
        self.last[bank] = emptied


def hybrid_kernel(nc, A, out):
    f32 = mybir.dt.float32
    i32 = mybir.dt.int32
    bf16 = mybir.dt.bfloat16
    ALU = mybir.AluOpType
    ACT = mybir.ActivationFunctionType
    AX = mybir.AxisListType.X
    ds = bass.ds

    ctx = ExitStack()
    with ctx:
        def sb(name, shape, dt=f32):
            return ctx.enter_context(nc.sbuf_tensor(name, shape, dt))

        def sem(name):
            return ctx.enter_context(nc.semaphore(name))

        ring = sb("ring", [P, NSLOT, SLOT])
        h = sb("h", [P, TT, D])
        hs = sb("hs", [P, TT, D])
        xT = sb("xT", [P, KD, T])
        const = sb("const", [P, NCONST])
        norm_gain = sb("norm_gain", [P, 4, KD])
        final_gain = sb("final_gain", [P, D])
        head_gain = sb("head_gain", [P, MH * DH])
        cols_raw = sb("cols_raw", [96, P])
        cols = sb("cols", [P, 96])
        w_gate = [sb(f"w_gate{i}", [P, KD, QUARTER]) for i in range(2)]
        gate_bias = sb("gate_bias", [MH, 2])
        router_w = [sb(f"router_w{i}", [P, KD, QUARTER]) for i in range(2)]
        router_b = [sb(f"router_b{i}", [P, LOGITS]) for i in range(2)]
        w_cmp2 = sb("w_cmp2", [P, 2, 2, DH])
        counters = sb("counters", [P, 2, P], bf16)
        ssq = sb("ssq", [P, 5, TT])
        rstd = sb("rstd", [P, 5, TT])
        arena = sb("arena", [P, ARENA])

        def C(name, rows=P):
            a, n = CONST_COLS[name]
            return const[0:rows, a:a + n]

        ident = C("ident")
        top = [0]

        def view(n, shape=None, parts=P, at=None):
            if at is None:
                at = top[0]
                top[0] += n
                assert top[0] <= ARENA, top[0]
            a = arena[0:parts, at:at + n]
            if shape is None:
                return a
            names = "abcd"[:len(shape)]
            return a.rearrange(f"p ({' '.join(names)}) -> p {' '.join(names)}", **dict(zip(names, shape)))

        yT = view(KD * T, (KD, T))
        NPROB, NPT = 4, 3
        probs = [view(384) for _ in range(NPROB)]
        probsT = [view(384) for _ in range(NPT)]
        amax = view(NPROB * 2, (NPROB, 2))
        abias = view(NPROB * 2, (NPROB, 2))
        asum = view(NPROB * 2, (NPROB, 2))
        arec = view(NPROB * 2, (NPROB, 2))
        gate_part = yT[:, 0, :]
        mark = top[0]
        qkT = view(8 * T, (8, T))
        rope_raw = view(8 * T, (8, T))
        rope_out = view(8 * T, (8, T))
        rope_cos = [hs[:, 0, i * 2 * T:(i + 1) * 2 * T] for i in range(2)]
        rope_sin = [hs[:, 1, i * 2 * T:(i + 1) * 2 * T] for i in range(2)]
        v_ext = view(TT * MH * (DH + 1), (TT, MH, DH + 1))
        v_b = view(TT * MH * DH, (TT, MH * DH))
        og = view(TT * MH * DH, (TT, MH * DH))
        rows0 = [view(2 * T, parts=MH) for _ in range(2)]
        row = [view(T, parts=MH) for _ in range(6)]
        acols = view(16, (4, MH))
        _lstm = rope_out.rearrange("p a b -> p (a b)")
        arg = [_lstm[:, 384 * i:384 * (i + 1)] for i in range(2)]
        lstm_pT = [_lstm[:, 384 * (2 + i):384 * (3 + i)] for i in range(2)]
        junk = [_lstm[:, 384 * 4 + DH * i:384 * 4 + DH * (i + 1)] for i in range(TT)]
        probsT0 = probsT + [xT[:, 0:2, :].rearrange("p a b -> p (a b)")[:, 0:384]]
        small0 = view(64, (8, 8))
        num = view(TT * MH * (DH + 1), (TT, MH, DH + 1), at=0)
        top[0] = mark
        lg = view(TT * LOGITS, (TT, LOGITS))
        g4 = [view(TT * GROUPS, (TT, GROUPS)) for _ in range(7)]
        e16 = [view(TT * EXPERTS, (TT, EXPERTS)) for _ in range(4)]
        t1 = [view(TT) for _ in range(7)]
        rexp = [g4[1], t1[6]]
        posm = view(TT * EXPERTS, (TT, EXPERTS))
        comb = view(TT * EXPERTS, (TT, EXPERTS))
        sel = view(TT * EXPERTS // 2).bitcast(bf16).rearrange("p (t n) -> p t n", t=TT)
        pick = [view(TT * S2 // 2).bitcast(bf16).rearrange("p (t s) -> p t s", t=TT) for _ in range(2)]
        hs_part = [view(TT * D // 2).bitcast(bf16).rearrange("p (t d) -> p t d", t=TT) for _ in range(3)]
        logit_part = view(T)
        wpick = [view(TT * S2, (TT, S2)) for _ in range(2)]
        xg = [view(KD * S2, (KD, S2)) for _ in range(2)]
        silu_t = view(HID)
        hdn = view(HID)
        turned = [view(HID + T) for _ in range(2)]
        slot_hot = [view(T // 2).bitcast(bf16) for _ in range(2)]
        slot_w = [view(1) for _ in range(2)]
        y_part = [view(D // 2).bitcast(bf16) for _ in range(3)]
        y_rest = view(D)
        top[0] = mark
        q_raw = view(NH * T, (NH, T))
        kk_raw = view(4 * T, (4, T))
        q_rot = view(NH * T, (NH, T))
        kk_rot = view(4 * T, (4, T))
        v_sw = view(2 * TT * NG * DH, (2, TT, NG * DH))
        blocks = [view(CMP_LEN * QUARTER, (CMP_LEN, QUARTER)) for _ in range(2)]
        cmp_part = [q_rot[:, NH - 2 + kv, :] for kv in range(2)]
        probsT1 = probsT + [view(384)]
        gelu_t = [view(2 * NG * NCMP, (2, NG * NCMP)) for _ in range(2)]
        kcmpT = view(NG * NCMP)
        vcmp = view(NG * DH, parts=NCMP)
        gates = view(TT * 3 * NH, (TT, NH, 3))
        pc = view(TT * NH * NCMP, (TT, NH, NCMP))
        pcs = [view(TT * NH, (TT, NH)) for _ in range(3)]
        pcT = [blocks[i // 2].rearrange("p l q -> p (l q)")[0:NCMP, i % 2 * 2 * T:(i % 2 + 1) * 2 * T]
               for i in range(4)]
        count_f = [sb(f"count_f{i}", [1, 4]) for i in range(2)]
        count_i = [sb(f"count_i{i}", [1, 1], i32) for i in range(2)]

        psum = ctx.enter_context(nc.psum_tensor("psum", [P, 8 * BANK], f32))

        def bank_ap(b, n=1):
            return psum[:, b * BANK:(b + n) * BANK]

        bank_filled = [sem(f"bank_filled{b}") for b in range(8)]
        bank_emptied = [sem(f"bank_emptied{b}") for b in range(8)]
        slot_loaded = [sem(f"slot_loaded{s}") for s in range(NSLOT)]
        x_loaded = [sem(f"x_loaded{t}") for t in range(TT)]
        first_loaded, const_loaded, params_loaded = sem("first_loaded"), sem("const_loaded"), sem("params_loaded")
        gate0_loaded, gate_padded = sem("gate0_loaded"), sem("gate_padded")
        small_loaded = sem("small_loaded")
        vec_step, act_step, pool_step = sem("vec_step"), sem("act_step"), sem("pool_step")
        sq_done, rstd_ready = sem("sq_done"), sem("rstd_ready")
        hsA_ready, hsV_ready = sem("hsA_ready"), sem("hsV_ready")
        h_updated, h_copiedA = sem("h_updated"), sem("h_copiedA")
        wout_used, cmp_used = sem("wout_used"), sem("cmp_used")
        ones_set, bias_scaled = sem("ones_set"), sem("bias_scaled")
        conv_seeded, qk_ready = sem("conv_seeded"), sem("qk_ready")
        cos_done, rope_ready = sem("cos_done"), sem("rope_ready")
        og_ready = sem("og_ready")
        logf_done, nm_ready, expnm_ready, m_ready = (sem("logf_done"), sem("nm_ready"), sem("expnm_ready"),
                                                     sem("m_ready"))
        arg_ready, decay_ready = sem("arg_ready"), sem("decay_ready")
        lstm_sq, denom_sq, lstm_rstd, lstm_y = sem("lstm_sq"), sem("denom_sq"), sem("lstm_rstd"), sem("lstm_y")
        abias_ready, aexp_done, arec_ready, aprob_ready = (sem("abias_ready"), sem("aexp_done"), sem("arec_ready"),
                                                           sem("aprob_ready"))
        pads_zeroed, gelu_done, pc_exp_in, pc_exp_out, pc_ready = (
            sem("pads_zeroed"), sem("gelu_done"), sem("pc_exp_in"), sem("pc_exp_out"),
            sem("pc_ready"))
        r_exp_in, r_exp_out, sel_ready, count_ready = (sem("r_exp_in"), sem("r_exp_out"), sem("sel_ready"),
                                                       sem("count_ready"))
        picked, wpicked, xg_filled, xg_ready = sem("picked"), sem("wpicked"), sem("xg_filled"), sem("xg_ready")
        hid_filled, silu_done, hdn_ready = sem("hid_filled"), sem("silu_done"), sem("hdn_ready")
        turn_filled, turned_ready = sem("turn_filled"), sem("turned_ready")
        tile0_done, counters_set, y_half_filled = sem("tile0_done"), sem("counters_set"), sem("y_half_filled")
        y_filled, slots_ready, scattered = sem("y_filled"), sem("slots_ready"), sem("scattered")
        y1_ready, y_rest_ready, y2_ready, y3_ready = (sem("y1_ready"), sem("y_rest_ready"), sem("y2_ready"),
                                                      sem("y3_ready"))
        more_parts = [sem(f"more_parts{i}") for i in range(2)]
        hs_part_ready, hs_rest_ready = sem("hs_part_ready"), sem("hs_rest_ready")
        more_loaded = [sem(f"more_loaded{i}") for i in range(2)]
        more_pe = [sem(f"more_pe{i}") for i in range(2)]
        more_vec = [sem(f"more_vec{i}") for i in range(2)]
        more_act = [sem(f"more_act{i}") for i in range(2)]
        more_done = [sem(f"more_done{i}") for i in range(2)]
        more_base = [sem(f"more_base{i}") for i in range(2)]
        router_padded, out_ready, out_stored = sem("router_padded"), sem("out_ready"), sem("out_stored")

        w_in_0 = A["w_in_0"].rearrange("(p k) n -> p k n", k=KD)
        w_in_1 = A["w_in_1"].rearrange("(p k) n -> p k n", k=KD)
        W0 = MH * DH
        Z0 = ([("qk", i, 256 * i) for i in range(4)]
              + [("vm", i, 2 * W0 + 256 * i) for i in range(2)]
              + [("rope", i, 4 * W0 + 2 * MH + 256 * i) for i in range(4)]
              + [("om", i, 3 * W0 + 256 * i) for i in range(2)]
              + [("vb", i, 6 * W0 + 2 * MH + 256 * i) for i in range(2)])
        QW, KW = NH * DH, NG * DH
        Z1 = ([("cmp", 0, QW), ("cmp", 1, QW + KW)]
              + [("rope", i, 256 * i) for i in range(4)]
              + [("rope", 4, QW + 2 * KW), ("rope", 5, QW + 4 * KW)]
              + [("vsw", 0, QW + 3 * KW), ("vsw", 1, QW + 5 * KW)])
        N_Z0, N_Z1, N_MOE = len(Z0), len(Z1), 3 * EXPERTS
        FIRST = {"z0": 0, "o0": N_Z0, "moe0": N_Z0 + 4}
        FIRST["z1"] = FIRST["moe0"] + N_MOE
        N_BEFORE_CMP = 3
        FIRST["cmp"] = FIRST["z1"] + N_BEFORE_CMP
        FIRST["z1b"] = FIRST["cmp"] + 8
        FIRST["o1"] = FIRST["z1"] + N_Z1 + 8
        SKIPPED = range(FIRST["o1"] + 4, -(-(FIRST["o1"] + 4) // PAIR_LOADS) * PAIR_LOADS)
        FIRST["moe1"] = SKIPPED.stop
        assert FIRST["moe0"] % PAIR_LOADS == 0 and len(SKIPPED) <= NSLOT

        def z_load(layer, i):
            return FIRST[f"z{layer}"] + i + (8 if layer == 1 and i >= N_BEFORE_CMP else 0)

        def slot_of(n):
            return n % NSLOT

        def loads_before(n):
            return n // NSLOT - sum(m < n and slot_of(m) == slot_of(n) for m in SKIPPED)

        jobs = Jobs(bank_filled, bank_emptied)

        def plan_norm(n):
            for j in range(4):
                jobs.plan(("x", n, j))

        def plan_out(layer):
            for i in range(4):
                jobs.plan(("o", layer, i), emptied=(h_updated, 4 * layer + i + 1))

        plan_norm(0)
        jobs.plan("cols")
        Z0_ORDER = [("z", 0), ("gp", 0), ("z", 1), ("gate0",), ("z", 2), ("z", 3), ("acols",), ("z", 4), ("mB", 0),
                    ("z", 5), ("mS", 0), ("mS", 1), ("z", 6), ("mN", 0), ("mN", 1), ("mB", 1), ("mS", 2), ("mS", 3),
                    ("z", 7), ("mN", 2), ("mN", 3), ("z", 8), ("z", 9), ("z", 10), ("z", 11), ("aS", 0), ("aS", 1),
                    ("z", 12), ("aS", 2), ("aS", 3), ("aT", 0), ("aT", 1), ("z", 13), ("aT", 2), ("aT", 3),
                    ("yt", 0), ("yt", 1), ("aO", 0), ("aO", 1), ("aO", 2), ("aO", 3)]
        for kind, *i in Z0_ORDER:
            if kind in ("z", "aS", "aT", "aO"):
                jobs.plan((kind, 0, *i))
            elif kind == "mB":
                jobs.plan((kind, *i), emptied=(arg_ready, 2 * i[0] + 2))
            elif kind == "mN":
                jobs.plan((kind, *i), emptied=(lstm_sq, i[0] + 1))
            else:
                jobs.plan((kind, *i) if i else kind)
        plan_out(0)

        def plan_moe(layer):
            n = 1 + 2 * layer
            for j in range(4):
                jobs.plan(("x", n, j), bank=j)
            jobs.plan(("part", layer), bank=2)
            jobs.plan(("logits", layer), bank=3)
            jobs.plan(("pos", layer), bank=2)
            jobs.next = 0

        plan_moe(0)
        BEFORE_ACC = [list(jobs.last)]
        plan_norm(2)
        Z1_ORDER = [("z", 0), ("z", 1), ("z", 2), ("cmp1", 0), ("cmp1", 1), ("fold", 0), ("fold", 1), ("z", 3),
                    ("kcmp",), ("vcmp",), ("z", 4), ("z", 5), ("z", 6), ("cS",), ("gp", 1), ("z", 7), ("gate1",),
                    ("z", 8), ("aS", 0), ("aS", 1), ("z", 9)]
        for kind, *i in Z1_ORDER:
            if kind in ("z", "aS"):
                jobs.plan((kind, 1, *i))
            elif kind == "fold":
                jobs.plan((kind, *i), emptied=(gelu_done, i[0] + 1))
            else:
                jobs.plan((kind, *i) if i else kind)
        for i in range(4):
            jobs.plan(("cT", i))
        for hd in range(NH + 1):
            if hd + 1 < NH:
                jobs.plan(("aS", 1, 2 * hd + 2))
                jobs.plan(("aS", 1, 2 * hd + 3))
            if hd < NH:
                jobs.plan(("aT", 1, 2 * hd))
                jobs.plan(("aT", 1, 2 * hd + 1))
            if hd >= 1:
                jobs.plan(("aO", 1, hd - 1))
        plan_out(1)
        plan_moe(1)
        BEFORE_ACC.append(list(jobs.last))

        def bank(name):
            return bank_ap(jobs.at[name]["bank"])

        def open_bank(pe, name):
            if jobs.at[name]["before"] is not None:
                pe.wait_ge(*jobs.at[name]["before"])
            return bank(name)

        def fill(ins, name):
            ins.then_inc(jobs.at[name]["filled"][0], 1)

        def wait_filled(eng, name):
            eng.wait_ge(*jobs.at[name]["filled"])
            return bank(name)

        def emptied(ins, name):
            ins.then_inc(jobs.at[name]["emptied"][0], 1)

        def wait_emptied(eng, name):
            eng.wait_ge(*jobs.at[name]["emptied"])

        def mm(o, lhsT, rhs, first=True, last=True):
            return nc.tensor.matmul(o, lhsT, rhs, start=first, stop=last)

        def flip(o, i):
            n = i.shape[0]
            return nc.tensor.transpose(o, i, ident[0:n, 0:n])

        MORE_STEPS = 5
        SHARE = 640
        NX = 5

        def wait_h(eng, n, tile):
            if n == 0:
                eng.wait_ge(x_loaded[tile], 16)
            else:
                eng.wait_ge(h_updated, 4 * (n // 2) + 2 * tile + 2)

        def unit(layer, u):
            if layer == 0:
                return (rope_out[:, u, :], rope_out[:, MH + u, :],
                        [v_b[:, t, u * DH:(u + 1) * DH] for t in range(TT)], None)
            hd, br = u // 2, u % 2
            g = hd // REP
            return (q_rot[:, hd, :], kk_rot[:, 2 * br + g, :],
                    [v_sw[:, br, t, g * DH:(g + 1) * DH] for t in range(TT)],
                    [gates[:, t, hd, 1 + br:2 + br] for t in range(TT)])

        def useq(layer, u):
            return u + 1 + (MH if layer else 0)

        block = ctx.enter_context(nc.Block())

        @block.sync
        def _(sp):
            xv = A["x"][0].rearrange("(t p) d -> p t d", p=P)
            for t in range(TT):
                sp.dma_start(h[:, t, :], xv[:, t, :]).then_inc(x_loaded[t], 16)
            sp.dma_start(const[:, 0:N_FIRST], A["const"][:, 0:N_FIRST]).then_inc(first_loaded, 16)
            for dst, src in ((norm_gain[:, 0, :], A["mix_norm_0"].rearrange("(p k) -> p k", k=KD)),
                             (cols_raw[0:32, :], A["mlstm_conv_0"].rearrange("j (c p) -> (j c) p", p=P)),
                             (cols_raw[32:96, :], A["nsa_cmp_pos_1"].rearrange("a l d -> (a l) d"))):
                sp.dma_start(dst, src).then_inc(params_loaded, 16)

            def load(n, dst, src):
                sp.dma_start(dst, src).then_inc(slot_loaded[slot_of(n)], 16)

            def wait_used(n):
                m = n - NSLOT
                if m in SKIPPED:
                    m -= NSLOT
                if m < 0:
                    return
                for name in ("moe1", "o1", "z1b", "cmp", "z1", "moe0", "o0", "z0"):
                    if m >= FIRST[name]:
                        i = m - FIRST[name] + (N_BEFORE_CMP if name == "z1b" else 0)
                        break
                layer = int(name[-1] != "0")
                if name[0] == "z":
                    sp.wait_ge(*jobs.at[("z", layer, i)]["filled"])
                elif name[0] == "o":
                    if i < 3:
                        sp.wait_ge(wout_used, 3 * layer + i + 1)
                    else:
                        sp.wait_ge(*jobs.at[("o", layer, 3)]["filled"])
                elif name == "cmp":
                    if i % 4 < 3:
                        sp.wait_ge(cmp_used, 3 * (i // 4) + i % 4 + 1)
                    else:
                        sp.wait_ge(*jobs.at[("cmp1", i // 4)]["filled"])
                else:
                    pair = i // PAIR_LOADS + PAIRS * layer
                    sp.wait_ge((hid_filled, hid_filled, y_filled)[i % PAIR_LOADS // 2], pair + 1)

            def slot(n, shape):
                a = ring[:, slot_of(n), :]
                return a.rearrange("p (a b) -> p a b", a=shape)

            def load_z(layer, i):
                col, w = (Z0, Z1)[layer][i][2], (w_in_0, w_in_1)[layer]
                n = z_load(layer, i)
                wait_used(n)
                load(n, slot(n, KD), w[:, :, col:col + 256])

            def load_out(layer):
                w = A[f"w_out_{layer}"].rearrange("(j k p) n -> p j k n", p=P, k=2)
                for j in range(4):
                    n = FIRST[f"o{layer}"] + j
                    wait_used(n)
                    load(n, slot(n, 2), w[:, j])

            def pair_loads(layer, n, pair):
                for c in range(PAIR_LOADS):
                    name, k = (("moe_w1", KD), ("moe_w3", KD), ("moe_w2", 2))[c // 2]
                    w = A[f"{name}_{layer}"]
                    e = pair * 2 + c % 2
                    dst = ring[:, slot_of(n + c):slot_of(n + c) + 1, :]
                    if k == KD:
                        src = w.rearrange("e (p k) n -> p e (k n)", k=k)[:, ds(e, 1), :]
                    else:
                        src = w.rearrange("e (k p) n -> p e k n", k=k)[:, ds(e, 1), :, :]
                        dst = dst.rearrange("p e (k n) -> p e k n", k=k)
                    yield c, dst, src

            def load_moe(layer):
                n0 = FIRST[f"moe{layer}"]
                for pair in range(2):
                    for c, dst, src in pair_loads(layer, n0 + PAIR_LOADS * pair, pair):
                        wait_used(n0 + PAIR_LOADS * pair + c)
                        load(n0 + PAIR_LOADS * pair + c, dst, src)
                with sp.Fori(1, PAIRS // 2) as it:
                    for b in range(2):
                        pair = it * 2 + b
                        for c, dst, src in pair_loads(layer, n0 + PAIR_LOADS * b, pair):
                            sp.wait_ge((hid_filled, hid_filled, y_filled)[c // 2], PAIRS * layer + pair - 2 + 1)
                            load(n0 + PAIR_LOADS * b + c, dst, src)
                sp.wait_ge(count_ready, layer + 1)
                nx = sp.value_load(count_i[layer][0:1, 0:1], min_val=0, max_val=T // CAP - 1)
                with sp.If(nx > 0):
                    sp.wait_ge(y_filled, PAIRS * (layer + 1))
                    with sp.Fori(0, nx) as r:
                        with sp.Fori(0, PAIRS) as pair:
                            sp.wait_ge(more_pe[layer], (r * PAIRS + pair) * MORE_STEPS + 1)
                            for c, dst, src in pair_loads(layer, n0, pair):
                                sp.dma_start(dst, src).then_inc(more_loaded[layer], 16)
                    sp.wait_ge(more_done[layer], 1)

            small = [(norm_gain[:, 1, :], A["ffn_norm_0"].rearrange("(p k) -> p k", k=KD)),
                     (norm_gain[:, 2, :], A["mix_norm_1"].rearrange("(p k) -> p k", k=KD)),
                     (norm_gain[:, 3, :], A["ffn_norm_1"].rearrange("(p k) -> p k", k=KD)),
                     (head_gain[:, :], A["mlstm_head_norm_0"].partition_broadcast(P)),
                     (w_gate[1][:, :, 0:3 * NH], w_in_1[:, :, QW + 6 * KW:QW + 6 * KW + 3 * NH]),
                     (final_gain[:, :], A["final_norm"].partition_broadcast(P))]
            for i in range(2):
                small += [(router_w[i][:, :, 0:GROUPS], A[f"router_group_{i}"].rearrange("(p k) n -> p k n", k=KD)),
                          (router_w[i][:, :, GROUPS:LOGITS],
                           A[f"router_expert_{i}"].rearrange("(p k) n -> p k n", k=KD)),
                          (router_b[i][:, 0:GROUPS], A[f"router_group_b_{i}"].partition_broadcast(P)),
                          (router_b[i][:, GROUPS:LOGITS], A[f"router_expert_b_{i}"].partition_broadcast(P))]
            assert len(small) == N_SMALL - 2
            small2 = [(w_cmp2[:, 0, :, :], A["nsa_cmp_k2_1"].rearrange("(k p) n -> p k n", p=P)),
                      (w_cmp2[:, 1, :, :], A["nsa_cmp_v2_1"].rearrange("(k p) n -> p k n", p=P))]
            for i in range(N_Z0):
                load_z(0, i)
                if i == 0:
                    sp.dma_start(w_gate[0][:, :, 0:2 * MH], w_in_0[:, :, 4 * W0:4 * W0 + 2 * MH])\
                        .then_inc(gate0_loaded, 16)
                    sp.dma_start(gate_bias[:, :], A["mlstm_gate_b_0"].rearrange("(a h) -> h a", a=2),
                                 allow_slow_non_contiguous=True).then_inc(gate0_loaded, 16)
                if i == N_Z0 - 3:
                    for dst, src in small + small2:
                        sp.dma_start(dst, src).then_inc(small_loaded, 16)
                if i == 1:
                    sp.dma_start(const[:, N_FIRST:NCONST], A["const"][:, N_FIRST:NCONST]).then_inc(const_loaded, 16)
            load_out(0)
            load_moe(0)
            for i in range(N_BEFORE_CMP):
                load_z(1, i)
            for kv, w in enumerate((A["nsa_cmp_k1_1"], A["nsa_cmp_v1_1"])):
                wl = w.rearrange("(l p) n -> p l n", p=P)
                for i in range(4):
                    n = FIRST["cmp"] + 4 * kv + i
                    wait_used(n)
                    load(n, slot(n, 8), wl[:, 8 * i:8 * i + 8, :])
            for i in range(N_BEFORE_CMP, N_Z1):
                load_z(1, i)
            load_out(1)
            load_moe(1)
            ov = out[0].rearrange("(t p) d -> p t d", p=P)
            for i in range(4):
                sp.wait_ge(out_ready, i + 1)
                cols_i = slice((i % 2) * BANK, (i % 2 + 1) * BANK)
                sp.dma_start(ov[:, i // 2, cols_i], h[:, i // 2, cols_i]).then_inc(out_stored, 16)
            sp.wait_ge(out_stored, 16 * 4)

        @block.gpsimd
        def _(pool):
            steps = [0]

            def step(ins):
                steps[0] += 1
                ins.then_inc(pool_step, 1)
                pool.wait_ge(pool_step, steps[0])

            nc.gpsimd.memset(v_ext[:, :, :, DH:DH + 1], 1.0).then_inc(ones_set, 1)
            nc.gpsimd.memset(row[5], 1.0).then_inc(ones_set, 1)
            for i, n in enumerate((2 * MH, 3 * NH)):
                nc.gpsimd.memset(w_gate[i][:, :, n:QUARTER], 0.0).then_inc(gate_padded, 1)
            for i in range(2):
                nc.gpsimd.memset(router_w[i][:, :, LOGITS:QUARTER], 0.0).then_inc(router_padded, 1)
            def norm(n):
                pool.wait_ge(sq_done, 2 * (n + 1))
                if n == 0:
                    pool.wait_ge(first_loaded, 16)
                step(nc.gpsimd.tensor_scalar(rstd[:, n, :], ssq[:, n, :], EPS, 1.0, ALU.add, ALU.mult))
                nc.gpsimd.tensor_tensor(rstd[:, n, :], rstd[:, n, :], C("power")[:, 0:TT], ALU.pow)\
                    .then_inc(rstd_ready, 1)

            def rope(layer, i, raw, cosd):
                z = [k for k, zz in enumerate((Z0, Z1)[layer]) if zz[0] == "rope"][i]
                wait_emptied(pool, ("z", layer, z))
                done = 4 * layer + i
                if i >= 2:
                    pool.wait_ge(rope_ready, done - 1)
                c = C("cos").unsqueeze(1).to_broadcast([P, 2, T])
                nc.gpsimd.tensor_tensor(cosd[i % 2].rearrange("p (a b) -> p a b", a=2), raw, c, ALU.mult)\
                    .then_inc(cos_done, 1)

            norm(0)
            pool.wait_ge(gate0_loaded, 16 * N_GATE0)
            nc.gpsimd.tensor_scalar(gate_bias[:, :], gate_bias[:, :], 1.0 / GATE_CAP, 1.0, ALU.mult,
                                    ALU.mult).then_inc(bias_scaled, 1)
            pool.wait_ge(const_loaded, 16)
            c = CONST_COLS["before"][0]
            nc.gpsimd.tensor_copy(counters.rearrange("p a b -> p (a b)"), const[:, c:c + 2 * P])\
                .then_inc(counters_set, 1)
            for i in range(2):
                rope(0, i, rope_raw[:, 2 * i:2 * i + 2, :], rope_cos)
            pool.wait_ge(denom_sq, 1)
            step(nc.gpsimd.tensor_scalar(small0[:, 3, :], small0[:, 3, :], 1.0 / DH, EPS, ALU.mult, ALU.add))
            nc.gpsimd.tensor_tensor(small0[:, 4, :], small0[:, 3, :], C("power"), ALU.pow).then_inc(lstm_rstd, 1)
            for i in range(2, 4):
                rope(0, i, rope_raw[:, 2 * i:2 * i + 2, :], rope_cos)
            pool.wait_ge(small_loaded, 16 * N_SMALL)
            for i in range(2):
                wait_emptied(pool, ("z", 0, [k for k, z in enumerate(Z0) if z[0] == "om"][i]))
                o = og[:, :, 256 * i:256 * i + 256]
                g = head_gain[:, 256 * i:256 * i + 256].unsqueeze(1).to_broadcast([P, TT, 256])
                nc.gpsimd.tensor_tensor(o, o, g, ALU.mult).then_inc(og_ready, 1)

            def normalise(layer, u):
                _, _, _, gate = unit(layer, u)
                k = useq(layer, u)
                pool.wait_ge(arec_ready, k)
                p = probs[u % NPROB]
                for t, (a, b) in enumerate(((0, 128), (128, 384))):
                    ins = nc.gpsimd.tensor_scalar(p[:, a:b], p[:, a:b], arec[:, u % NPROB, t:t + 1],
                                                  1.0 if gate is None else gate[t], ALU.mult, ALU.mult)
                ins.then_inc(aprob_ready, 1)

            for u in range(MH):
                normalise(0, u)

            def split_rows(layer):
                for j in range(4):
                    pool.wait_ge(*jobs.at[("x", 1 + 2 * layer, j)]["filled"])
                for i in range(2):
                    for tile in range(TT):
                        pool.wait_ge(hs_part_ready, TT * (2 * layer + i) + tile + 1)
                        if i:
                            pool.wait_ge(hs_rest_ready, TT * 2 * layer + tile + 1)
                        nc.gpsimd.tensor_tensor(hs_part[2][:, tile] if i else hs[:, tile, :], hs[:, tile, :],
                                                hs_part[i][:, tile], ALU.subtract).then_inc(hs_rest_ready, 1)

            def split_outputs(layer):
                def third(p):
                    pool.wait_ge(y2_ready, (PAIRS - 1) * layer + p + 1)
                    nc.gpsimd.tensor_tensor(y_part[2], y_rest, y_part[1], ALU.subtract).then_inc(y3_ready, 1)

                with pool.Fori(0, PAIRS - 1) as p:
                    third(p)

            norm(1)
            split_rows(0)
            split_outputs(0)
            norm(2)
            for kv in range(2):
                nc.gpsimd.memset(blocks[kv][:, :, NG * NCMP:QUARTER], 0.0).then_inc(pads_zeroed, 1)
            for i in range(6):
                raw = q_raw[:, 2 * i:2 * i + 2, :] if i < 4 else kk_raw[:, 2 * i - 8:2 * i - 6, :]
                rope(1, i, raw, rope_cos)
            for u in range(2 * NH):
                normalise(1, u)
            norm(3)
            split_rows(1)
            split_outputs(1)
            norm(4)

        @block.scalar
        def _(act):
            steps = [0]

            def step(ins):
                steps[0] += 1
                ins.then_inc(act_step, 1)
                act.wait_ge(act_step, steps[0])

            def square(n, tile, src):
                nc.scalar.activation(hs[:, tile, :], src, ACT.Square, scale=D ** -0.5,
                                     accum_out=ssq[:, n, tile:tile + 1]).then_inc(sq_done, 1)

            def squares_of_sums(n):
                square(n, 0, bank_ap(4, 2))
                act.wait_ge(scattered, PAIRS * (n // 2))
                square(n, 1, bank_ap(6, 2))

            def norm(n):
                if n == 2:
                    squares_of_sums(n)
                    nc.scalar.activation(h[:, 0, :], bank_ap(4, 2), ACT.Copy).then_inc(h_copiedA, 1)
                    act.wait_ge(h_copiedA, 1)
                else:
                    for tile in range(TT):
                        wait_h(act, n, tile)
                        square(n, tile, h[:, tile, :])
                act.wait_ge(rstd_ready, n + 1)
                nc.scalar.activation(hs[:, 0, 0:SHARE], h[:, 0, 0:SHARE], ACT.Copy, scale=rstd[:, n, 0:1])\
                    .then_inc(hsA_ready, 1)

            def norm_evac(n):
                if n == 0:
                    act.wait_ge(params_loaded, 16 * N_PARAMS)
                if n == 1:
                    act.wait_ge(small_loaded, 16 * N_SMALL)
                for j in (1, 3):
                    b = wait_filled(act, ("x", n, j))
                    for k in (2 * j, 2 * j + 1):
                        a = (k - 2 * j) * T
                        ins = nc.scalar.activation(xT[:, k, :], b[:, a:a + T], ACT.Copy, scale=norm_gain[:, n, k:k + 1])
                    emptied(ins, ("x", n, j))

            def copy_out(dst, name, src=None):
                b = wait_filled(act, name)
                emptied(nc.scalar.activation(dst, b if src is None else src(b), ACT.Copy), name)

            norm(0)
            norm_evac(0)

            wait_emptied(act, "cols")

            def conv_seed(i):
                b = wait_filled(act, ("z", 0, i))
                for k in (2 * i, 2 * i + 1):
                    a = (k - 2 * i) * T
                    tap = cols[:, (CONV - 1) * 8 + k:(CONV - 1) * 8 + k + 1]
                    ins = nc.scalar.activation(qkT[:, k, :], b[:, a:a + T], ACT.Copy, scale=tap)
                ins.then_inc(conv_seeded, 1)

            def conv_silu(i):
                wait_emptied(act, ("z", 0, i))
                nc.scalar.activation(qkT[:, 2 * i:2 * i + 2, :], qkT[:, 2 * i:2 * i + 2, :], ACT.Silu)\
                    .then_inc(qk_ready, 1)

            conv_seed(0)
            copy_out(gate_part, ("gp", 0), lambda b: b[:, 0:T])
            conv_seed(1)
            conv_silu(0)
            b = wait_filled(act, "gate0")
            act.wait_ge(bias_scaled, 1)
            for i in range(2):
                ins = nc.scalar.activation(rows0[0][:, i * T:(i + 1) * T], b[0:MH, i * T:(i + 1) * T], ACT.Tanh,
                                           bias=gate_bias[:, i:i + 1], scale=1.0 / GATE_CAP)
            emptied(ins, "gate0")
            wait_emptied(act, "gate0")
            step(nc.scalar.activation(rows0[1][:, 0:T], rows0[0][:, T:2 * T], ACT.Exp, scale=-GATE_CAP))
            nc.scalar.activation(rows0[1][:, T:2 * T], rows0[1][:, 0:T], ACT.Ln, bias=1.0).then_inc(logf_done, 1)
            act.wait_ge(nm_ready, 1)
            nc.scalar.activation(row[4], row[3], ACT.Exp).then_inc(expnm_ready, 1)
            conv_seed(2)
            conv_silu(1)
            conv_seed(3)
            conv_silu(2)
            conv_silu(3)

            def piece(kind, i):
                return ("z", 0, [k for k, z in enumerate(Z0) if z[0] == kind][i])

            def copy_vm(i):
                if i == 0:
                    act.wait_ge(ones_set, 2)
                copy_out(v_ext[:, :, 2 * i:2 * i + 2, 0:DH], piece("vm", i),
                         lambda b: b.rearrange("p (t a e) -> p t a e", t=TT, a=2))

            def copy_vb(i):
                copy_out(v_b[:, :, 256 * i:256 * i + 256], piece("vb", i),
                         lambda b: b.rearrange("p (t n) -> p t n", t=TT))

            def copy_rope(i):
                copy_out(rope_raw[:, 2 * i:2 * i + 2, :].rearrange("p a b -> p (a b)"), piece("rope", i))

            def output_gate(i):
                b = wait_filled(act, piece("om", i))
                emptied(nc.scalar.activation(og[:, :, 256 * i:256 * i + 256], b.rearrange("p (t n) -> p t n", t=TT),
                                             ACT.Sigmoid), piece("om", i))

            def attn_exp(layer, u):
                k = useq(layer, u)
                act.wait_ge(abias_ready, k)
                p = probs[u % NPROB]
                for t, (a, b) in enumerate(((0, 128), (128, 384))):
                    ins = nc.scalar.activation(p[:, a:b], p[:, a:b], ACT.Exp, bias=abias[:, u % NPROB, t:t + 1],
                                               scale=SCALE, accum_out=asum[:, u % NPROB, t:t + 1])
                ins.then_inc(aexp_done, 1)

            def lstm_decay(hd):
                act.wait_ge(arg_ready, hd + 1)
                nc.scalar.activation(arg[hd % 2], arg[hd % 2], ACT.Exp).then_inc(decay_ready, 1)

            def lstm_num(hd):
                b = wait_filled(act, ("mN", hd))
                if hd:
                    act.wait_ge(lstm_sq, hd)
                for t in range(TT):
                    c = t * (DH + 1)
                    nc.scalar.activation(junk[t], b[:, c:c + DH], ACT.Square,
                                         accum_out=small0[:, 0, t * MH + hd:t * MH + hd + 1])
                nc.scalar.activation(num[:, :, hd, :], b[:, 0:TT * (DH + 1)].rearrange("p (t e) -> p t e", t=TT),
                                     ACT.Copy).then_inc(lstm_sq, 1)

            copy_vm(0)
            lstm_decay(0)
            lstm_decay(1)
            copy_vm(1)
            copy_rope(0)
            lstm_num(0)
            lstm_num(1)
            lstm_decay(2)
            lstm_decay(3)
            copy_rope(1)
            lstm_num(2)
            lstm_num(3)
            copy_rope(2)
            copy_rope(3)
            output_gate(0)
            output_gate(1)
            attn_exp(0, 0)
            attn_exp(0, 1)
            copy_vb(0)
            attn_exp(0, 2)
            attn_exp(0, 3)
            for u in range(2):
                copy_out(probsT0[u], ("aT", 0, u), lambda b: b[:, 0:384])
            copy_vb(1)
            for u in range(2, MH):
                copy_out(probsT0[u], ("aT", 0, u), lambda b: b[:, 0:384])
            copy_out(yT[:, 2:4, :].rearrange("p a b -> p (a b)"), ("yt", 1))
            for hd in range(MH):
                copy_out(yT[:, MH + hd, :], ("aO", 0, hd), lambda b: b[:, 0:T])

            def moe(layer):
                norm(1 + 2 * layer)

                def upper_bits(i, tile):
                    if i:
                        act.wait_ge(hs_rest_ready, TT * 2 * layer + tile + 1)
                    elif tile == 0:
                        act.wait_ge(hsA_ready, 2 + 2 * layer)
                        act.wait_ge(hsV_ready, 2 + 2 * layer)
                    nc.scalar.activation(hs_part[i][:, tile], hs[:, tile, :], ACT.Copy).then_inc(hs_part_ready, 1)

                upper_bits(0, 0)
                norm_evac(1 + 2 * layer)
                upper_bits(0, 1)
                copy_out(logit_part, ("part", layer), lambda b: b[:, 0:T])
                for tile in range(TT):
                    upper_bits(1, tile)
                for i in range(2):
                    act.wait_ge(r_exp_in, 2 * layer + i + 1)
                    a = rexp[i]
                    nc.scalar.activation(a, a, ACT.Exp).then_inc(r_exp_out, 1)
                b0 = PAIRS * layer
                c0 = (PAIRS - 1) * layer

                def silu():
                    return nc.scalar.activation(silu_t, bank_ap(2)[:, 0:HID], ACT.Silu)

                def pair_steps(p, b, last=False):
                    act.wait_ge(hid_filled, b0 + p + 1)
                    silu().then_inc(silu_done, 1)
                    act.wait_ge(turn_filled, b0 + p + 1)
                    nc.scalar.activation(turned[b], bank_ap(3), ACT.Copy).then_inc(turned_ready, 1)
                    if last:
                        act.wait_ge(y_half_filled, layer + 1)
                        nc.scalar.activation(y_rest[:, 0:BANK], bank_ap(0), ACT.Copy).then_inc(y1_ready, 1)
                        return
                    act.wait_ge(y_filled, b0 + p + 1)
                    act.wait_ge(slots_ready, c0 + p + 1)
                    nc.scalar.activation(y_part[0], bank_ap(0, 2), ACT.Copy, scale=slot_w[b]).then_inc(y1_ready, 1)

                pair_steps(0, 0)
                with act.Fori(0, PAIRS // 2 - 1) as it:
                    for b in (1, 0):
                        pair_steps(it * 2 + 2 - b, b)
                pair_steps(PAIRS - 1, 1, last=True)
                act.wait_ge(count_ready, layer + 1)
                nx = act.value_load(count_i[layer][0:1, 0:1], min_val=0, max_val=T // CAP - 1)
                with act.If(nx > 0):
                    with act.Fori(0, nx) as r:
                        with act.Fori(0, PAIRS) as pair:
                            act.wait_ge(more_pe[layer], (r * PAIRS + pair) * MORE_STEPS + 3)
                            silu().then_inc(more_act[layer], 1)
                    act.wait_ge(more_done[layer], 1)
                act.wait_ge(tile0_done, layer + 1)

            moe(0)

            norm(2)
            norm_evac(2)

            def copy_raw(i):
                dst = q_raw[:, 2 * i:2 * i + 2, :] if i < 4 else kk_raw[:, 2 * i - 8:2 * i - 6, :]
                copy_out(dst.rearrange("p a b -> p (a b)"), ("z", 1, 2 + i))

            def copy_v(i):
                copy_out(v_sw[:, i].rearrange("p t n -> p (t n)"), ("z", 1, 8 + i))

            copy_raw(0)
            for kv in range(2):
                copy_out(cmp_part[kv], ("cmp1", kv), lambda b: b[:, 0:CMP_HID])
            for kv in range(2):
                b = wait_filled(act, ("fold", kv))
                nc.scalar.activation(gelu_t[kv].rearrange("p a b -> p (a b)"), b[:, 0:2 * NG * NCMP],
                                     ACT.Gelu_apprx_tanh).then_inc(gelu_done, 1)
            copy_raw(1)
            copy_out(kcmpT, "kcmp", lambda b: b[:, 0:NG * NCMP])
            copy_out(vcmp, "vcmp", lambda b: b[0:NCMP, 0:NG * DH])
            for i in range(2, 5):
                copy_raw(i)
            copy_out(gate_part, ("gp", 1), lambda b: b[:, 0:T])
            act.wait_ge(pc_exp_in, 1)
            nc.scalar.activation(pc, pc, ACT.Exp, scale=SCALE).then_inc(pc_exp_out, 1)
            copy_raw(5)
            b = wait_filled(act, "gate1")
            emptied(nc.scalar.activation(gates.rearrange("p t h c -> p (t h c)"), b[:, 0:TT * 3 * NH], ACT.Sigmoid),
                    "gate1")
            copy_v(0)
            for u in range(2):
                attn_exp(1, u)
            copy_v(1)
            for i in range(4):
                copy_out(pcT[i], ("cT", i), lambda b: b[0:NCMP, :])
            for hd in range(NH + 1):
                if hd + 1 < NH:
                    attn_exp(1, 2 * hd + 2)
                    attn_exp(1, 2 * hd + 3)
                if hd < NH:
                    copy_out(probsT1[2 * hd % 4], ("aT", 1, 2 * hd), lambda b: b[:, 0:384])
                if hd >= 1:
                    copy_out(yT[:, hd - 1, :], ("aO", 1, hd - 1), lambda b: b[:, 0:T])
            moe(1)
            squares_of_sums(4)

        @block.vector
        def _(vec):
            steps = [0]

            def step(ins):
                steps[0] += 1
                ins.then_inc(vec_step, 1)
                vec.wait_ge(vec_step, steps[0])

            V = nc.vector

            def norm(n):
                vec.wait_ge(rstd_ready, n + 1)
                if n == 2:
                    vec.wait_ge(h_copiedA, 1)
                V.tensor_scalar(hs[:, 0, SHARE:D], h[:, 0, SHARE:D], rstd[:, n, 0:1], None, ALU.mult)
                V.tensor_scalar(hs[:, 1, :], h[:, 1, :], rstd[:, n, 1:2], None, ALU.mult).then_inc(hsV_ready, 1)
                for j in (0, 2):
                    b = wait_filled(vec, ("x", n, j))
                    if n == 0 and j == 0:
                        vec.wait_ge(params_loaded, 16 * N_PARAMS)
                    if n == 1 and j == 0:
                        vec.wait_ge(small_loaded, 16 * N_SMALL)
                    for k in (2 * j, 2 * j + 1):
                        a = (k - 2 * j) * T
                        ins = V.tensor_scalar(xT[:, k, :], b[:, a:a + T], norm_gain[:, n, k:k + 1], None, ALU.mult)
                    emptied(ins, ("x", n, j))

            def rotate(layer, i):
                z = [k for k, zz in enumerate((Z0, Z1)[layer]) if zz[0] == "rope"][i]
                wait_emptied(vec, ("z", layer, z))
                if layer == 0:
                    raw = rope_raw[:, 2 * i:2 * i + 2, :]
                else:
                    raw = q_raw[:, 2 * i:2 * i + 2, :] if i < 4 else kk_raw[:, 2 * i - 8:2 * i - 6, :]
                sn = rope_sin[i % 2]
                half = DH // 2
                for a in range(2):
                    src, dst = slice(a * half, (a + 1) * half), slice((1 - a) * half, (2 - a) * half)
                    s = C("sin")[src].unsqueeze(1).to_broadcast([half, 2, T])
                    ins = V.tensor_tensor(sn[dst].rearrange("p (a b) -> p a b", a=2), raw[src], s, ALU.mult)
                step(ins)
                vec.wait_ge(cos_done, 4 * layer + i + 1)
                if layer == 0:
                    dst = rope_out[:, 2 * i:2 * i + 2, :]
                else:
                    dst = q_rot[:, 2 * i:2 * i + 2, :] if i < 4 else kk_rot[:, 2 * i - 8:2 * i - 6, :]
                V.tensor_tensor(dst.rearrange("p a b -> p (a b)"), sn, rope_cos[i % 2], ALU.add).then_inc(rope_ready, 1)

            def scores(layer, u):
                k, r = useq(layer, u), u % NPROB
                b = wait_filled(vec, ("aS", layer, u))
                if u >= NPROB:
                    vec.wait_ge(*jobs.at[("aT", layer, u - NPROB)]["filled"])
                for t, (a, z) in enumerate(((0, 128), (128, 384))):
                    ins = V.tensor_tensor_reduce(out=probs[r][:, a:z], in0=b[:, a:z], in1=C("mask_ts")[:, a:z],
                                                 scale=1.0, scalar=-3e38, op0=ALU.add, op1=ALU.max,
                                                 accum_out=amax[:, r, t:t + 1])
                emptied(ins, ("aS", layer, u))
                wait_emptied(vec, ("aS", layer, u))
                V.tensor_scalar(abias[:, r, :], amax[:, r, :], -SCALE, None, ALU.mult).then_inc(abias_ready, 1)

            def sums(layer, u):
                k, r = useq(layer, u), u % NPROB
                vec.wait_ge(aexp_done, k)
                V.reciprocal(arec[:, r, :], asum[:, r, :]).then_inc(arec_ready, 1)

            norm(0)
            b = wait_filled(vec, "cols")
            emptied(V.tensor_copy(cols[:, :], b[:, 0:96]), "cols")
            wait_emptied(vec, "cols")

            for i in range(4):
                if i == 2:
                    neg_f, a_row, m_row, nm_row, _, one_row = row
                    vec.wait_ge(logf_done, 1)
                    vec.wait_ge(ones_set, 2)
                    step(V.tensor_tensor_scan(neg_f, one_row, rows0[1][:, T:2 * T], 0.0, ALU.mult, ALU.add))
                    step(V.scalar_tensor_tensor(out=a_row, in0=rows0[0][:, 0:T], scalar=GATE_CAP, in1=neg_f,
                                                op0=ALU.mult, op1=ALU.add))
                    V.tensor_tensor_scan(m_row, a_row, a_row, 0.0, ALU.max, ALU.max).then_inc(m_ready, 1)
                    vec.wait_ge(m_ready, 1)
                    V.tensor_tensor(nm_row, neg_f, m_row, ALU.subtract).then_inc(nm_ready, 1)
                if i == 3:
                    b = wait_filled(vec, "acols")
                    emptied(V.tensor_copy(acols.rearrange("p a b -> p (a b)"), b[:, 0:16]), "acols")
                    wait_emptied(vec, "acols")
                vec.wait_ge(conv_seeded, i + 1)
                b = bank(("z", 0, i))
                for j in range(CONV - 2, -1, -1):
                    s = CONV - 1 - j
                    for k in (2 * i, 2 * i + 1):
                        a = (k - 2 * i) * T
                        ins = V.scalar_tensor_tensor(out=qkT[:, k, s:T], in0=b[:, a:a + T - s],
                                                     scalar=cols[:, j * 8 + k:j * 8 + k + 1], in1=qkT[:, k, s:T],
                                                     op0=ALU.mult, op1=ALU.add)
                        if j:
                            ins.then_inc(vec_step, 1)
                            steps[0] += 1
                    if j:
                        vec.wait_ge(vec_step, steps[0])
                emptied(ins, ("z", 0, i))

            def lstm_arg(hd):
                b = wait_filled(vec, ("mB", hd // 2))
                a = (hd % 2) * T
                V.scalar_tensor_tensor(out=arg[hd % 2][:, 0:T], in0=C("mask_sT"), scalar=acols[:, 0, hd:hd + 1],
                                       in1=b[:, a:a + T], op0=ALU.add, op1=ALU.subtract)
                V.scalar_tensor_tensor(out=arg[hd % 2][:, T:384], in0=C("mask_sT")[:, 0:P],
                                       scalar=acols[:, 1, hd:hd + 1], in1=b[:, a + P:a + T],
                                       op0=ALU.add, op1=ALU.subtract).then_inc(arg_ready, 1)

            def lstm_weights(hd):
                b = wait_filled(vec, ("mS", hd))
                vec.wait_ge(decay_ready, hd + 1)
                if hd >= 2:
                    vec.wait_ge(*jobs.at[("mN", hd - 2)]["filled"])
                emptied(V.scalar_tensor_tensor(out=lstm_pT[hd % 2], in0=b[:, 0:384], scalar=SCALE, in1=arg[hd % 2],
                                               op0=ALU.mult, op1=ALU.mult), ("mS", hd))

            for hd in (0, 2):
                lstm_arg(hd)
                lstm_arg(hd + 1)
                lstm_weights(hd)
                lstm_weights(hd + 1)
            vec.wait_ge(lstm_sq, MH)
            den = num[:, :, :, DH]
            th = [small0[:, i, :].rearrange("p (t h) -> p t h", t=TT) for i in range(8)]
            step(V.scalar_tensor_tensor(out=th[1], in0=den, scalar=-1.0, in1=den, op0=ALU.mult, op1=ALU.max))
            step(V.tensor_tensor(th[1], th[1], acols[:, 2:4, :], ALU.max))
            step(V.reciprocal(small0[:, 2, :], small0[:, 1, :]))
            step(V.tensor_tensor(small0[:, 3, :], small0[:, 0, :], small0[:, 2, :], ALU.mult))
            V.tensor_tensor(small0[:, 3, :], small0[:, 3, :], small0[:, 2, :], ALU.mult).then_inc(denom_sq, 1)
            for i in range(4):
                rotate(0, i)
            for u in (0, 2):
                scores(0, u)
                scores(0, u + 1)
                sums(0, u)
                sums(0, u + 1)
            vec.wait_ge(lstm_rstd, 1)
            step(V.tensor_tensor(small0[:, 5, :], small0[:, 4, :], small0[:, 2, :], ALU.mult))
            vec.wait_ge(og_ready, 2)
            for hd in range(MH):
                for t in range(TT):
                    o = og[:, t, hd * DH:(hd + 1) * DH]
                    ins = V.scalar_tensor_tensor(out=o, in0=num[:, t, hd, 0:DH],
                                                 scalar=small0[:, 5, t * MH + hd:t * MH + hd + 1], in1=o,
                                                 op0=ALU.mult, op1=ALU.mult)
                if hd % 2:
                    ins.then_inc(lstm_y, 1)
            b = wait_filled(vec, ("yt", 0))
            emptied(V.tensor_copy(yT[:, 0:2, :].rearrange("p a b -> p (a b)"), b), ("yt", 0))

            def add_out(layer):
                for i in range(4):
                    b = wait_filled(vec, ("o", layer, i))
                    piece = h[:, i // 2, (i % 2) * BANK:(i % 2 + 1) * BANK]
                    V.tensor_tensor(piece, b, piece, ALU.add).then_inc(h_updated, 1)

            add_out(0)

            def moe(layer):
                b0 = PAIRS * layer
                c0 = (PAIRS - 1) * layer
                norm(1 + 2 * layer)

                def wide(a, n):
                    return a.unsqueeze(2).to_broadcast([P, TT, n])

                gl, el = lg[:, :, 0:GROUPS], lg[:, :, GROUPS:LOGITS]
                b = wait_filled(vec, ("logits", layer))
                bias = router_b[layer][:, :].unsqueeze(1).to_broadcast([P, TT, LOGITS])
                emptied(V.tensor_tensor(lg, b[:, 0:TT * LOGITS].rearrange("p (t n) -> p t n", t=TT), bias, ALU.add),
                        ("logits", layer))
                wait_emptied(vec, ("logits", layer))
                gmax, gsum, gw, wm, w1, w2, dif = t1
                g_hot, g_less, g_tmp, m1, m2, m_tmp, g_dif = g4
                hot1, hot2, e_left, e_tmp = e16

                def by_group(a):
                    return a.rearrange("p t (g x) -> p (t g) x", g=GROUPS)

                def flat(a):
                    return a.rearrange("p t g -> p (t g)")

                def per_expert(a):
                    return flat(a).unsqueeze(2).to_broadcast([P, TT * GROUPS, PER_GROUP])

                desc4 = C("desc")[:, EXPERTS - GROUPS:EXPERTS]
                desc_x = desc4.unsqueeze(1).to_broadcast([P, TT * GROUPS, PER_GROUP])
                els = el.rearrange("p t (g x) -> p t g x", g=GROUPS)

                def ready(ins):
                    steps[0] += 1
                    ins.then_inc(vec_step, 1)
                    return steps[0]

                def need(k):
                    vec.wait_ge(vec_step, k)

                g = ready(V.tensor_reduce(gmax, gl, AX, ALU.max))
                for t in range(TT):
                    e = ready(V.tensor_reduce(m1[:, t], els[:, t], AX, ALU.max))
                need(g)
                for t in range(TT):
                    g = ready(V.scalar_tensor_tensor(out=g_tmp[:, t, :], in0=gl[:, t, :], scalar=gmax[:, t:t + 1],
                                                     in1=desc4, op0=ALU.is_equal, op1=ALU.mult))
                need(e)
                for t in range(TT):
                    e = ready(V.tensor_tensor(e_tmp[:, t, :].rearrange("p (g x) -> p g x", g=GROUPS), els[:, t],
                                              m1[:, t].unsqueeze(2).to_broadcast([P, GROUPS, PER_GROUP]), ALU.is_equal))
                need(g)
                g = ready(V.tensor_reduce(wm, g_tmp, AX, ALU.max))
                need(e)
                e = ready(V.tensor_tensor(by_group(e_tmp), by_group(e_tmp), desc_x, ALU.mult))
                need(g)
                g = ready(V.tensor_tensor(g_hot, g_tmp, wide(wm, GROUPS), ALU.is_equal))
                need(e)
                e = ready(V.tensor_reduce(flat(m_tmp), by_group(e_tmp), AX, ALU.max))
                V.tensor_tensor(g_less, gl, wide(gmax, GROUPS), ALU.subtract).then_inc(r_exp_in, 1)
                need(e)
                step(V.tensor_tensor(by_group(hot1), by_group(e_tmp), per_expert(m_tmp), ALU.is_equal))
                step(V.scalar_tensor_tensor(out=e_left, in0=hot1, scalar=2 * NEG, in1=el, op0=ALU.mult, op1=ALU.add))
                step(V.tensor_reduce(flat(m2), by_group(e_left), AX, ALU.max))
                step(V.tensor_tensor(by_group(e_tmp), by_group(e_left), per_expert(m2), ALU.is_equal))
                step(V.tensor_tensor(by_group(e_tmp), by_group(e_tmp), desc_x, ALU.mult))
                e = ready(V.tensor_reduce(flat(m_tmp), by_group(e_tmp), AX, ALU.max))
                g = ready(V.tensor_tensor(by_group(hot1), by_group(hot1), per_expert(g_hot), ALU.mult))
                need(e)
                step(V.tensor_tensor(by_group(hot2), by_group(e_tmp), per_expert(m_tmp), ALU.is_equal))
                step(V.tensor_tensor(by_group(hot2), by_group(hot2), per_expert(g_hot), ALU.mult))
                V.tensor_tensor(sel, hot1, hot2, ALU.add).then_inc(sel_ready, 1)
                step(V.tensor_tensor(g_dif, m2, m1, ALU.subtract))
                step(V.tensor_tensor(g_dif, g_dif, g_hot, ALU.mult))
                V.tensor_reduce(dif, g_dif, AX, ALU.add).then_inc(r_exp_in, 1)
                b = wait_filled(vec, ("pos", layer))
                step(V.scalar_tensor_tensor(out=posm, in0=b[:, 0:TT * EXPERTS].rearrange("p (t n) -> p t n", t=TT),
                                            scalar=1.0, in1=sel, op0=ALU.add, op1=ALU.mult))
                cf = count_f[layer]

                def build_pick(pair, b):
                    for t in range(TT):
                        for i in range(2):
                            ins = V.tensor_scalar(pick[b][:, t, i * CAP:(i + 1) * CAP], C("iota"),
                                                  posm[:, t, ds(pair * 2 + i, 1)], None, ALU.is_equal)
                    return ins

                def build_wpick(pair, b):
                    for t in range(TT):
                        for i in range(2):
                            e = pair * 2 + i
                            ins = V.tensor_scalar(wpick[b][:, t, i * CAP:(i + 1) * CAP], C("iota"),
                                                  posm[:, t, ds(e, 1)], comb[:, t, ds(e, 1)], ALU.is_equal, ALU.mult)
                    return ins

                def gathered(b, half):
                    k = slice(half * KD // 2, (half + 1) * KD // 2)
                    g = norm_gain[:, 1 + 2 * layer, k].unsqueeze(2).to_broadcast([P, KD // 2, S2])
                    return V.tensor_tensor(xg[b][:, k, :], bank_ap(half).rearrange("p (k s) -> p k s", k=KD // 2), g,
                                           ALU.mult)

                def weigh_slots(b):
                    V.tensor_scalar(slot_hot[b], turned[b][:, HID:HID + T], 0.0, None, ALU.is_gt)
                    return V.tensor_reduce(slot_w[b], turned[b][:, HID:HID + T], AX, ALU.max)

                def rest(b):
                    return V.scalar_tensor_tensor(out=y_rest, in0=bank_ap(0, 2), scalar=slot_w[b], in1=y_part[0],
                                                  op0=ALU.mult, op1=ALU.subtract)

                def gated():
                    return V.tensor_tensor(hdn, bank_ap(2)[:, HID:2 * HID], silu_t, ALU.mult)

                build_pick(0, 0).then_inc(picked, 1)
                emptied(V.tensor_reduce(cf[0:1, 0:1], b[0:1, 2 * EXPERTS:3 * EXPERTS], AX, ALU.max), ("pos", layer))
                wait_emptied(vec, ("pos", layer))
                step(V.tensor_scalar(cf[0:1, 1:2], cf[0:1, 0:1], float(CAP), None, ALU.is_gt))
                step(V.scalar_tensor_tensor(out=cf[0:1, 2:3], in0=cf[0:1, 0:1], scalar=2.0 * CAP, in1=cf[0:1, 1:2],
                                            op0=ALU.is_gt, op1=ALU.add))
                V.scalar_tensor_tensor(out=count_i[layer][0:1, 0:1], in0=cf[0:1, 0:1], scalar=3.0 * CAP,
                                       in1=cf[0:1, 2:3], op0=ALU.is_gt, op1=ALU.add).then_inc(count_ready, 1)
                vec.wait_ge(r_exp_out, 2 * layer + 1)
                step(V.tensor_reduce(gsum, g_less, AX, ALU.add))
                step(V.reciprocal(gw, gsum))
                vec.wait_ge(r_exp_out, 2 * layer + 2)
                step(V.tensor_scalar(w1, dif, 1.0, None, ALU.add))
                step(V.reciprocal(w2, w1))
                step(V.tensor_tensor(w1, w2, gw, ALU.mult))
                step(V.tensor_tensor(w2, w1, dif, ALU.mult))
                step(V.tensor_tensor(hot1, hot1, wide(w1, EXPERTS), ALU.mult))
                step(V.tensor_tensor(hot2, hot2, wide(w2, EXPERTS), ALU.mult))
                step(V.tensor_tensor(comb, hot1, hot2, ALU.add))
                for half in range(2):
                    vec.wait_ge(xg_filled, b0 * 2 + half + 1)
                    gathered(0, half).then_inc(xg_ready, 1)

                def pair_steps(p, b, last=False):
                    build_wpick(p, b).then_inc(wpicked, 1)
                    if not last:
                        build_pick(p + 1, 1 - b).then_inc(picked, 1)
                    vec.wait_ge(silu_done, b0 + p + 1)
                    gated().then_inc(hdn_ready, 1)
                    if not last:
                        for half in range(2):
                            vec.wait_ge(xg_filled, (b0 + p) * 2 + half + 3)
                            gathered(1 - b, half).then_inc(xg_ready, 1)
                    if last:
                        vec.wait_ge(y_filled, b0 + p + 1)
                        V.tensor_copy(y_rest[:, BANK:D], bank_ap(1)).then_inc(y_rest_ready, 1)
                        return
                    vec.wait_ge(turned_ready, b0 + p + 1)
                    weigh_slots(b).then_inc(slots_ready, 1)
                    vec.wait_ge(slots_ready, c0 + p + 1)
                    vec.wait_ge(y1_ready, b0 + p + 1)
                    rest(b).then_inc(y_rest_ready, 1)
                    vec.wait_ge(y_rest_ready, b0 + p + 1)
                    V.tensor_copy(y_part[1], y_rest).then_inc(y2_ready, 1)

                pair_steps(0, 0)
                with vec.Fori(0, PAIRS // 2 - 1) as it:
                    for b in (1, 0):
                        pair_steps(it * 2 + 2 - b, b)
                pair_steps(PAIRS - 1, 1, last=True)
                vec.wait_ge(count_ready, layer + 1)
                nx = vec.value_load(count_i[layer][0:1, 0:1], min_val=0, max_val=T // CAP - 1)
                with vec.If(nx > 0):
                    vec.wait_ge(scattered, PAIRS * (layer + 1))
                    with vec.Fori(0, nx) as r:
                        V.tensor_scalar(posm, posm, -float(CAP), None, ALU.add).then_inc(more_base[layer], 1)
                        with vec.Fori(0, PAIRS) as pair:
                            k = (r * PAIRS + pair) * MORE_STEPS
                            vec.wait_ge(more_pe[layer], k + 1)
                            vec.wait_ge(more_base[layer], r + 1)
                            build_pick(pair, 0)
                            build_wpick(pair, 0).then_inc(more_vec[layer], 1)
                            vec.wait_ge(more_pe[layer], k + 2)
                            gathered(0, 0)
                            gathered(0, 1).then_inc(more_vec[layer], 1)
                            vec.wait_ge(more_act[layer], r * PAIRS + pair + 1)
                            gated().then_inc(more_vec[layer], 1)
                            vec.wait_ge(more_pe[layer], k + 4)
                            V.tensor_copy(turned[0], bank_ap(3)).then_inc(more_parts[layer], 1)
                            kp = (r * PAIRS + pair) * 4
                            vec.wait_ge(more_parts[layer], kp + 1)
                            weigh_slots(0).then_inc(more_vec[layer], 1)
                            vec.wait_ge(more_vec[layer], k + 4)
                            vec.wait_ge(more_pe[layer], k + 5)
                            V.tensor_scalar(y_part[0], bank_ap(0, 2), slot_w[0], None, ALU.mult)\
                                .then_inc(more_parts[layer], 1)
                            vec.wait_ge(more_parts[layer], kp + 2)
                            rest(0).then_inc(more_parts[layer], 1)
                            vec.wait_ge(more_parts[layer], kp + 3)
                            V.tensor_copy(y_part[1], y_rest).then_inc(more_parts[layer], 1)
                            vec.wait_ge(more_parts[layer], kp + 4)
                            V.tensor_tensor(y_part[2], y_rest, y_part[1], ALU.subtract).then_inc(more_vec[layer], 1)
                    vec.wait_ge(more_done[layer], 1)
                vec.wait_ge(scattered, PAIRS * (layer + 1))
                if layer == 0:
                    vec.wait_ge(sq_done, 2 * 3)
                    step(V.tensor_copy(h[:, 1, :], bank_ap(6, 2)))

            moe(0)

            norm(2)
            for kv in range(2):
                b = wait_filled(vec, ("z", 1, kv)).rearrange("p (g n b) -> p b g n", g=NG, b=CMP_STRIDE)
                for half in range(CMP_LEN // CMP_STRIDE):
                    c = MH * 8 + kv * CMP_LEN + half * CMP_STRIDE
                    for g in range(NG):
                        pos = cols[:, c:c + CMP_STRIDE].unsqueeze(2).to_broadcast([P, CMP_STRIDE, NCMP])
                        ins = V.tensor_tensor(blocks[kv][:, half * CMP_STRIDE:(half + 1) * CMP_STRIDE,
                                                         g * NCMP:(g + 1) * NCMP],
                                              b[:, :, g, half:half + NCMP], pos, ALU.add)
                emptied(ins, ("z", 1, kv))
            for i in range(4):
                if i == 3:
                    vec.wait_ge(gelu_done, 2)
                rotate(1, i)

            b = wait_filled(vec, "cS")
            add = C("cmp_add").rearrange("p (t n) -> p t n", t=TT)
            keep = C("cmp_keep").rearrange("p (t n) -> p t n", t=TT)
            bv = b[:, 0:TT * NH * NCMP].rearrange("p (t h n) -> p t h n", t=TT, h=NH)
            for t in range(TT):
                ins = V.tensor_tensor(pc[:, t], bv[:, t], add[:, t].unsqueeze(1).to_broadcast([P, NH, NCMP]), ALU.add)
            emptied(ins, "cS")
            wait_emptied(vec, "cS")
            pcr = pc.rearrange("p t h n -> p (t h) n")
            s0, s1, s2 = [a.rearrange("p t h -> p (t h)") for a in pcs]

            def per_head(a):
                return a.unsqueeze(2).to_broadcast([P, TT * NH, NCMP])

            step(V.tensor_reduce(s0, pcr, AX, ALU.max))
            V.tensor_tensor(pcr, pcr, per_head(s0), ALU.subtract).then_inc(pc_exp_in, 1)
            rotate(1, 4)
            vec.wait_ge(pc_exp_out, 1)
            for t in range(TT):
                ins = V.tensor_tensor(pc[:, t], pc[:, t], keep[:, t].unsqueeze(1).to_broadcast([P, NH, NCMP]), ALU.mult)
            step(ins)
            step(V.tensor_reduce(s0, pcr, AX, ALU.add))
            step(V.tensor_scalar(s1, s0, 1e-30, None, ALU.max))
            step(V.reciprocal(s2, s1))
            rotate(1, 5)
            wait_emptied(vec, "gate1")
            step(V.tensor_tensor(pcs[2], pcs[2], gates[:, :, :, 0], ALU.mult))
            V.tensor_tensor(pcr, pcr, per_head(s2), ALU.mult).then_inc(pc_ready, 1)
            for u in range(2):
                scores(1, u)
            for u in range(2):
                sums(1, u)
            for hd in range(NH):
                if hd + 1 < NH:
                    scores(1, 2 * hd + 2)
                    scores(1, 2 * hd + 3)
                b = wait_filled(vec, ("aT", 1, 2 * hd + 1))
                emptied(V.tensor_copy(probsT1[(2 * hd + 1) % 4], b[:, 0:384]), ("aT", 1, 2 * hd + 1))
                if hd + 1 < NH:
                    sums(1, 2 * hd + 2)
                    sums(1, 2 * hd + 3)
            add_out(1)
            moe(1)
            vec.wait_ge(rstd_ready, NX)
            for i in range(4):
                V.scalar_tensor_tensor(out=h[:, i // 2, (i % 2) * BANK:(i % 2 + 1) * BANK], in0=bank_ap(4 + i),
                                       scalar=rstd[:, NX - 1, i // 2:i // 2 + 1],
                                       in1=final_gain[:, (i % 2) * BANK:(i % 2 + 1) * BANK],
                                       op0=ALU.mult, op1=ALU.mult).then_inc(out_ready, 1)

        @block.tensor
        def _(pe):
            def slot(n, k):
                return ring[:, slot_of(n), :].rearrange("p (a b) -> p a b", a=k)

            def wait_slot(n, more=0):
                pe.wait_ge(slot_loaded[slot_of(n)], (more + (loads_before(n) + 1)) * 16)

            def norm(n):
                pe.wait_ge(hsA_ready, n + 1)
                pe.wait_ge(hsV_ready, n + 1)
                for j in range(4):
                    b = open_bank(pe, ("x", n, j))
                    for k in (2 * j, 2 * j + 1):
                        for t in range(TT):
                            a = (k - 2 * j) * T + t * P
                            ins = flip(b[:, a:a + P], hs[:, t, k:D:KD])
                    fill(ins, ("x", n, j))

            def wait_x(n, k):
                if k % 2 == 0:
                    wait_emptied(pe, ("x", n, k // 2))

            def project(layer, i, natural):
                n = z_load(layer, i)
                name = ("z", layer, i)
                wait_slot(n)
                w = slot(n, KD)
                b = open_bank(pe, name)
                for c in range(2):
                    for k in range(KD):
                        if i == 0 and c == 0:
                            wait_x(2 * layer, k)
                        if natural:
                            ins = mm(b[:, c * 256:c * 256 + 256], xT[:, k, c * P:(c + 1) * P], w[:, k, :],
                                     k == 0, k == KD - 1)
                        else:
                            ins = mm(b[:, c * T:(c + 1) * T], w[:, k, c * P:(c + 1) * P], xT[:, k, :],
                                     k == 0, k == KD - 1)
                fill(ins, name)

            def attn_scores(layer, u):
                q, k, _, _ = unit(layer, u)
                b = open_bank(pe, ("aS", layer, u))
                mm(b[:, 0:P], q[:, 0:P], k[:, 0:P])
                fill(mm(b[:, P:384], q[:, P:T], k[:, 0:T]), ("aS", layer, u))

            def attn_flip(layer, u):
                pe.wait_ge(aprob_ready, useq(layer, u))
                b = open_bank(pe, ("aT", layer, u))
                for i in range(3):
                    ins = flip(b[:, i * P:(i + 1) * P], probs[u % NPROB][:, i * P:(i + 1) * P])
                fill(ins, ("aT", layer, u))

            def attn_values(b, layer, u, first, last):
                wait_emptied(pe, ("aT", layer, u))
                _, _, v, _ = unit(layer, u)
                pT = (probsT0, probsT1)[layer][u % 4]
                mm(b[:, 0:T], v[0], pT[:, 0:T], first, False)
                return mm(b[:, P:T], v[1], pT[:, T:384], False, last)

            def out_proj(layer):
                for j in range(4):
                    n = FIRST[f"o{layer}"] + j
                    wait_slot(n)
                    if layer == 0 and j < 2:
                        wait_emptied(pe, ("yt", j))
                    else:
                        for hd in (2 * j, 2 * j + 1):
                            wait_emptied(pe, ("aO", layer, hd if layer else hd - MH))
                    w = slot(n, 2)
                    for i in range(4):
                        t, half = i // 2, i % 2
                        b = open_bank(pe, ("o", layer, i)) if j == 0 else bank(("o", layer, i))
                        for k in range(2):
                            ins = mm(b, yT[:, 2 * j + k, t * P:(t + 1) * P], w[:, k, half * BANK:(half + 1) * BANK],
                                     j == 0 and k == 0, j == 3 and k == 1)
                        if j == 3:
                            fill(ins, ("o", layer, i))
                    if j < 3:
                        ins.then_inc(wout_used, 1)

            pe.wait_ge(first_loaded, 16)
            norm(0)
            pe.wait_ge(params_loaded, 16 * N_PARAMS)
            b = open_bank(pe, "cols")
            fill(flip(b[:, 0:96], cols_raw[:, :]), "cols")

            def gate_parts(layer):
                if layer == 0:
                    pe.wait_ge(gate0_loaded, 16 * N_GATE0)
                    pe.wait_ge(gate_padded, 2)
                b = open_bank(pe, ("gp", layer))
                for k in range(KD):
                    q = (k % 4) * QUARTER
                    ins = mm(b[q:q + QUARTER, 0:T], w_gate[layer][:, k, :], xT[:, k, :], k < 4, k >= 4)
                fill(ins, ("gp", layer))

            def gate_rows():
                wait_emptied(pe, ("gp", 0))
                b = open_bank(pe, "gate0")
                for i in range(2):
                    ins = mm(b[0:MH, i * T:(i + 1) * T], C("fold")[:, i * MH:(i + 1) * MH], gate_part)
                fill(ins, "gate0")

            def columns():
                pe.wait_ge(m_ready, 1)
                pe.wait_ge(expnm_ready, 1)
                b = open_bank(pe, "acols")
                for i, r in enumerate((row[1], row[4])):
                    for t in range(TT):
                        c = (2 * i + t) * MH
                        ins = flip(b[:, c:c + MH], r[:, t * P:(t + 1) * P])
                fill(ins, "acols")

            def lstm_maxima(i):
                b = open_bank(pe, ("mB", i))
                for a in range(2):
                    hd = 2 * i + a
                    ins = mm(b[:, a * T:(a + 1) * T], C("head_row", MH)[:, hd * P:(hd + 1) * P], row[2])
                fill(ins, ("mB", i))

            def lstm_scores(hd):
                if hd == 0:
                    pe.wait_ge(qk_ready, 4)
                b = open_bank(pe, ("mS", hd))
                q, k = qkT[:, hd, :], qkT[:, MH + hd, :]
                mm(b[:, 0:T], k[:, 0:P], q)
                fill(mm(b[:, T:384], k[:, P:T], q[:, P:T]), ("mS", hd))

            def lstm_values(hd):
                wait_emptied(pe, ("mS", hd))
                if hd == 0:
                    for i in range(2):
                        wait_emptied(pe, ("z", 0, [k for k, z in enumerate(Z0) if z[0] == "vm"][i]))
                b = open_bank(pe, ("mN", hd))
                w = lstm_pT[hd % 2]
                E1 = DH + 1
                mm(b[:, 0:E1], w[:, 0:P], v_ext[:, 0, hd, :])
                mm(b[:, E1:2 * E1], w[:, P:T], v_ext[:, 0, hd, :], True, False)
                fill(mm(b[:, E1:2 * E1], w[:, T:384], v_ext[:, 1, hd, :], False, True), ("mN", hd))

            def lstm_turn(i):
                pe.wait_ge(lstm_y, 2)
                b = open_bank(pe, ("yt", i))
                for a in range(2):
                    for t in range(TT):
                        hd = 2 * i + a
                        ins = flip(b[:, a * T + t * P:a * T + (t + 1) * P], og[:, t, hd * DH:(hd + 1) * DH])
                fill(ins, ("yt", i))

            for kind, *i in Z0_ORDER:
                if kind == "z":
                    project(0, *i, Z0[i[0]][0] in ("om", "vm", "vb"))
                elif kind == "gp":
                    gate_parts(*i)
                elif kind == "gate0":
                    gate_rows()
                    pe.wait_ge(const_loaded, 16)
                elif kind == "acols":
                    columns()
                elif kind == "mB":
                    lstm_maxima(*i)
                elif kind == "mS":
                    lstm_scores(*i)
                elif kind == "mN":
                    lstm_values(*i)
                elif kind == "aS":
                    if i[0] == 0:
                        pe.wait_ge(rope_ready, 4)
                    attn_scores(0, *i)
                elif kind == "aT":
                    attn_flip(0, *i)
                elif kind == "yt":
                    lstm_turn(*i)
                else:
                    if i[0] == 0:
                        for a in range(2):
                            wait_emptied(pe, ("z", 0, [k for k, z in enumerate(Z0) if z[0] == "vb"][a]))
                    b = open_bank(pe, ("aO", 0, *i))
                    fill(attn_values(b, 0, *i, True, True), ("aO", 0, *i))
            out_proj(0)

            def moe(layer):
                n0 = FIRST[f"moe{layer}"]
                b0 = PAIRS * layer
                c0 = (PAIRS - 1) * layer

                def seed(i):
                    if BEFORE_ACC[layer][4 + i] is not None:
                        pe.wait_ge(*BEFORE_ACC[layer][4 + i])
                    mm(bank_ap(4 + i), ident, h[:, i // 2, (i % 2) * BANK:(i % 2 + 1) * BANK])

                for i in range(2):
                    pe.wait_ge(h_updated, 4 * layer + 2 * i + 2)
                    seed(i)
                norm(1 + 2 * layer)
                pe.wait_ge(router_padded, 2)
                pe.wait_ge(small_loaded, 16 * N_SMALL)
                b = open_bank(pe, ("part", layer))
                for k in range(KD):
                    wait_x(1 + 2 * layer, k)
                    q = (k % 4) * QUARTER
                    ins = mm(b[q:q + QUARTER, 0:T], router_w[layer][:, k, :], xT[:, k, :], k < 4, k >= 4)
                fill(ins, ("part", layer))
                wait_emptied(pe, ("part", layer))
                b = open_bank(pe, ("logits", layer))
                for t in range(TT):
                    ins = mm(b[:, t * LOGITS:(t + 1) * LOGITS], logit_part[:, t * P:(t + 1) * P],
                             C("fold")[:, 0:LOGITS])
                fill(ins, ("logits", layer))
                pe.wait_ge(counters_set, 1)
                pe.wait_ge(sel_ready, layer + 1)
                b = open_bank(pe, ("pos", layer))
                mm(b[:, 0:EXPERTS], counters[:, 0, :], sel[:, 0, :])
                mm(b[:, EXPERTS:2 * EXPERTS], counters[:, 1, :], sel[:, 0, :], True, False)
                mm(b[:, EXPERTS:2 * EXPERTS], counters[:, 0, :], sel[:, 1, :], False, True)
                mm(b[:, 2 * EXPERTS:3 * EXPERTS], counters[:, 1, :], sel[:, 0, :], True, False)
                fill(mm(b[:, 2 * EXPERTS:3 * EXPERTS], counters[:, 1, :], sel[:, 1, :], False, True), ("pos", layer))

                for i in range(2, 4):
                    seed(i)

                def gather(b, filled=None):
                    for k in range(KD):
                        for i in range(3):
                            for t in range(TT):
                                ins = mm(bank_ap(0, 2)[:, k * S2:(k + 1) * S2], hs_part[i][:, t, k:D:KD],
                                         pick[b][:, t, :], i == 0 and t == 0, i == 2 and t == TT - 1)
                        if filled is not None and k % 4 == 3:
                            ins.then_inc(filled, 1)
                    return ins

                def hidden(n, b, second_half=None):
                    for k in range(KD):
                        if second_half is not None and k == KD // 2:
                            pe.wait_ge(xg_ready, second_half)
                        for i in range(2):
                            rows = slice(i * CAP, (i + 1) * CAP)
                            at = slot_of(n) + i
                            ins = mm(bank_ap(2)[rows, :].rearrange("p (m n) -> p m n", m=2), xg[b][:, k, rows],
                                     ring[:, at:at + 3:2, k * HID:(k + 1) * HID], k == 0, k == KD - 1)
                    return ins

                def turn(b):
                    for c in range(2):
                        flip(bank_ap(3)[:, c * P:(c + 1) * P], hdn[:, c * P:(c + 1) * P])
                    for t in range(TT):
                        ins = flip(bank_ap(3)[:, HID + t * P:HID + (t + 1) * P], wpick[b][:, t, :])
                    return ins

                def down(n, b, half_filled=None):
                    for half in range(2):
                        for c in range(2):
                            for i in range(2):
                                rows = slice(i * CAP, (i + 1) * CAP)
                                ins = mm(bank_ap(half)[rows, :], turned[b][:, c * P + i * CAP:c * P + (i + 1) * CAP],
                                         slot(n + i, 2)[:, c, half * BANK:(half + 1) * BANK], c == 0, c == 1)
                        if half == 0 and half_filled is not None:
                            ins.then_inc(half_filled, 1)
                    return ins

                def scatter(b, banks=range(4)):
                    for i in banks:
                        t = (i // 2) * P
                        for part in y_part:
                            ins = nc.tensor.matmul(bank_ap(4 + i), slot_hot[b][:, t:t + P],
                                                   part[:, (i % 2) * BANK:(i % 2 + 1) * BANK],
                                                   start=False, stop=True, skip_group_check=True)
                    return ins

                for bb in (("x", 1 + 2 * layer, 0), ("x", 1 + 2 * layer, 1), ("pos", layer), ("logits", layer)):
                    wait_emptied(pe, bb)
                pe.wait_ge(hs_part_ready, TT * (2 * layer + 2))
                pe.wait_ge(hs_rest_ready, TT * (2 * layer + 2))
                pe.wait_ge(picked, b0 + 1)
                gather(0, xg_filled)

                def scatter_last(p, b):
                    pe.wait_ge(y3_ready, c0 + p)
                    scatter(b).then_inc(scattered, 1)

                def steps(p, b, more, n, first=False, last=False):
                    pe.wait_ge(xg_ready, (b0 + p) * 2 + 1)
                    if not first:
                        pe.wait_ge(hdn_ready, b0 + p)
                    for i in range(4):
                        wait_slot(n + i, more)
                    hidden(n, b, (b0 + p) * 2 + 2).then_inc(hid_filled, 1)
                    if not last:
                        pe.wait_ge(picked, b0 + p + 2)
                        if not first:
                            pe.wait_ge(y_rest_ready, b0 + p)
                        gather(1 - b, xg_filled)
                    if last:
                        pe.wait_ge(y3_ready, c0 + p)
                        scatter(1 - b, range(2))
                    pe.wait_ge(hdn_ready, b0 + p + 1)
                    pe.wait_ge(wpicked, b0 + p + 1)
                    if not first:
                        pe.wait_ge(turned_ready, b0 + p)
                    turn(b).then_inc(turn_filled, 1)
                    if last:
                        scatter(1 - b, range(2, 4)).then_inc(scattered, 1)
                    elif not first:
                        scatter_last(p, 1 - b)
                    pe.wait_ge(turned_ready, b0 + p + 1)
                    if not last:
                        pe.wait_ge(xg_ready, (b0 + p) * 2 + 4)
                    for i in range(2):
                        wait_slot(n + 4 + i, more)
                    down(n + 4, b, y_half_filled if last else None).then_inc(y_filled, 1)

                steps(0, 0, 0, n0, first=True)
                with pe.Fori(0, PAIRS // 2 - 1) as it:
                    steps(it * 2 + 1, 1, it, n0 + PAIR_LOADS)
                    steps(it * 2 + 2, 0, it, n0 + 2 * PAIR_LOADS)
                steps(PAIRS - 1, 1, 0, n0 + PAIR_LOADS * (PAIRS - 1), last=True)
                pe.wait_ge(y1_ready, b0 + PAIRS)
                for i in (0, 2, 1, 3):
                    if i == 1:
                        pe.wait_ge(y_rest_ready, b0 + PAIRS)
                    t = HID + (i // 2) * P
                    ins = nc.tensor.matmul(bank_ap(4 + i), turned[1][:, t:t + P],
                                           y_rest[:, (i % 2) * BANK:(i % 2 + 1) * BANK],
                                           start=False, stop=True, skip_group_check=True)
                    if i == 1:
                        ins.then_inc(tile0_done, 1)
                ins.then_inc(scattered, 1)
                pe.wait_ge(count_ready, layer + 1)
                nx = pe.value_load(count_i[layer][0:1, 0:1], min_val=0, max_val=T // CAP - 1)
                with pe.If(nx > 0):
                    mm(bank_ap(2)[:, 0:EXPERTS], counters[:, 1, :], sel[:, 0, :]).then_inc(more_pe[layer], 1)
                    with pe.Fori(0, nx) as r:
                        with pe.Fori(0, PAIRS) as pair:
                            k = (r * PAIRS + pair) * MORE_STEPS
                            pe.wait_ge(more_vec[layer], k + 1)
                            gather(0).then_inc(more_pe[layer], 1)
                            pe.wait_ge(more_vec[layer], k + 2)
                            pe.wait_ge(more_loaded[layer], (r * PAIRS + pair + 1) * (16 * PAIR_LOADS))
                            hidden(n0, 0).then_inc(more_pe[layer], 1)
                            pe.wait_ge(more_vec[layer], k + 3)
                            turn(0).then_inc(more_pe[layer], 1)
                            pe.wait_ge(more_vec[layer], k + 4)
                            down(n0 + 4, 0).then_inc(more_pe[layer], 1)
                            pe.wait_ge(more_vec[layer], k + 5)
                            scatter(0).then_inc(more_pe[layer], 1)
                    mm(bank_ap(2)[:, 0:EXPERTS], counters[:, 1, :], sel[:, 0, :]).then_inc(more_done[layer], 1)

            moe(0)

            norm(2)

            def compress(kv):
                wait_emptied(pe, ("z", 1, kv))
                if kv == 0:
                    pe.wait_ge(pads_zeroed, 2)
                b = open_bank(pe, ("cmp1", kv))
                for i in range(4):
                    n = FIRST["cmp"] + 4 * kv + i
                    wait_slot(n)
                    w = slot(n, 8)
                    for l in range(8):
                        q = (l % 4) * QUARTER
                        ins = mm(b[q:q + QUARTER, 0:CMP_HID], blocks[kv][:, 8 * i + l, :], w[:, l, :],
                                 i == 0 and l < 4, i == 3 and l >= 4)
                    if i < 3:
                        ins.then_inc(cmp_used, 1)
                fill(ins, ("cmp1", kv))

            def fold(kv):
                wait_emptied(pe, ("cmp1", kv))
                b = open_bank(pe, ("fold", kv))
                for c in range(2):
                    ins = mm(b[:, c * NG * NCMP:(c + 1) * NG * NCMP], cmp_part[kv][:, c * P:(c + 1) * P], C("fold"))
                fill(ins, ("fold", kv))

            def compressed_keys():
                pe.wait_ge(gelu_done, 1)
                b = open_bank(pe, "kcmp")
                for c in range(2):
                    ins = mm(b[:, 0:NG * NCMP], w_cmp2[:, 0, c, :], gelu_t[0][:, c, :], c == 0, c == 1)
                fill(ins, "kcmp")

            def compressed_values():
                pe.wait_ge(gelu_done, 2)
                b = open_bank(pe, "vcmp")
                for g in range(NG):
                    for c in range(2):
                        ins = mm(b[0:NCMP, g * DH:(g + 1) * DH], gelu_t[1][:, c, g * NCMP:(g + 1) * NCMP],
                                 w_cmp2[:, 1, c, :], c == 0, c == 1)
                fill(ins, "vcmp")

            def compressed_scores():
                wait_emptied(pe, "kcmp")
                for i in range(2, 6):
                    wait_emptied(pe, ("z", 1, i))
                b = open_bank(pe, "cS")
                for t in range(TT):
                    for hd in range(NH):
                        c = (t * NH + hd) * NCMP
                        g = hd // REP
                        ins = mm(b[:, c:c + NCMP], q_raw[:, hd, t * P:(t + 1) * P], kcmpT[:, g * NCMP:(g + 1) * NCMP])
                fill(ins, "cS")

            def branch_gates():
                wait_emptied(pe, ("gp", 1))
                b = open_bank(pe, "gate1")
                for t in range(TT):
                    ins = mm(b[:, t * 3 * NH:(t + 1) * 3 * NH], gate_part[:, t * P:(t + 1) * P], C("fold")[:, 0:3 * NH])
                fill(ins, "gate1")

            for kind, *i in Z1_ORDER:
                if kind == "z":
                    project(1, *i, Z1[i[0]][0] == "vsw")
                elif kind == "cmp1":
                    compress(*i)
                elif kind == "fold":
                    fold(*i)
                elif kind == "kcmp":
                    compressed_keys()
                elif kind == "vcmp":
                    compressed_values()
                elif kind == "cS":
                    compressed_scores()
                elif kind == "gp":
                    gate_parts(1)
                elif kind == "gate1":
                    branch_gates()
                elif i[0] == 0:
                    pe.wait_ge(rope_ready, 10)
                    attn_scores(1, 0)
                else:
                    attn_scores(1, 1)
            pe.wait_ge(pc_ready, 1)
            for i in range(4):
                b = open_bank(pe, ("cT", i))
                for a in range(2):
                    for t in range(TT):
                        ins = flip(b[0:NCMP, a * T + t * P:a * T + (t + 1) * P], pc[:, t, 2 * i + a, :])
                fill(ins, ("cT", i))
            wait_emptied(pe, "vcmp")
            for i, z in enumerate(Z1):
                if z[0] == "vsw":
                    wait_emptied(pe, ("z", 1, i))
            for hd in range(NH + 1):
                if hd + 1 < NH:
                    attn_scores(1, 2 * hd + 2)
                    attn_scores(1, 2 * hd + 3)
                if hd < NH:
                    attn_flip(1, 2 * hd)
                    attn_flip(1, 2 * hd + 1)
                if hd >= 1:
                    last = hd - 1
                    b = open_bank(pe, ("aO", 1, last))
                    wait_emptied(pe, ("cT", last // 2))
                    attn_values(b, 1, 2 * last, True, False)
                    attn_values(b, 1, 2 * last + 1, False, False)
                    g = last // REP
                    fill(mm(b[:, 0:T], vcmp[:, g * DH:(g + 1) * DH],
                            pcT[last // 2][:, (last % 2) * T:(last % 2 + 1) * T], False, True), ("aO", 1, last))
            out_proj(1)
            moe(1)


def _constants():
    import numpy as np
    r = np.arange(P)
    t = {}
    t["ident"] = np.eye(P)
    t["ones"] = np.ones((P, P))
    t["before"] = r[:, None] < r[None, :]
    tri = np.where(r[:, None] > r[None, :], NEG, 0.0)
    zero = np.zeros((P, P))
    t["mask_sT"] = np.concatenate([tri, zero], 1)
    t["mask_ts"] = np.concatenate([tri.T, zero, tri.T], 1)
    half = DH // 2
    inv = np.float32(10000.0) ** (-(np.arange(half, dtype=np.float32) / np.float32(half)))
    ang = np.arange(T, dtype=np.float32)[None, :] * inv.astype(np.float32)[:, None]
    t["cos"] = np.concatenate([np.cos(ang), np.cos(ang)], 0)
    t["sin"] = np.concatenate([np.sin(ang), -np.sin(ang)], 0)
    t["iota"] = np.tile(np.arange(1, CAP + 1), (P, 1))
    t["desc"] = np.tile(np.arange(EXPERTS, 0, -1), (P, 1))
    t["head_row"] = np.repeat(r[:, None] == np.arange(MH)[None, :], P, 1)
    end = np.arange(NCMP) * CMP_STRIDE + CMP_LEN - 1
    ok = end[None, :] <= np.arange(T)[:, None]
    ok = np.concatenate([ok[i * P:(i + 1) * P] for i in range(TT)], 1)
    t["cmp_add"] = np.where(ok, 0.0, NEG)
    t["cmp_keep"] = ok
    t["power"] = np.full((P, 8), -0.5)
    t["fold"] = r[:, None] % QUARTER == np.arange(NG * NCMP)[None, :]
    return np.concatenate([np.asarray(t[n], np.float32) for n in CONST_COLS], 1)


_INS = ["x", "mix_norm_0", "w_in_0", "mlstm_conv_0", "mlstm_gate_b_0", "mlstm_head_norm_0", "w_out_0", "ffn_norm_0",
        "router_group_0", "router_group_b_0", "router_expert_0", "router_expert_b_0", "moe_w1_0", "moe_w3_0",
        "moe_w2_0", "mix_norm_1", "w_in_1", "nsa_cmp_pos_1", "nsa_cmp_k1_1", "nsa_cmp_k2_1", "nsa_cmp_v1_1",
        "nsa_cmp_v2_1", "w_out_1", "ffn_norm_1", "router_group_1", "router_group_b_1", "router_expert_1",
        "router_expert_b_1", "moe_w1_1", "moe_w3_1", "moe_w2_1", "final_norm"]


def kernel(**inputs):
    import numpy as _np
    import concourse.bacc as _bacc
    from concourse import mybir as _mybir
    from concourse.bass_utils import run_bass_kernel_spmd as _run

    nc = _bacc.Bacc("TRN2", target_bir_lowering=False, num_devices=1)
    arrays, A = {}, {}
    for name in _INS + ["const"]:
        a = _constants() if name == "const" else _np.ascontiguousarray(inputs[name])
        arrays[f"in_{name}_dram"] = a
        A[name] = nc.dram_tensor(f"in_{name}_dram", a.shape, _mybir.dt.from_np(a.dtype), kind="ExternalInput").ap()
    out = nc.dram_tensor("out_0_dram", (1, T, D), _mybir.dt.float32, kind="ExternalOutput").ap()
    hybrid_kernel(nc, A, out)
    r = _run(nc, [arrays], core_ids=[0])
    return r.results[0]["out_0_dram"]
```
